# Optimizing a Trainium2 kernel written in Bass

```python
import jax, jax.numpy as jnp
from jax import lax
import numpy as np
import math

D_MODEL = 2048
BATCH = 1
SEQ = 256
DEPTH = 1

MLA_HEADS = 8
MLA_Q_RANK = 512
MLA_KV_RANK = 256
MLA_NOPE_DIM = 128
MLA_ROPE_DIM = 64
MLA_QK_DIM = MLA_NOPE_DIM + MLA_ROPE_DIM
MLA_V_DIM = 128
MLA_WIDTH = MLA_HEADS * MLA_V_DIM
ROPE_THETA = 10000.0
Q_BLOCK = 128
NEG_INF = -1e30

GLA_HEADS = 4
GLA_VALUE_DIM = D_MODEL // 2
GLA_KEY_DIM = GLA_VALUE_DIM // 2
GLA_HEAD_K = GLA_KEY_DIM // GLA_HEADS
GLA_HEAD_V = GLA_VALUE_DIM // GLA_HEADS
GLA_GATE_RANK = 16
GLA_GATE_TAU = 16.0
GLA_CHUNK = 64

MIX_WIDTH = MLA_WIDTH + GLA_VALUE_DIM
IN_SPLITS = (MLA_Q_RANK, MLA_KV_RANK, MLA_ROPE_DIM,
             GLA_KEY_DIM, GLA_KEY_DIM, GLA_VALUE_DIM, GLA_GATE_RANK, GLA_VALUE_DIM)
IN_COLS = sum(IN_SPLITS)

D_FF = -(-8 * D_MODEL // (3 * 256)) * 256
N_MOD = 6
RMS_EPS = 1e-6


def rms_norm(x, w, eps=RMS_EPS):
    xf = x.astype(jnp.float32)
    y = xf * lax.rsqrt(jnp.mean(xf * xf, axis=-1, keepdims=True) + eps)
    return (y * w.astype(jnp.float32)).astype(x.dtype)

def split_cols(z, sizes):
    out, start = [], 0
    for s in sizes:
        out.append(z[..., start:start + s])
        start += s
    return out

def rope_cos_sin(positions, dim):
    inv_freq = 1.0 / (ROPE_THETA ** (jnp.arange(0, dim, 2, dtype=jnp.float32) / dim))
    ang = positions.astype(jnp.float32)[..., None] * inv_freq
    return jnp.cos(ang), jnp.sin(ang)

def apply_rope(x, cos, sin):
    half = x.shape[-1] // 2
    x1 = x[..., :half].astype(jnp.float32)
    x2 = x[..., half:].astype(jnp.float32)
    out = jnp.concatenate([x1 * cos - x2 * sin, x2 * cos + x1 * sin], axis=-1)
    return out.astype(x.dtype)

def mla_mixer(c_q, c_kv, k_rope, positions, g_q, w_uq, g_kv, w_uk, w_uv):
    B, S, _ = c_q.shape
    H = MLA_HEADS
    q = (rms_norm(c_q, g_q) @ w_uq).reshape(B, S, H, MLA_QK_DIM)
    c_kv = rms_norm(c_kv, g_kv)
    k_nope = (c_kv @ w_uk).reshape(B, S, H, MLA_NOPE_DIM)
    v = (c_kv @ w_uv).reshape(B, S, H, MLA_V_DIM)
    cos, sin = rope_cos_sin(positions, MLA_ROPE_DIM)
    q_rope = apply_rope(q[..., MLA_NOPE_DIM:], cos[:, :, None, :], sin[:, :, None, :])
    k_rope = apply_rope(k_rope, cos, sin)
    q = jnp.concatenate([q[..., :MLA_NOPE_DIM], q_rope], axis=-1) * (MLA_QK_DIM ** -0.5)
    k = jnp.concatenate(
        [k_nope, jnp.broadcast_to(k_rope[:, :, None, :], (B, S, H, MLA_ROPE_DIM))], axis=-1)
    q = q.transpose(0, 2, 1, 3)
    k = k.transpose(0, 2, 1, 3)
    v = v.transpose(0, 2, 1, 3)
    nb = S // Q_BLOCK
    q_blocks = q.reshape(B, H, nb, Q_BLOCK, MLA_QK_DIM).transpose(2, 0, 1, 3, 4)
    k_pos = jnp.arange(S)

    def attend(args):
        q_blk, blk = args
        q_pos = blk * Q_BLOCK + jnp.arange(Q_BLOCK)
        s = jnp.einsum('bhqd,bhkd->bhqk', q_blk, k).astype(jnp.float32)
        s = jnp.where(k_pos[None, :] <= q_pos[:, None], s, NEG_INF)
        p = jax.nn.softmax(s, axis=-1).astype(v.dtype)
        return jnp.einsum('bhqk,bhkd->bhqd', p, v)

    o = lax.map(attend, (q_blocks, jnp.arange(nb)))
    return o.transpose(1, 0, 3, 2, 4).reshape(B, S, MLA_WIDTH)

def gla_mixer(q, k, v, a_lr, r, w_gate_up, b_gate, g_gla):
    B, S, _ = q.shape
    H, dk, dv, C = GLA_HEADS, GLA_HEAD_K, GLA_HEAD_V, GLA_CHUNK
    N = S // C
    f32 = jnp.float32
    log_a = jax.nn.log_sigmoid((a_lr @ w_gate_up + b_gate).astype(f32)) / GLA_GATE_TAU

    def chunked(t, d):
        return t.reshape(B, N, C, H, d).transpose(0, 3, 1, 2, 4).astype(f32)

    qc = chunked(q, dk) * (dk ** -0.5)
    kc = chunked(k, dk)
    vc = chunked(v, dv)
    bc = jnp.cumsum(chunked(log_a, dk), axis=3)
    b_last = bc[:, :, :, -1:, :]
    q_dec = qc * jnp.exp(bc)
    k_inv = kc * jnp.exp(-bc)
    k_dec = kc * jnp.exp(b_last - bc)
    causal = jnp.tril(jnp.ones((C, C), dtype=bool))
    attn = jnp.einsum('bhncd,bhnjd->bhncj', q_dec, k_inv)
    attn = jnp.where(causal, attn, 0.0)
    o_intra = jnp.einsum('bhncj,bhnjv->bhncv', attn, vc)
    d_state = jnp.einsum('bhncd,bhncv->bhndv', k_dec, vc)
    decay = jnp.exp(b_last[:, :, :, 0, :])

    def step(state, inp):
        q_n, ds_n, decay_n = inp
        o_n = jnp.einsum('bhcd,bhdv->bhcv', q_n, state)
        state = decay_n[..., None] * state + ds_n
        return state, o_n

    init = jnp.zeros((B, H, dk, dv), f32)
    _, o_inter = lax.scan(step, init, (jnp.moveaxis(q_dec, 2, 0),
                                       jnp.moveaxis(d_state, 2, 0),
                                       jnp.moveaxis(decay, 2, 0)))
    o = o_intra + jnp.moveaxis(o_inter, 0, 2)
    o = o.transpose(0, 2, 3, 1, 4).reshape(B, S, H, dv)
    o = rms_norm(o, g_gla) * jax.nn.silu(r.reshape(B, S, H, dv).astype(f32))
    return o.reshape(B, S, GLA_VALUE_DIM).astype(q.dtype)

def first_inputs(seed: int = 0) -> dict:
    key = jax.random.key(seed)
    ks = jax.random.split(key, 24)
    f32 = jnp.float32
    L = DEPTH

    def nrm(k, shape, scale):
        return jax.random.normal(k, shape, f32) * scale

    def gain(k, shape):
        return 1.0 + 0.02 * jax.random.normal(k, shape, f32)

    offsets = jax.random.randint(ks[2], (BATCH, 1), 0, 4096, dtype=jnp.int32)
    positions = offsets + jnp.arange(SEQ, dtype=jnp.int32)[None, :]
    return {
        'x': nrm(ks[0], (BATCH, SEQ, D_MODEL), 1.0),
        'c': nrm(ks[1], (BATCH, D_MODEL), 1.0),
        'positions': positions,
        'w_ada': nrm(ks[3], (L, D_MODEL, N_MOD * D_MODEL), D_MODEL ** -0.5),
        'b_ada': nrm(ks[4], (L, N_MOD * D_MODEL), 0.01),
        'g_pre_mix': gain(ks[5], (L, D_MODEL)),
        'g_post_mix': gain(ks[6], (L, D_MODEL)),
        'w_in': nrm(ks[7], (L, D_MODEL, IN_COLS), D_MODEL ** -0.5),
        'g_q': gain(ks[8], (L, MLA_Q_RANK)),
        'w_uq': nrm(ks[9], (L, MLA_Q_RANK, MLA_HEADS * MLA_QK_DIM), MLA_Q_RANK ** -0.5),
        'g_kv': gain(ks[10], (L, MLA_KV_RANK)),
        'w_uk': nrm(ks[11], (L, MLA_KV_RANK, MLA_HEADS * MLA_NOPE_DIM), MLA_KV_RANK ** -0.5),
        'w_uv': nrm(ks[12], (L, MLA_KV_RANK, MLA_HEADS * MLA_V_DIM), MLA_KV_RANK ** -0.5),
        'w_gate_up': nrm(ks[13], (L, GLA_GATE_RANK, GLA_KEY_DIM), GLA_GATE_RANK ** -0.5),
        'b_gate': nrm(ks[14], (L, GLA_KEY_DIM), 0.1),
        'g_gla': gain(ks[15], (L, GLA_HEAD_V)),
        'w_out': nrm(ks[16], (L, MIX_WIDTH, D_MODEL), MIX_WIDTH ** -0.5),
        'g_pre_ffn': gain(ks[17], (L, D_MODEL)),
        'g_post_ffn': gain(ks[18], (L, D_MODEL)),
        'w_ffn_gate': nrm(ks[19], (L, D_MODEL, D_FF), D_MODEL ** -0.5),
        'w_ffn_up': nrm(ks[20], (L, D_MODEL, D_FF), D_MODEL ** -0.5),
        'w_ffn_down': nrm(ks[21], (L, D_FF, D_MODEL), D_FF ** -0.5),
    }

def first_block(x, c, positions, w_ada, b_ada, g_pre_mix, g_post_mix, w_in, g_q, w_uq,
              g_kv, w_uk, w_uv, w_gate_up, b_gate, g_gla, w_out, g_pre_ffn, g_post_ffn,
              w_ffn_gate, w_ffn_up, w_ffn_down):
    for l in range(DEPTH):
        ada = jax.nn.silu(c) @ w_ada[l] + b_ada[l]
        shift_m, scale_m, gate_m, shift_f, scale_f, gate_f = [
            t[:, None, :] for t in jnp.split(ada, N_MOD, axis=-1)]

        h = rms_norm(x, g_pre_mix[l]) * (1.0 + scale_m) + shift_m
        z = h @ w_in[l]
        c_q, c_kv, k_rope, q_g, k_g, v_g, a_g, r_g = split_cols(z, IN_SPLITS)
        o_mla = mla_mixer(c_q, c_kv, k_rope, positions, g_q[l], w_uq[l],
                          g_kv[l], w_uk[l], w_uv[l])
        o_gla = gla_mixer(q_g, k_g, v_g, a_g, r_g, w_gate_up[l], b_gate[l], g_gla[l])
        o = jnp.concatenate([o_mla, o_gla], axis=-1) @ w_out[l]
        x = x + gate_m * rms_norm(o, g_post_mix[l])

        h = rms_norm(x, g_pre_ffn[l]) * (1.0 + scale_f) + shift_f
        f = (jax.nn.silu(h @ w_ffn_gate[l]) * (h @ w_ffn_up[l])) @ w_ffn_down[l]
        x = x + gate_f * rms_norm(f, g_post_ffn[l])
    return x


N_MEM = 256
NSA_HEADS = 16
NSA_GROUPS = 4
NSA_HPG = NSA_HEADS // NSA_GROUPS
HEAD_DIM = 64
NSA_WIDTH = NSA_HEADS * HEAD_DIM
KV_WIDTH = NSA_GROUPS * HEAD_DIM
CMP_LEN = 32
CMP_STRIDE = 16
CMP_HID = 2 * HEAD_DIM
SEL_BLK = 64
SEL_TOPN = 16
WIN = 512
Q_BLK = 128
FORCE_SCORE = 1e4
POOL_WINDOWS = (2, 4, 8, 16)
POOL_GROUPS = 4
POOL_WIDTH = D_MODEL // 2
POOL_GW = POOL_WIDTH // POOL_GROUPS
REL_BUCKETS = 32
REL_MAX_DIST = 2048
X_HEADS = 4
X_HEAD_DIM = 128
X_WIDTH = X_HEADS * X_HEAD_DIM
D_FF_2 = -(-8 * D_MODEL // (3 * 256)) * 256
IN_WIDTH = NSA_WIDTH + 6 * KV_WIDTH + 3 * NSA_HEADS + POOL_WIDTH + 2 * D_MODEL


def rms_norm_2(x, g, eps=1e-6):
    xf = x.astype(jnp.float32)
    y = xf * lax.rsqrt(jnp.mean(xf * xf, axis=-1, keepdims=True) + eps)
    return (y * g.astype(jnp.float32)).astype(x.dtype)

def rel_bucket(dist):
    n = jnp.maximum(dist, 0)
    exact = REL_BUCKETS // 2
    nf = jnp.maximum(n, 1).astype(jnp.float32)
    large = exact + (jnp.log(nf / exact) / math.log(REL_MAX_DIST / exact)
                     * (REL_BUCKETS - exact)).astype(jnp.int32)
    return jnp.where(n < exact, n, jnp.minimum(large, REL_BUCKETS - 1))

def masked_softmax(s, mask):
    s = jnp.where(mask, s.astype(jnp.float32), -1e30)
    m = jnp.max(s, axis=-1, keepdims=True)
    e = jnp.where(mask, jnp.exp(s - m), 0.0)
    return e / jnp.maximum(jnp.sum(e, axis=-1, keepdims=True), 1.0)

def compress_kv(raw, pe, w1, w2):
    b, s = raw.shape[0], raw.shape[1]
    n_cmp = (s - CMP_LEN) // CMP_STRIDE + 1
    idx = jnp.arange(n_cmp)[:, None] * CMP_STRIDE + jnp.arange(CMP_LEN)[None, :]
    blk = raw[:, idx] + pe[:, None, :]
    flat = jnp.transpose(blk, (0, 1, 3, 2, 4)).reshape(b, n_cmp, NSA_GROUPS, CMP_LEN * HEAD_DIM)
    return jax.nn.gelu(flat @ w1) @ w2

def cmp_to_sel_overlap(n_cmp, n_sel):
    i = jnp.arange(n_cmp)[:, None]
    j = jnp.arange(n_sel)[None, :]
    lo = jnp.maximum(i * CMP_STRIDE, j * SEL_BLK)
    hi = jnp.minimum(i * CMP_STRIDE + CMP_LEN, (j + 1) * SEL_BLK)
    return jnp.maximum(hi - lo, 0).astype(jnp.float32) / CMP_LEN

def nsa_attention(q, k_cmp_raw, v_cmp_raw, k_sel, v_sel, k_win, v_win, gate_logits,
                  cmp_pe, cmp_w1, cmp_w2, rel_bias):
    b, s = q.shape[0], q.shape[1]
    scale = HEAD_DIM ** -0.5
    kc = compress_kv(k_cmp_raw, cmp_pe[0], cmp_w1[0], cmp_w2[0])
    vc = compress_kv(v_cmp_raw, cmp_pe[1], cmp_w1[1], cmp_w2[1])
    n_cmp = kc.shape[1]
    n_sel = s // SEL_BLK
    topn = min(SEL_TOPN, n_sel)
    overlap = cmp_to_sel_overlap(n_cmp, n_sel)
    cmp_end = jnp.arange(n_cmp) * CMP_STRIDE + CMP_LEN - 1
    kb = k_sel.reshape(b, n_sel, SEL_BLK, NSA_GROUPS, HEAD_DIM).transpose(0, 3, 1, 2, 4)
    vb = v_sel.reshape(b, n_sel, SEL_BLK, NSA_GROUPS, HEAD_DIM).transpose(0, 3, 1, 2, 4)
    kw_pad = jnp.pad(k_win, ((0, 0), (WIN, 0), (0, 0), (0, 0)))
    vw_pad = jnp.pad(v_win, ((0, 0), (WIN, 0), (0, 0), (0, 0)))
    gates = jax.nn.sigmoid(gate_logits.astype(jnp.float32)).astype(q.dtype).reshape(b, s, NSA_HEADS, 3)
    tab_g = rel_bias.reshape(NSA_GROUPS, NSA_HPG, REL_BUCKETS)
    gather_blocks = jax.vmap(jax.vmap(lambda blocks, idx: blocks[idx]))
    group_bias = jax.vmap(jax.vmap(lambda tab, bk: tab[:, bk]), in_axes=(None, 0))

    def head_bias(dist):
        return tab_g[:, :, rel_bucket(dist)]

    def block(qi):
        q0 = qi * Q_BLK
        t = q0 + jnp.arange(Q_BLK)
        qg = lax.dynamic_slice_in_dim(q, q0, Q_BLK, 1).reshape(b, Q_BLK, NSA_GROUPS, NSA_HPG, HEAD_DIM)
        gq = lax.dynamic_slice_in_dim(gates, q0, Q_BLK, 1)
        d_c = t[:, None] - cmp_end[None, :]
        s_c = jnp.einsum('bqghd,bngd->bghqn', qg, kc).astype(jnp.float32) * scale + head_bias(d_c)
        p_c = masked_softmax(s_c, d_c >= 0)
        o_c = jnp.einsum('bghqn,bngd->bqghd', p_c.astype(vc.dtype), vc)
        imp = jnp.einsum('bghqn,nj->bgqj', p_c, overlap)
        cur = t // SEL_BLK
        j = jnp.arange(n_sel)[None, :]
        forced = (j == 0) | (j == cur[:, None]) | (j == cur[:, None] - 1)
        imp = jnp.where(forced, FORCE_SCORE, imp)
        imp = jnp.where(j > cur[:, None], -1.0, imp)
        top_val, top_idx = lax.top_k(imp, topn)
        ks = gather_blocks(kb, top_idx)
        vs = gather_blocks(vb, top_idx)
        pos = top_idx[..., None] * SEL_BLK + jnp.arange(SEL_BLK)
        d_s = t[:, None, None] - pos
        mask_s = (top_val >= 0)[..., None] & (d_s >= 0)
        bias_s = group_bias(tab_g, rel_bucket(d_s))
        s_s = jnp.einsum('bqghd,bgqnkd->bghqnk', qg, ks).astype(jnp.float32) * scale + bias_s
        m_len = topn * SEL_BLK
        p_s = masked_softmax(s_s.reshape(b, NSA_GROUPS, NSA_HPG, Q_BLK, m_len),
                             mask_s.reshape(b, NSA_GROUPS, 1, Q_BLK, m_len))
        o_s = jnp.einsum('bghqm,bgqmd->bqghd', p_s.astype(vs.dtype),
                         vs.reshape(b, NSA_GROUPS, Q_BLK, m_len, HEAD_DIM))
        kw = lax.dynamic_slice_in_dim(kw_pad, q0, WIN + Q_BLK, 1)
        vw = lax.dynamic_slice_in_dim(vw_pad, q0, WIN + Q_BLK, 1)
        s_pos = q0 - WIN + jnp.arange(WIN + Q_BLK)
        d_w = t[:, None] - s_pos[None, :]
        mask_w = (d_w >= 0) & (d_w < WIN) & (s_pos[None, :] >= 0)
        s_w = jnp.einsum('bqghd,bkgd->bghqk', qg, kw).astype(jnp.float32) * scale + head_bias(d_w)
        p_w = masked_softmax(s_w, mask_w)
        o_w = jnp.einsum('bghqk,bkgd->bqghd', p_w.astype(vw.dtype), vw)
        o = jnp.stack([o_c, o_s, o_w], axis=-1).reshape(b, Q_BLK, NSA_HEADS, HEAD_DIM, 3)
        return jnp.einsum('bqhdc,bqhc->bqhd', o, gq)

    out = lax.map(block, jnp.arange(s // Q_BLK))
    return jnp.transpose(out, (1, 0, 2, 3, 4)).reshape(b, s, NSA_WIDTH)

def pool_mixer(u, w_pool, pool_scale):
    b, s, _ = u.shape
    uf = u.astype(jnp.float32)
    cnt_base = jnp.arange(s) + 1
    outs = []
    for gi, w in enumerate(POOL_WINDOWS):
        ug = uf[..., gi * POOL_GW:(gi + 1) * POOL_GW]
        c = jnp.concatenate([jnp.zeros((b, 1, POOL_GW), jnp.float32), jnp.cumsum(ug, axis=1)], axis=1)
        hi = c[:, 1:]
        lo = jnp.pad(c[:, :s + 1 - w], ((0, 0), (w - 1, 0), (0, 0)))
        cnt = jnp.minimum(cnt_base, w).astype(jnp.float32)[None, :, None]
        outs.append((hi - lo) / cnt - ug)
    y = jnp.stack(outs, axis=2).astype(u.dtype)
    y = jnp.einsum('bsgc,gcd->bsgd', y, w_pool)
    return y.reshape(b, s, POOL_WIDTH) * pool_scale

def memory_cross_attention(h, mem_n, wq, wkv, wo):
    b, s, _ = h.shape
    q = (h @ wq).reshape(b, s, X_HEADS, X_HEAD_DIM)
    k, v = jnp.split(mem_n @ wkv, 2, axis=-1)
    k = k.reshape(b, -1, X_HEADS, X_HEAD_DIM)
    v = v.reshape(b, -1, X_HEADS, X_HEAD_DIM)
    sc = jnp.einsum('bshd,bmhd->bhsm', q, k).astype(jnp.float32) * (X_HEAD_DIM ** -0.5)
    p = jax.nn.softmax(sc, axis=-1).astype(v.dtype)
    o = jnp.einsum('bhsm,bmhd->bshd', p, v).reshape(b, s, X_WIDTH)
    return o @ wo

def second_inputs(seed: int = 0) -> dict:
    key = jax.random.key(seed)
    ks = jax.random.split(key, 32)
    f32 = jnp.float32

    def w(k, shape, fan_in):
        return jax.random.normal(k, shape, f32) * (fan_in ** -0.5)

    def gain(k, shape):
        return 1.0 + 0.05 * jax.random.normal(k, shape, f32)

    L = DEPTH
    return {
        "x": jax.random.normal(ks[0], (BATCH, SEQ, D_MODEL), f32),
        "mem": jax.random.normal(ks[1], (BATCH, N_MEM, D_MODEL), f32),
        "rel_bias": 0.5 * jax.random.normal(ks[2], (NSA_HEADS, REL_BUCKETS), f32),
        "ln_mix_pre": gain(ks[3], (L, D_MODEL)),
        "ln_mix_post": gain(ks[4], (L, D_MODEL)),
        "ln_x_pre": gain(ks[5], (L, D_MODEL)),
        "ln_x_post": gain(ks[6], (L, D_MODEL)),
        "ln_mem": gain(ks[7], (L, D_MODEL)),
        "ln_ffn_pre": gain(ks[8], (L, D_MODEL)),
        "ln_ffn_post": gain(ks[9], (L, D_MODEL)),
        "w_in": w(ks[10], (L, D_MODEL, IN_WIDTH), D_MODEL),
        "cmp_pe": 0.1 * jax.random.normal(ks[11], (L, 2, CMP_LEN, HEAD_DIM), f32),
        "cmp_w1": w(ks[12], (L, 2, CMP_LEN * HEAD_DIM, CMP_HID), CMP_LEN * HEAD_DIM),
        "cmp_w2": w(ks[13], (L, 2, CMP_HID, HEAD_DIM), CMP_HID),
        "w_pool": w(ks[14], (L, POOL_GROUPS, POOL_GW, POOL_GW), POOL_GW),
        "pool_scale": gain(ks[15], (L, POOL_WIDTH)),
        "w_br_attn": w(ks[16], (L, NSA_WIDTH, D_MODEL), NSA_WIDTH),
        "w_br_pool": w(ks[17], (L, POOL_WIDTH, D_MODEL), POOL_WIDTH),
        "w_mix_out": w(ks[18], (L, D_MODEL, D_MODEL), D_MODEL),
        "w_xq": w(ks[19], (L, D_MODEL, X_WIDTH), D_MODEL),
        "w_xkv": w(ks[20], (L, D_MODEL, 2 * X_WIDTH), D_MODEL),
        "w_xo": w(ks[21], (L, X_WIDTH, D_MODEL), X_WIDTH),
        "w_gate": w(ks[22], (L, D_MODEL, D_FF_2), D_MODEL),
        "w_up": w(ks[23], (L, D_MODEL, D_FF_2), D_MODEL),
        "w_down": w(ks[24], (L, D_FF_2, D_MODEL), D_FF_2),
    }

def second_block(x, mem, rel_bias, ln_mix_pre, ln_mix_post, ln_x_pre, ln_x_post, ln_mem,
              ln_ffn_pre, ln_ffn_post, w_in, cmp_pe, cmp_w1, cmp_w2, w_pool, pool_scale,
              w_br_attn, w_br_pool, w_mix_out, w_xq, w_xkv, w_xo, w_gate, w_up, w_down):
    b, s, _ = x.shape
    splits = [NSA_WIDTH,
              NSA_WIDTH + 6 * KV_WIDTH,
              NSA_WIDTH + 6 * KV_WIDTH + 3 * NSA_HEADS,
              NSA_WIDTH + 6 * KV_WIDTH + 3 * NSA_HEADS + POOL_WIDTH]
    for l in range(DEPTH):
        h = rms_norm_2(x, ln_mix_pre[l])
        z = h @ w_in[l]
        q, kv, nsa_gl, u, merge_logits = jnp.split(z, splits, axis=-1)
        q = q.reshape(b, s, NSA_HEADS, HEAD_DIM)
        kv = kv.reshape(b, s, 6, NSA_GROUPS, HEAD_DIM)
        a = nsa_attention(q, kv[:, :, 0], kv[:, :, 1], kv[:, :, 2], kv[:, :, 3],
                          kv[:, :, 4], kv[:, :, 5], nsa_gl,
                          cmp_pe[l], cmp_w1[l], cmp_w2[l], rel_bias)
        p = pool_mixer(u, w_pool[l], pool_scale[l])
        g_a, g_p = jnp.split(jax.nn.sigmoid(merge_logits.astype(jnp.float32)).astype(x.dtype), 2, axis=-1)
        y = (g_a * (a @ w_br_attn[l]) + g_p * (p @ w_br_pool[l])) @ w_mix_out[l]
        x = x + rms_norm_2(y, ln_mix_post[l])
        h = rms_norm_2(x, ln_x_pre[l])
        mem_n = rms_norm_2(mem, ln_mem[l])
        y = memory_cross_attention(h, mem_n, w_xq[l], w_xkv[l], w_xo[l])
        x = x + rms_norm_2(y, ln_x_post[l])
        h = rms_norm_2(x, ln_ffn_pre[l])
        y = (jax.nn.silu(h @ w_gate[l]) * (h @ w_up[l])) @ w_down[l]
        x = x + rms_norm_2(y, ln_ffn_post[l])
    return x


def setup_inputs(seed=0):
    out = dict(first_inputs(seed))
    for name, value in second_inputs(seed + 1).items():
        if name != "x":
            out[name + "_2"] = value
    return out


def reference(
    x, c, positions, w_ada, b_ada, g_pre_mix, g_post_mix, w_in, g_q, w_uq, g_kv, w_uk, w_uv,
    w_gate_up, b_gate, g_gla, w_out, g_pre_ffn, g_post_ffn, w_ffn_gate, w_ffn_up, w_ffn_down,
    mem_2, rel_bias_2, ln_mix_pre_2, ln_mix_post_2, ln_x_pre_2, ln_x_post_2, ln_mem_2,
    ln_ffn_pre_2, ln_ffn_post_2, w_in_2, cmp_pe_2, cmp_w1_2, cmp_w2_2, w_pool_2, pool_scale_2,
    w_br_attn_2, w_br_pool_2, w_mix_out_2, w_xq_2, w_xkv_2, w_xo_2, w_gate_2, w_up_2, w_down_2,
):
    x = first_block(
        x, c, positions, w_ada, b_ada, g_pre_mix, g_post_mix, w_in, g_q, w_uq, g_kv, w_uk, w_uv,
        w_gate_up, b_gate, g_gla, w_out, g_pre_ffn, g_post_ffn, w_ffn_gate, w_ffn_up,
        w_ffn_down,
    )
    return second_block(
        x, mem_2, rel_bias_2, ln_mix_pre_2, ln_mix_post_2, ln_x_pre_2, ln_x_post_2, ln_mem_2,
        ln_ffn_pre_2, ln_ffn_post_2, w_in_2, cmp_pe_2, cmp_w1_2, cmp_w2_2, w_pool_2,
        pool_scale_2, w_br_attn_2, w_br_pool_2, w_mix_out_2, w_xq_2, w_xkv_2, w_xo_2, w_gate_2,
        w_up_2, w_down_2,
    )


_drawn_inputs = setup_inputs


def setup_inputs(seed=0):
    import zlib

    import numpy as np

    out = dict(_drawn_inputs(seed))
    spreads = {}
    factors = {'g_pre_mix': 2.747,
     'g_post_mix': 4.431,
     'g_q': 8.0,
     'g_kv': 7.691,
     'g_gla': 15.135,
     'g_pre_ffn': 4.171,
     'g_post_ffn': 18.768,
     'rel_bias_2': 2.868,
     'ln_mix_pre_2': 4.563,
     'ln_mix_post_2': 4.875,
     'ln_x_pre_2': 5.249,
     'ln_x_post_2': 14.878,
     'ln_mem_2': 3.442,
     'ln_ffn_pre_2': 3.566,
     'ln_ffn_post_2': 17.056,
     'cmp_pe_2': 24.174,
     'pool_scale_2': 5.413}
    for name, (base, spread) in spreads.items():
        noise = np.random.default_rng([zlib.crc32(name.encode()), seed]).standard_normal(out[name].shape)
        drawn = base * np.exp(spread * noise) if base else spread * noise
        out[name] = __import__('jax').numpy.asarray(drawn.astype(out[name].dtype))
    for name, factor in factors.items():
        out[name] = (out[name] * factor).astype(out[name].dtype)
    return out
```

```python
from contextlib import ExitStack, contextmanager

import numpy as np

import concourse.bass as bass
from concourse import mybir

F32 = mybir.dt.float32
F32R = mybir.dt.float32r
I32 = mybir.dt.int32
U32 = mybir.dt.uint32
ACT = mybir.ActivationFunctionType
ALU = mybir.AluOpType
AX = mybir.AxisListType

P = 128
SEQ, D, RB = 256, 2048, 2
KT = D // P
EPS = 1e-6
NEG = -1e30
MH, QR, KVR, NOPE, ROPE, VD = 8, 512, 256, 128, 64, 128
QKD = NOPE + ROPE
HALF = ROPE // 2
GH, GK, GV, CH = 4, 128, 256, 64
GKEY, GVAL, GR = GH * GK, GH * GV, 16
NCH = SEQ // CH
Z_CQ, Z_CKV, Z_KR = 0, QR, QR + KVR
Z_QG = Z_KR + ROPE
Z_KG = Z_QG + GKEY
Z_VG = Z_KG + GKEY
Z_AG = Z_VG + GVAL
Z_RG = Z_AG + GR
ZW = Z_RG + GVAL
ZC, ZN = ZW // 8, 8
NH, NG, HD = 16, 4, 64
HPG = NH // NG
KVW = NG * HD
CL, CS, CHID = 32, 16, 128
NCMP = (SEQ - CL) // CS + 1
NCMP0 = (P - CL) // CS + 1
POOLW = (2, 4, 8, 16)
PG, PGW = 4, 256
Z2_KV = NH * HD
Z2_GL = Z2_KV + 6 * KVW
Z2_U = Z2_GL + 3 * NH
Z2_M = Z2_U + PG * PGW
Z2W = Z2_M + 2 * D
Z2C, Z2N = Z2W // 24, 24
XH, XD = 4, 128
DFF = 5632
FN = DFF // 512
BUCKETS, MAXD = 32, 2048
TWO_PI_PARTS = (6.28125, 0.0019350051879882812, 3.019916050561733e-07)
MAGIC = 12582912.0

C_ID, C_TRI, C_BLK, C_ONE, C_FLIP, C_MASK, C_INVF = 0, 128, 256, 384, 512, 640, 1024
CONST_W = C_INVF + HALF


def shape_constants():
    i = np.arange(P)
    c = np.zeros((P, CONST_W), np.float32)
    c[:, C_ID:C_ID + P] = np.eye(P)
    same = (i[:, None] // CH) == (i[None, :] // CH)
    c[:, C_TRI:C_TRI + P] = same & (i[:, None] <= i[None, :])
    c[:, C_BLK:C_BLK + P] = same
    c[:, C_ONE:C_ONE + P] = 1.0
    c[:, C_FLIP:C_FLIP + P] = np.eye(P)[::-1]
    causal = np.where(i[None, :] <= i[:, None], 0.0, NEG)
    c[:, C_MASK:C_MASK + P] = causal
    c[:, C_MASK + 2 * P:C_MASK + 3 * P] = causal
    c[:, C_INVF:] = (1.0 / (np.float32(10000.0) ** (np.arange(0, ROPE, 2, dtype=np.float32) / np.float32(ROPE))))
    t = np.arange(SEQ)
    band = np.zeros((P, PG, 3 * P), np.float32)
    for g, w in enumerate(POOLW):
        m = ((t[:, None] - t[None, :] >= 0) & (t[:, None] - t[None, :] < w)) / np.minimum(t + 1, w)[:, None]
        m = (m - np.eye(SEQ)).T
        band[:, g, :SEQ] = m[:P]
        band[:, g, SEQ:] = m[P:, P:]
    n = np.maximum(SEQ - 1 - np.arange(SEQ), 0)
    exact = BUCKETS // 2
    big = exact + (np.log(np.maximum(n, 1) / exact) / np.log(MAXD / exact) * (BUCKETS - exact)).astype(np.int64)
    bucket = np.where(n < exact, n, np.minimum(big, BUCKETS - 1))
    onehot = (np.arange(BUCKETS)[:, None] == bucket[None, :]).astype(np.float32)
    return c, band.reshape(P, PG * 3 * P), onehot


class Slabs:

    def __init__(self):
        self.raw = self.lin = 0
        self.i = None
        self.praw = self.plin = 0

    @contextmanager
    def loop(self, i, count, praw, plin):
        assert praw % 4 == 0 and plin % 2 == 0
        r, n = self.raw, self.lin
        self.i, self.praw, self.plin = i, praw, plin
        yield
        assert self.raw == r + praw and self.lin == n + plin, (self.raw - r, self.lin - n)
        self.i = None
        self.raw += praw * (count - 1)
        self.lin += plin * (count - 1)

    def plus(self, value, per):
        return value if self.i is None else self.i * per + value

    def raws(self, ahead=0):
        return self.plus(self.raw + ahead, self.praw)

    def lins(self, ahead=0):
        return self.plus(self.lin + ahead, self.plin)

    def landed(self):
        return self.plus(16 * (self.raw // 4 + 1), 4 * self.praw)

    def next(self, linear=True):
        self.raw += 1
        self.lin += linear


class Chain:

    def __init__(self, eng, sem):
        self.eng, self.sem, self.n = eng, sem, 0

    def __call__(self, ins):
        self.n += 1
        ins.then_inc(self.sem, 1)
        self.eng.wait_ge(self.sem, self.n)


TURNS = [("mem", 8, 1), ("x", 8, 1), ("cq", 2, 1), ("ckv", 1, 1), ("o", 8, 0), ("f1", 8, 1), ("z2", 8, 1),
         ("att", 4, 0), ("y", 8, 0), ("xq", 8, 1), ("xo", 2, 0), ("f2", 8, 1)]
TURN_N = {name: n for name, n, _ in TURNS}
TURN0 = {name: sum(m[1] for m in TURNS[:k]) for k, (name, _, _) in enumerate(TURNS)}
GAIN0 = {name: sum(m[1] * m[2] for m in TURNS[:k]) for k, (name, _, _) in enumerate(TURNS)}
GAINED = {name for name, _, gain in TURNS if gain}
NORMS = ["mem", "x", "cq", "ckv", "o", "f1", "y1", "z2", "mix", "xq", "xo", "f2", "y2"]
ROWED = ["mem", "x", "cq", "ckv", "f1", "z2", "xq", "f2"]
CHUNKS = [("xkv", 2), ("zin", ZN), ("uq", 3), ("uv", 2), ("wout", 4), ("zin2", Z2N), ("mix", 4), ("xq", 1), ("xo", 4)]
CHUNK0 = {name: sum(n for _, n in CHUNKS[:k]) for k, (name, _) in enumerate(CHUNKS)}


def build(nc, A, out):
    ctx = ExitStack()
    with ctx:
        named = {}

        def S(name):
            if name not in named:
                named[name] = ctx.enter_context(nc.semaphore(name))
            return named[name]

        base = [-(-nc.sbuf_base // 64) * 64]

        def sb(name, shape, dt=F32):
            t = nc.alloc_sbuf_tensor_at(name, shape, dt, offset=base[0])
            base[0] += -(-4 * int(np.prod(shape[1:])) // 32) * 32
            return t

        def at(name, shape, offset, dt=F32):
            return nc.alloc_sbuf_tensor_at(name, shape, dt, offset=offset)

        raw = sb("raw", [P, 4, 2048])
        wh = sb("wh", [P, 2, 2048], F32R)
        wl = sb("wl", [P, 2, 2048], F32R)
        X = sb("X", [P, RB, D])
        xt0 = base[0]
        XTh = sb("XTh", [P, KT, SEQ], F32R)
        xt1 = base[0]
        XTl = sb("XTl", [P, KT, SEQ], F32R)
        xkT = sb("xkT", [P, XH, SEQ])
        xv = sb("xv", [P, RB, XH * XD])
        zb = base[0]
        ZB = sb("ZB", [P, RB * Z2W])
        misc = base[0]
        MISC = sb("MISC", [P, 5120])
        CON = sb("CON", [P, CONST_W])
        vT = sb("vT", [P, P])
        bT = sb("bT", [P, P])
        modA = sb("modA", [P, 4, KT])
        gT = sb("gT", [P, KT])
        cT = sb("cT", [P, KT])
        nstat = sb("nstat", [P, len(NORMS), 3, RB])
        eps = sb("eps", [P, 1])
        one = sb("one", [P, 1])
        mtmp = sb("mtmp", [P, KT])
        msum = sb("msum", [P, 2 * KT])
        nwt = sb("nwt", [P, 4, 3])
        ang = sb("ang", [P, RB, 2, HALF])
        cs = sb("cs", [P, RB, 2, HALF])
        posi = sb("posi", [P, RB], I32)
        posf = sb("posf", [P, RB])
        assert base[0] <= nc.sbuf_usable_end, (base[0], nc.sbuf_usable_end)

        Z = at("Z", [P, RB, ZW], zb)
        Z2 = at("Z2", [P, RB, Z2W], zb)
        ROWB = at("ROWB", [P, RB, D], zb)
        MEM = at("MEM", [P, RB, D], zb + 4 * 4096)
        HROW = at("HROW", [P, RB, 512], zb + 4 * 4096)
        SIL = at("SIL", [P, RB, 512], zb + 4 * 5120)
        JUNK = at("JUNK", [P, D], zb + 4 * 8192)
        TMP = at("TMP", [P, 2, 512], zb + 4 * 10240)
        HTh = at("HTh", [P, 4, SEQ], zb + 4 * 11264, F32R)
        HTl = at("HTl", [P, 4, SEQ], zb + 4 * 12288, F32R)
        ACC = at("ACC", [P, D], zb + 4 * 13408)
        wgu = at("wgu", [GR, GKEY], zb + 4 * 11264)
        bgr = at("bgr", [1, GKEY], zb + 4 * 11776)
        aT = at("aT", [GR, SEQ], zb + 4 * 12288)
        VROW = at("VROW", [P, P], zb + 4 * 12928)
        BROW = at("BROW", [P, P], zb + 4 * 13056)
        G = at("G", [P, D], misc)
        assert xt1 - xt0 == 4 * 4096 and zb + 4 * 15360 <= misc

        PB = [ctx.enter_context(nc.psum_tensor(f"bank{b}", [P, 512], F32)) for b in range(8)]

        ident = CON[:, C_ID:C_ID + P]
        tri = CON[:, C_TRI:C_TRI + P]
        blk = CON[:, C_BLK:C_BLK + P]
        ones = CON[:, C_ONE:C_ONE + P]
        flip = CON[:, C_FLIP:C_FLIP + P]
        mask3 = CON[:, C_MASK:C_MASK + 3 * P]
        invf = CON[:, C_INVF:C_INVF + HALF]
        V_PRE_MIX, V_PRE_FFN, V_LN_MIX, V_LN_X, V_LN_MEM, V_LN_FFN, V_C, V_GQ, V_GKV, V_PS = (
            0, 16, 32, 48, 64, 80, 96, 112, 116, 118)

        def f32(ap):
            return ap.bitcast(F32)

        def scr(name, off, shape):
            return at(name, shape, xt0 + 4 * off)

        la = scr("la", 0, [P, RB, GKEY])
        eb = scr("eb", 1024, [P, RB, GKEY])
        einv = scr("einv", 2048, [P, RB, GKEY])
        kd = scr("kd", 3072, [P, RB, GKEY])
        bcs = scr("bcs", 4096, [P, RB, GKEY])
        qdT = scr("qdT", 5120, [P, GH, SEQ])
        kiT = scr("kiT", 6144, [P, GH, SEQ])
        attT = scr("attT", 7168, [P, GH, RB, P])
        states = at("states", [P, GH, 3, GV], misc + 4 * 2048)
        decay = sb("decay", [P, GH, NCH])
        ggla = at("ggla", [P, GV], zb + 4 * 12544)
        gst = sb("gst", [P, 3, GH, RB])
        qrow = [at(f"qrow{r}", [P, MH, QKD], (xt0, xt1)[r] + 4 * 1536) for r in range(RB)]
        kTn = [at(f"kTn{r}", [P, 4, SEQ], (xt0, xt1)[r] + 4 * 3072) for r in range(2)]
        vrow = at("vrow", [P, RB, MH * VD], misc + 4 * 2048)
        qTs = at("qTs", [P, 2, 512], misc + 4 * 4096)
        krT = at("krT", [ROPE, SEQ], zb + 4 * 11264)
        prob = at("prob", [P, 2, 384], zb + 4 * 11520)
        probT = at("probT", [P, 2, 384], zb + 4 * 12288)
        rt = [at(f"rt{k}", [P, MH, HALF], zb + 4 * (8192 + 256 * k)) for k in range(4)]
        ropes = at("ropes", [P, 3, HALF], zb + 4 * 12800)
        mst = sb("mst", [P, 4, 3, RB])
        QT = at("QT", [HD, NH, SEQ], xt0)
        relraw = at("relraw", [P, NH, SEQ], xt0)
        KT2 = at("KT2", [HD, NG, 2, SEQ], xt0 + 4 * 4096)
        rawT = at("rawT", [HD, 2, NG, SEQ], xt0 + 4 * 6144)
        REL = at("REL", [P, NH, SEQ], misc)
        pT = at("pT", [P, 2, 512], misc + 4 * 4096)
        w1s = at("w1s", [HD, CL, CHID], misc)
        w2s = at("w2s", [CHID, 2, HD], misc + 4 * 4096)
        peT = at("peT", [HD, 2, CL], misc + 4 * 4224)
        perow = at("perow", [2 * CL, HD], misc + 4 * 4288)
        blkT = at("blkT", [HD, 2, NG, NCMP], misc + 4 * 4352)
        hidT = at("hidT", [CHID, 2, NG * NCMP], misc + 4 * 4480)
        relrow = at("relrow", [NH, 384], misc + 4 * 4608)
        rb16 = at("rb16", [NH, BUCKETS], misc + 4 * 4992)
        rbT = at("rbT", [BUCKETS, NH], misc + 4 * 5024)
        onehot = at("onehot", [BUCKETS, SEQ], xt0 + 4 * 4096)
        kcT = sb("kcT", [HD, NG, NCMP])
        vc = sb("vc", [NCMP, NG, HD])
        pcT = sb("pcT", [NCMP, 2, P])
        pc = sb("pc", [P, 2, 16])
        nst = sb("nst", [P, 4, 3, 3])
        band = at("band", [P, PG, 3 * P], misc)
        assert base[0] <= nc.sbuf_usable_end, (base[0], nc.sbuf_usable_end)
        NSPROB = lambda k: Z2[:, k, Z2_KV:Z2_KV + 512]
        xqT = at("xqT", [P, XH, SEQ], xt0)
        TMPP = at("TMPP", [P, 2, 512], misc + 4 * 1536)
        xp = at("xp", [P, 2, 512], xt0 + 4 * 1024)
        xpT = at("xpT", [P, 2, 512], xt0 + 4 * 2048)

        rel_d = nc.dram_tensor("rel_scratch", [NH, 384], F32, kind="Internal").ap()

        def kview(w, rows):
            return w.rearrange("(t p) n -> p t n", p=P)

        W = {k: kview(A[k], None) for k in (
            "w_ada", "w_in", "w_uq", "w_uk", "w_uv", "w_out", "w_ffn_gate", "w_ffn_up", "w_ffn_down", "w_in_2",
            "w_br_attn_2", "w_br_pool_2", "w_mix_out_2", "w_xq_2", "w_xkv_2", "w_xo_2", "w_gate_2", "w_up_2",
            "w_down_2")}
        wpool = A["w_pool_2"].rearrange("g (t p) n -> p g t n", p=P)

        block = ctx.enter_context(nc.Block())
        slab_done, hi_made, slab_used, chunk_out = S("slab_done"), S("hi_made"), S("slab_used"), S("chunk_out")
        landed = [S(f"slab_landed{k}") for k in range(4)]

        @block.sync
        def _(sp):
            st = Slabs()

            def slab(src, parts, linear=True):
                r = st.raw
                if r >= 4:
                    sp.wait_ge(slab_done, st.raws(-3))
                n = int(np.prod(parts))
                dst = raw[:, r % 4, 0:n]
                if len(parts) == 2:
                    dst = dst.rearrange("p (t n) -> p t n", t=parts[0])
                if len(parts) == 3:
                    dst = dst.rearrange("p (g t n) -> p g t n", g=parts[0], t=parts[1])
                sp.dma_start(dst, src).then_inc(landed[r % 4], 16)
                st.next(linear)

            def ada(v, k):
                slab(W["w_ada"][:, k, v * D:(v + 1) * D], (D,), False)

            def cols(w, s, c0, width):
                slab(W[w][:, 4 * s:4 * s + 4, c0:c0 + width], (4, width))

            def load(name, dst, src, **how):
                sp.dma_start(dst, src, **how).then_inc(S(name), 16)

            load("mem_in", MEM[:, :, :], A["mem_2"].rearrange("(r p) n -> p r n", p=P))
            load("con_in", CON[:, :], A["const"])
            at_row = 0
            for name, n in (("g_pre_mix", 16), ("g_pre_ffn", 16), ("ln_mix_pre_2", 16), ("ln_x_pre_2", 16),
                            ("ln_mem_2", 16), ("ln_ffn_pre_2", 16), ("c", 16), ("g_q", 4), ("g_kv", 2),
                            ("pool_scale_2", 8)):
                load("vec_in", VROW[at_row:at_row + n, :], A[name].rearrange("(t p) -> t p", p=P))
                at_row += n
            load("vec_in", BROW[0:96, :], A["b_ada"].rearrange("(t p) -> t p", p=P))
            load("vec_in", BROW[96:112, :], A["g_post_mix"].rearrange("(t p) -> t p", p=P))
            load("vec_in", BROW[112:128, :], A["g_post_ffn"].rearrange("(t p) -> t p", p=P))
            load("pos_in", posi[:, :], A["positions"].rearrange("(r p) -> p r", p=P), allow_slow_non_contiguous=True)
            load("x_in", X[:, :, :], A["x"].rearrange("(r p) n -> p r n", p=P))
            for c in range(2):
                for s in range(4):
                    cols("w_xkv_2", s, 512 * c, 512)
                    for k in range(4):
                        ada(c, 4 * s + k)
            with sp.Fori(0, 2) as i, st.loop(i, 2, 32, 16):
                for c in range(4):
                    for s in range(4):
                        slab(W["w_in"][:, 4 * s:4 * s + 4, bass.ds(i * (4 * ZC) + c * ZC, ZC)], (4, ZC))
                        slab(W["w_ada"][:, 4 * c + s, bass.ds(i * D + 2 * D, D)], (D,), False)
            cols("w_uq", 0, 0, 512)
            load("gla_in", wgu[:, :], A["w_gate_up"])
            load("gla_in", bgr[:, :], A["b_gate"].rearrange("(a n) -> a n", a=1))
            load("gla_in", ggla[:, :], A["g_gla"].partition_broadcast(P))
            for k in range(16):
                ada(4, k)
            for c in (1, 2):
                cols("w_uq", 0, 512 * c, 512)
            slab(W["w_uk"], (2, 1024))
            slab(W["w_uv"], (2, 1024))
            for c in range(4):
                for s in range(4):
                    cols("w_out", s, 512 * c, 512)
                    ada(5, 4 * c + s)

            def ffn(gate, up, down):
                def part(w, j):
                    for s in range(4):
                        src = bass.ds(j * 512, 512) if st.i is not None else slice(j * 512, j * 512 + 512)
                        slab(W[w][:, 4 * s:4 * s + 4, src], (4, 512))

                def part_down(j):
                    for n in range(4):
                        src = bass.ds(j * 4, 4) if st.i is not None else slice(j * 4, j * 4 + 4)
                        slab(W[down][:, src, 512 * n:512 * n + 512], (4, 512))

                part(gate, 0)
                part(up, 0)
                with sp.Fori(0, FN - 1) as i, st.loop(i, FN - 1, 12, 12):
                    part(gate, i + 1)
                    part(up, i + 1)
                    part_down(i)
                part_down(FN - 1)

            ffn("w_ffn_gate", "w_ffn_up", "w_ffn_down")
            with sp.Fori(0, Z2N // 2) as i, st.loop(i, Z2N // 2, 8, 8):
                for c in range(2):
                    for s in range(4):
                        slab(W["w_in_2"][:, 4 * s:4 * s + 4, bass.ds(i * (2 * Z2C) + c * Z2C, Z2C)], (4, Z2C))
            slab(wpool, (4, 2, 256))
            sp.wait_ge(S("x_added"), 4)
            for k in range(2):
                load("cmp_in", w2s[:, k, :], A["cmp_w2_2"][k])
                load("cmp_in", perow[CL * k:CL * k + CL, :], A["cmp_pe_2"][k])
            load("cmp_in", rb16[:, :], A["rel_bias_2"])
            sp.wait_ge(chunk_out, RB * CHUNK0["mix"])
            load("onehot_in", onehot[:, :], A["onehot"])
            for k in range(2):
                if k:
                    sp.wait_ge(S("blk_used"), CL)
                load("w1_in", w1s[:, :, :], A["cmp_w1_2"][k].rearrange("(l d) n -> d l n", d=HD))
            sp.wait_ge(S("rel_row"), 1)
            sp.wait_ge(S("pe_out"), 3)
            load("rel_out", rel_d, relrow[:, :])
            sp.wait_ge(S("rel_out"), 16)
            src = bass.AP(rel_d.tensor, 0, [[1, P], [384, NH], [1, SEQ]])
            load("rel_in", relraw[:, :, :], src)
            sp.wait_ge(S("nsa_o"), 3 * NH * RB)
            load("band_in", band[:, :, :], A["band"].rearrange("p (g n) -> p g n", g=PG))
            for c in range(4):
                for w in ("w_br_attn_2", "w_br_pool_2"):
                    for s in range(2):
                        cols(w, s, 512 * c, 512)
            sp.wait_ge(S("pool_lo"), 2 * PG)
            load("gain_in", G[:, :], A["ln_mix_post_2"].partition_broadcast(P))
            for c in range(4):
                for s in range(4):
                    cols("w_mix_out_2", s, 512 * c, 512)
            for s in range(4):
                cols("w_xq_2", s, 0, 512)
            sp.wait_ge(S("x_added"), 6)
            load("gain_in", G[:, :], A["ln_x_post_2"].partition_broadcast(P))
            for c in range(4):
                cols("w_xo_2", 0, 512 * c, 512)
            ffn("w_gate_2", "w_up_2", "w_down_2")
            sp.wait_ge(S("x_added"), 8)
            load("gain_in", G[:, :], A["ln_ffn_post_2"].partition_broadcast(P))
            for r in range(RB):
                sp.wait_ge(S("x_added"), 9 + r)
                load("stored", out.rearrange("(r p) n -> p r n", p=P)[:, r, :], X[:, r, :])
            sp.wait_ge(S("stored"), 16 * RB)
        @block.scalar
        def _(act):
            st = Slabs()

            def f(out_, in_, func, name, **kw):
                act.activation(out_, in_, func, **kw).then_inc(S(name), 1)

            def hi(width=2048):
                act.wait_ge(landed[st.raw % 4], st.landed())
                if st.lin >= 2:
                    act.wait_ge(slab_used, st.lins(-1))
                act.activation(wh[:, st.lin % 2, 0:width], raw[:, st.raw % 4, 0:width], ACT.Copy).then_inc(hi_made, 1)
                st.next()

            def skip(n=1):
                for _ in range(n):
                    st.next(False)

            def norm_stats(name, src, n):
                j = NORMS.index(name)
                for r in range(RB):
                    act.wait_ge(S("squared"), RB * j + r) if j + r else None
                    f(JUNK[:, 0:n], src(r), ACT.Square, "squared", accum_out=nstat[:, j, 0, r:r + 1])
                act.wait_ge(S("squared"), RB * j + RB)
                f(nstat[:, j, 1, :], nstat[:, j, 0, :], ACT.Sqrt, "rooted", scale=1.0 / n, bias=eps[:, 0:1])

            def norm_rows(name, src, dst):
                j = NORMS.index(name)
                act.wait_ge(S("rooted_inv"), j + 1)
                for r in range(RB):
                    f(dst(r), src(r), ACT.Copy, "normed", scale=nstat[:, j, 2, r:r + 1])

            def turn_hi(name, dst, k0=0, take=None):
                for b in range(TURN_N[name]):
                    g = TURN0[name] + b
                    if name in GAINED:
                        act.wait_ge(S("gained"), GAIN0[name] + b + 1)
                        src = TMP[:, g % 2, :]
                    else:
                        act.wait_ge(S("turned"), g + 1)
                        src = PB[4 + g % 2][:, :]
                    f(dst[:, k0 + 2 * b:k0 + 2 * b + 2, :].rearrange("p t n -> p (t n)"), src, ACT.Copy, "turn_hi")

            def chunk_evac(c, dst, width, scale=1.0, done=None, it=None):
                act.wait_ge(slab_used, done)
                for r in range(RB):
                    act.activation(dst(r), PB[2 * (c % 2) + r][:, 0:width], ACT.Copy, scale=scale).then_inc(chunk_out, 1)

            act.wait_ge(S("vec_out"), 2)
            f(cT[:, :], vT[:, V_C:V_C + 16], ACT.Silu, "c_gated")
            act.wait_ge(S("mem_in"), 16)
            act.wait_ge(S("zeroed"), 2)
            norm_stats("mem", lambda r: MEM[:, r, :], D)
            norm_rows("mem", lambda r: MEM[:, r, :], lambda r: ROWB[:, r, :])
            turn_hi("mem", XTh)
            hi()
            for s in range(4):
                skip(4)
                hi()
            chunk_evac(0, lambda r: HROW[:, r, :], 512, done=4)
            for b in range(2):
                act.wait_ge(S("xk_turned"), b + 1)
                f(xkT[:, 2 * b:2 * b + 2, :].rearrange("p h n -> p (h n)"), PB[6 + b][:, :], ACT.Copy, "xk_out")
            for s in range(3):
                skip(4)
                hi()
            skip(4)
            act.wait_ge(S("angle"), 2 * RB)
            for r in range(RB):
                for k in range(2):
                    f(cs[:, r, k, :], ang[:, r, k, :], ACT.Sin, "sines")
            act.wait_ge(S("x_in"), 16)
            norm_stats("x", lambda r: X[:, r, :], D)
            act.wait_ge(S("turned"), TURN0["x"])
            norm_rows("x", lambda r: X[:, r, :], lambda r: ROWB[:, r, :])
            chunk_evac(1, lambda r: xv[:, r, :], 512, done=8)
            turn_hi("x", XTh)
            hi()
            with act.Fori(0, 2) as i, st.loop(i, 2, 32, 16):
                for c in range(4):
                    for s in range(3):
                        skip()
                        hi(4 * ZC)
                    skip()
                    hi()
                    act.wait_ge(slab_used, st.lins(-1))
                    for r in range(RB):
                        act.activation(Z[:, r, bass.ds(i * (4 * ZC) + c * ZC, ZC)],
                                       PB[2 * (c % 2) + r][:, 0:ZC], ACT.Copy).then_inc(chunk_out, 1)
            for b in range(4):
                act.wait_ge(S("g_wide"), b + 1)
                f(G[:, 512 * b:512 * b + 512], PB[4 + b % 2][:, :], ACT.Copy, "g_out")
            for r in range(RB):
                act.wait_ge(S("gate_in"), r + 1)
                f(eb[:, r, :], PB[r][:, :], ACT.Abs, "gla_f")
            act.wait_ge(S("gla_f"), 2)
            for r in range(RB):
                f(einv[:, r, :], eb[:, r, :], ACT.Exp, "gla_f", scale=-1.0)
            act.wait_ge(S("gla_f"), 4)
            for r in range(RB):
                f(kd[:, r, :], einv[:, r, :], ACT.Ln, "log1p", bias=one[:, 0:1])
            for r in range(RB):
                act.wait_ge(S("cum"), r + 1)
                f(bcs[:, r, :], PB[2 + r][:, :], ACT.Copy, "bc_out")
            for r in range(RB):
                f(eb[:, r, :], PB[2 + r][:, :], ACT.Exp, "eb_out")
                f(einv[:, r, :], PB[2 + r][:, :], ACT.Exp, "einv_out", scale=-1.0)
            act.wait_ge(S("cum"), 2 * RB + 1)
            f(decay[:, :, :].rearrange("p h n -> p (h n)"), PB[5][:, 0:GH * NCH], ACT.Exp, "decay_out")
            for r in range(RB):
                act.wait_ge(S("left"), r + 1)
                f(kd[:, r, :], bcs[:, r, :], ACT.Exp, "edec_out")
            for k in range(4):
                act.wait_ge(S("qk_turned"), k + 1)
                dst = (qdT, kiT)[k % 2]
                f(dst[:, 2 * (k // 2):2 * (k // 2) + 2, :].rearrange("p h n -> p (h n)"), PB[k][:, :], ACT.Copy,
                  "qk_out")
            for r in range(RB):
                f(Z[:, r, Z_RG:Z_RG + GVAL], Z[:, r, Z_RG:Z_RG + GVAL], ACT.Silu, "r_gated")
            for h in range(GH):
                act.wait_ge(S("gla_o"), h + 1)
                for r in range(RB):
                    if h + r:
                        act.wait_ge(S("gla_sq"), RB * h + r)
                    f(JUNK[:, 0:GV], PB[h][:, GV * r:GV * r + GV], ACT.Square, "gla_sq",
                      accum_out=gst[:, 0, h, r:r + 1])
            act.wait_ge(S("gla_sq"), RB * GH)
            f(gst[:, 1, :, :], gst[:, 0, :, :], ACT.Sqrt, "gla_root", scale=1.0 / GV, bias=eps[:, 0:1])
            for name, c0, n in (("cq", Z_CQ, QR), ("ckv", Z_CKV, KVR)):
                norm_stats(name, lambda r: Z[:, r, c0:c0 + n], n)
                norm_rows(name, lambda r: Z[:, r, c0:c0 + n], lambda r: Z[:, r, c0:c0 + n])
            turn_hi("cq", XTh)
            turn_hi("ckv", XTh, 4)
            skip(16)
            for c in range(3):
                hi()
                chunk_evac(CHUNK0["uq"] + c, lambda r: qrow[r][:, :, :].rearrange("p h d -> p (h d)")[:, 512 * c:512 * c + 512],
                           512, scale=QKD ** -0.5, done=st.lin - 1)
            for b in range(4):
                if b == 1:
                    hi()
                act.wait_ge(S("kT_made"), b + 1) if b < 3 else act.wait_ge(slab_used, st.lins(-1))
                f(kTn[b // 2][:, 2 * (b % 2):2 * (b % 2) + 2, :].rearrange("p h n -> p (h n)"),
                  PB[(4, 5, 6, 7)[b]][:, :], ACT.Copy, "kT_out")
            for c in range(2):
                act.wait_ge(S("v_made"), c + 1) if c == 0 else act.wait_ge(slab_used, st.lins())
                for r in range(RB):
                    act.activation(vrow[:, r, 512 * c:512 * c + 512], PB[2 * ((CHUNK0["uv"] + c) % 2) + r][:, :],
                                   ACT.Copy).then_inc(chunk_out, 1)
            hi()
            act.wait_ge(S("kr_turned"), 1)
            f(krT[:, :], PB[4][0:ROPE, 0:SEQ], ACT.Copy, "kr_out")
            for h in range(MH + 2):
                if h < MH:
                    act.wait_ge(S("q_turned"), h + 1)
                    if h >= 2:
                        act.wait_ge(S("scored"), h - 1)
                    f(qTs[:, h % 2, 0:SEQ], PB[4 + h % 2][:, 0:SEQ], ACT.Copy, "q_out")
                    f(qTs[0:ROPE, h % 2, SEQ:2 * SEQ], PB[4 + h % 2][0:ROPE, SEQ:2 * SEQ], ACT.Copy, "q_out")
                g = h - 1
                if 0 <= g < MH:
                    act.wait_ge(S("maxed"), RB * (g + 1))
                    for r in range(RB):
                        part = prob[:, g % 2, P * r:P * (2 * r + 1)]
                        f(part, part, ACT.Exp, "exped", bias=mst[:, g % 4, 0, r:r + 1], accum_out=mst[:, g % 4, 1, r:r + 1])
                g = h - 2
                if 0 <= g < MH:
                    act.wait_ge(S("p_turned"), g + 1)
                    if g >= 2:
                        act.wait_ge(S("pv_done"), g - 1)
                    f(probT[:, g % 2, :], PB[2 + g % 2][:, 0:3 * P], ACT.Copy, "pT_out")
            turn_hi("o", XTh)
            for c in range(4):
                for s in range(4):
                    skip()
                    hi()
                chunk_evac(CHUNK0["wout"] + c, lambda r: ROWB[:, r, 512 * c:512 * c + 512], 512,
                           done=st.lin - 1)
            act.wait_ge(chunk_out, RB * CHUNK0["zin2"])
            norm_stats("o", lambda r: ROWB[:, r, :], D)

            def ffn(k, pre, more):
                norm_stats(pre, lambda r: X[:, r, :], D)
                norm_rows(pre, lambda r: X[:, r, :], lambda r: ROWB[:, r, :])
                turn_hi(pre, XTh)
                b0 = RB * FN * k

                def chunk(j):
                    for _ in range(4):
                        hi()
                    act.wait_ge(slab_used, st.lins(-1))
                    if not isinstance(j, int) or k or j:
                        act.wait_ge(S("h_made"), j * RB + b0)
                    for r in range(RB):
                        act.activation(SIL[:, r, :], PB[r][:, :], ACT.Silu).then_inc(S("silu_out"), 1)
                    for _ in range(3):
                        hi()

                def hidden_hi(j):
                    for b in range(2):
                        act.wait_ge(S("h_turned"), j * 2 + (b0 + b + 1))
                        act.activation(HTh[:, 2 * b:2 * b + 2, :].rearrange("p t n -> p (t n)"), PB[4 + b][:, :],
                                       ACT.Copy).then_inc(S("hid_hi"), 1)

                chunk(0)
                hi()
                hidden_hi(0)
                with act.Fori(0, FN - 1) as i, st.loop(i, FN - 1, 12, 12):
                    chunk(i + 1)
                    for _ in range(5):
                        hi()
                    hidden_hi(i + 1)
                for n in range(4):
                    if n < 3 or more:
                        hi()
                act.wait_ge(S("y_added"), 8 * (FN + 1) * (k + 1))
                norm_stats(("y1", "y2")[k], lambda r: ROWB[:, r, :], D)

            act.wait_ge(S("x_added"), 2)
            for b in range(4):
                act.wait_ge(S("g_wide"), 4 + b + 1)
                f(G[:, 512 * b:512 * b + 512], PB[6 + b % 2][:, :], ACT.Copy, "g_out")
            ffn(0, "f1", True)
            act.wait_ge(S("x_added"), 4)
            norm_stats("z2", lambda r: X[:, r, :], D)
            norm_rows("z2", lambda r: X[:, r, :], lambda r: ROWB[:, r, :])
            turn_hi("z2", XTh)
            with act.Fori(0, Z2N // 2) as i, st.loop(i, Z2N // 2, 8, 8):
                for c in range(2):
                    for s in range(3):
                        hi(4 * Z2C)
                    hi()
                    act.wait_ge(slab_used, st.lins(-1))
                    for r in range(RB):
                        act.activation(Z2[:, r, bass.ds(i * (2 * Z2C) + c * Z2C, Z2C)],
                                       PB[2 * (c % 2) + r][:, 0:Z2C], ACT.Copy).then_inc(chunk_out, 1)
            for k in range(4):
                act.wait_ge(S("raw_turned"), k + 1)
                f(rawT[:, k // 2, 2 * (k % 2):2 * (k % 2) + 2, :].rearrange("p g n -> p (g n)"),
                  PB[k % 4][0:HD, :], ACT.Copy, "raw_out")
            for k in range(2):
                act.wait_ge(S("blk_used"), CL * (k + 1))
                f(hidT[:, k, :], PB[4 + k][:, 0:NG * NCMP], ACT.Gelu_apprx_tanh, "gelued")
            act.wait_ge(S("kc_done"), 1)
            f(kcT[:, :, :].rearrange("p g n -> p (g n)"), PB[6][0:HD, 0:NG * NCMP], ACT.Copy, "kc_out")
            act.wait_ge(S("kc_done"), 2)
            f(vc[:, :, :].rearrange("p g n -> p (g n)"), PB[7][0:NCMP, 0:NG * HD], ACT.Copy, "kc_out")
            for k in range(8):
                act.wait_ge(S("rel_flipped"), k + 1)
                f(REL[:, 2 * k:2 * k + 2, :].rearrange("p h n -> p (h n)"), PB[k % 4][:, :], ACT.Copy, "rel_done")
            for k in range(8):
                act.wait_ge(S("nq_turned"), k + 1)
                f(QT[:, 2 * k:2 * k + 2, :].rearrange("p h n -> p (h n)"), PB[4 + k % 4][0:HD, :], ACT.Copy, "nq_out",
                  scale=HD ** -0.5)
            for k in range(4):
                act.wait_ge(S("nk_turned"), k + 1)
                f(KT2[:, k, :, :].rearrange("p b n -> p (b n)"), PB[k][0:HD, :], ACT.Copy, "nk_out")
            for r in range(RB):
                f(Z2[:, r, Z2_GL:Z2_U], Z2[:, r, Z2_GL:Z2_U], ACT.Sigmoid, "gates_out")
            for t in range(NH * RB + 2):
                u = t - 1
                if 0 <= u < NH * RB:
                    nk, nc_ = (P, NCMP0) if u % 2 == 0 else (SEQ, NCMP)
                    act.wait_ge(S("n_maxed"), u + 1)
                    for b in range(2):
                        f(NSPROB(u % 2)[:, b * nk:b * nk + nk], NSPROB(u % 2)[:, b * nk:b * nk + nk], ACT.Exp, "n_exped",
                          bias=nst[:, u % 4, 0, b:b + 1], accum_out=nst[:, u % 4, 1, b + 1:b + 2])
                    f(pc[:, u % 2, 0:nc_], pc[:, u % 2, 0:nc_], ACT.Exp, "n_exped",
                      bias=nst[:, u % 4, 0, 2:3], accum_out=nst[:, u % 4, 1, 0:1])
                u = t - 2
                if 0 <= u < NH * RB:
                    nb = 2 + 2 * (u % 2)
                    act.wait_ge(S("n_turned"), u + 1)
                    if u >= 2:
                        act.wait_ge(S("n_pv"), u - 1)
                    f(pT[:, u % 2, 0:nb * P], PB[4 + u % 2][:, 0:nb * P], ACT.Copy, "npT_out")
            for r in range(RB):
                f(Z2[:, r, Z2_M:Z2W], Z2[:, r, Z2_M:Z2W], ACT.Sigmoid, "merge_gated")
            for g in range(PG):
                act.wait_ge(S("pool_mixed"), 2 * g + 2)
                f(XTh[:, 2 * g:2 * g + 2, :].rearrange("p t n -> p (t n)"), PB[g][:, :], ACT.Copy, "pool_hi")
            hi()
            for g in range(PG):
                act.wait_ge(S("pool_scaled"), g + 1)
                f(XTh[:, 8 + 2 * g:10 + 2 * g, :].rearrange("p t n -> p (t n)"), TMPP[:, g % 2, :], ACT.Copy, "pool_hi")
            turn_hi("att", XTh)
            for c in range(4):
                for s in range(4):
                    hi()
            turn_hi("y", XTh)
            for c in range(4):
                for s in range(4):
                    hi()
                chunk_evac(CHUNK0["mix"] + c, lambda r: ROWB[:, r, 512 * c:512 * c + 512], 512,
                           done=st.lin - 1)
            act.wait_ge(chunk_out, RB * CHUNK0["xq"])
            norm_stats("mix", lambda r: ROWB[:, r, :], D)
            act.wait_ge(S("x_added"), 6)
            norm_stats("xq", lambda r: X[:, r, :], D)
            norm_rows("xq", lambda r: X[:, r, :], lambda r: ROWB[:, r, :])
            turn_hi("xq", XTh)
            for s in range(4):
                hi()
            chunk_evac(CHUNK0["xq"], lambda r: HROW[:, r, :], 512, scale=XD ** -0.5, done=st.lin - 1)
            for b in range(2):
                act.wait_ge(S("xq_turned"), b + 1)
                f(xqT[:, 2 * b:2 * b + 2, :].rearrange("p h n -> p (h n)"), PB[6 + b][:, :], ACT.Copy, "xq_out")
            for h in range(XH + 1):
                if h < XH:
                    act.wait_ge(S("x_maxed"), h + 1)
                    for r in range(RB):
                        if h >= 2:
                            act.wait_ge(S("xp_turned"), h - 1)
                        f(xp[:, h % 2, SEQ * r:SEQ * r + SEQ], PB[h % 2][:, SEQ * r:SEQ * r + SEQ], ACT.Exp, "x_exped",
                          bias=mst[:, h % 4, 0, r:r + 1], accum_out=mst[:, h % 4, 1, r:r + 1])
                g = h - 1
                if g >= 0:
                    act.wait_ge(S("xp_turned"), g + 1)
                    if g >= 2:
                        act.wait_ge(S("x_pv"), g - 1)
                    f(xpT[:, g % 2, :], PB[4 + g % 2][:, :], ACT.Copy, "xpT_out")
            turn_hi("xo", XTh, 12)
            for c in range(4):
                hi()
                chunk_evac(CHUNK0["xo"] + c, lambda r: ROWB[:, r, 512 * c:512 * c + 512], 512,
                           done=st.lin - 1)
            act.wait_ge(chunk_out, RB * (CHUNK0["xo"] + 4))
            norm_stats("xo", lambda r: ROWB[:, r, :], D)
            act.wait_ge(S("x_added"), 8)
            ffn(1, "f2", False)

        @block.tensor
        def _(pe):
            st = Slabs()

            def turn(name, src, ready):
                ready()
                for b in range(TURN_N[name]):
                    g = TURN0[name] + b
                    if g >= 2:
                        pe.wait_ge(S("turn_free"), g - 1)
                    for k in range(2):
                        for r in range(RB):
                            mm = pe.transpose(PB[4 + g % 2][:, SEQ * k + P * r:SEQ * k + P * r + P],
                                              src(r, 2 * b + k), ident)
                    mm.then_inc(S("turned"), 1)

            def turned_ready(name):
                pe.wait_ge(S("turn_free"), TURN0[name] + TURN_N[name])

            def slab_mm(banks, kts, width, first, last, lhs=None):
                hi_t, lo_t = lhs or (XTh, XTl)
                pe.wait_ge(slab_done, st.raws(1))
                n = len(kts)
                w = [t[:, st.lin % 2, 0:n * width].rearrange("p (t n) -> p t n", t=n) for t in (wh, wl)]
                for r in range(RB):
                    for q, k in enumerate(kts):
                        rows = slice(P * r, P * r + P)
                        out_ = PB[banks[r]][:, 0:width]
                        pe.matmul(out_, hi_t[:, k, rows], w[0][:, q, :], start=first and q == 0, stop=False)
                        pe.matmul(out_, hi_t[:, k, rows], w[1][:, q, :], start=False, stop=False)
                        mm = pe.matmul(out_, lo_t[:, k, rows], w[0][:, q, :], start=False, stop=last and q == n - 1)
                mm.then_inc(slab_used, 1)
                st.next()

            def chunk(c, kts, width, skip=0, free=None):
                if free is not None:
                    pe.wait_ge(chunk_out, free)
                elif c >= 2:
                    pe.wait_ge(chunk_out, RB * (c - 1))
                n = len(kts) // 4
                for s in range(n):
                    slab_mm((2 * (c % 2), 2 * (c % 2) + 1), kts[4 * s:4 * s + 4], width, s == 0, s == n - 1)
                    for _ in range(skip):
                        st.next(False)

            ALL = list(range(KT))

            def mod_sum(v):
                pe.wait_ge(slab_done, st.raws())
                if v:
                    pe.wait_ge(S("mod_ready"), v)
                for k in range(KT):
                    mm = pe.matmul(PB[7][:, k:k + 1], ACC[:, P * k:P * k + P], ones[:, 0:1], start=True, stop=True)
                mm.then_inc(S("mod_sum"), 1)

            def gain_rows(banks):
                for b in range(4):
                    if b >= 2:
                        pe.wait_ge(S("g_out"), gain_rows.n + b - 1)
                    for k in range(4):
                        mm = pe.matmul(PB[banks[b % 2]][:, P * k:P * k + P],
                                       gT[:, 4 * b + k:4 * b + k + 1].broadcast_to([P, P]), ident, start=True, stop=True)
                    mm.then_inc(S("g_wide"), 1)
                gain_rows.n += 4

            gain_rows.n = 0

            pe.wait_ge(S("con_in"), 16)
            pe.wait_ge(S("vec_in"), 16 * 13)
            pe.transpose(PB[0][:, 0:126], VROW[0:126, :], ident[0:126, 0:126]).then_inc(S("vec_turned"), 1)
            pe.transpose(PB[1][:, 0:P], BROW[:, :], ident).then_inc(S("vec_turned"), 1)
            turn("mem", lambda r, k: ROWB[:, r, P * k:P * k + P], lambda: pe.wait_ge(S("normed"), RB))
            turned_ready("mem")
            pe.wait_ge(S("vec_out"), 2)
            chunk(0, ALL, 512, skip=4)
            pe.wait_ge(chunk_out, RB)
            for b in range(2):
                for k in range(2):
                    for r in range(RB):
                        h = 2 * b + k
                        mm = pe.transpose(PB[6 + b][:, SEQ * k + P * r:SEQ * k + P * r + P], HROW[:, r, XD * h:XD * h + XD],
                                          ident)
                mm.then_inc(S("xk_turned"), 1)
            pe.wait_ge(S("xk_out"), 2)
            mod_sum(0)
            chunk(1, ALL, 512, skip=4)
            mod_sum(1)
            turn("x", lambda r, k: ROWB[:, r, P * k:P * k + P], lambda: pe.wait_ge(S("normed"), RB * 2))
            turned_ready("x")
            with pe.Fori(0, 2) as i, st.loop(i, 2, 32, 16):
                for c in range(4):
                    chunk(c, ALL, ZC, skip=1, free=i * 8 + (RB * (c + 1) if c else RB))
                pe.wait_ge(slab_done, st.raws())
                pe.wait_ge(S("mod_ready"), i + 2)
                for k in range(KT):
                    mm = pe.matmul(PB[7][:, k:k + 1], ACC[:, P * k:P * k + P], ones[:, 0:1], start=True, stop=True)
                mm.then_inc(S("mod_sum"), 1)
            pe.wait_ge(S("gate_ready"), 1)
            gain_rows((4, 5))
            pe.wait_ge(chunk_out, RB * CHUNK0["uq"])
            for r in range(RB):
                mm = pe.transpose(PB[6][0:GR, P * r:P * r + P], Z[:, r, Z_AG:Z_RG], ident)
            mm.then_inc(S("a_turned"), 1)
            pe.wait_ge(S("gla_in"), 48)
            pe.wait_ge(S("a_out"), 1)
            for r in range(RB):
                pe.matmul(PB[r][:, :], aT[:, P * r:P * r + P], wgu[:, :], start=True, stop=False)
                pe.matmul(PB[r][:, :], ones[0:1, :], bgr[:, :], start=False, stop=True).then_inc(S("gate_in"), 1)
            pe.wait_ge(S("log_a"), RB)
            for r in range(RB):
                pe.matmul(PB[2 + r][:, :], tri, la[:, r, :], start=True, stop=True).then_inc(S("cum"), 1)
            for r in range(RB):
                pe.matmul(PB[6 + r][:, :], blk, la[:, r, :], start=True, stop=True).then_inc(S("cum"), 1)
            pe.wait_ge(S("g_out"), 4)
            for h in range(GH):
                for r in range(RB):
                    n = NCH * h + 2 * r
                    mm = pe.matmul(PB[5][:, n:n + 2], la[:, r, GK * h:GK * h + GK], blk[:, 0:CH + 1:CH], start=True, stop=True)
            mm.then_inc(S("cum"), 1)
            pe.wait_ge(S("decayed"), 2 * RB)
            pe.wait_ge(S("einv_out"), RB)
            for b in range(4):
                c0 = (Z_QG, Z_KG)[b % 2]
                for k in range(2):
                    for r in range(RB):
                        h = 2 * (b // 2) + k
                        mm = pe.transpose(PB[b][:, SEQ * k + P * r:SEQ * k + P * r + P],
                                          Z[:, r, c0 + GK * h:c0 + GK * h + GK], ident)
                mm.then_inc(S("qk_turned"), 1)
            pe.wait_ge(S("qk_out"), 4)
            pe.wait_ge(S("decay_out"), 1)
            for b in range(2):
                for k in range(2):
                    for r in range(RB):
                        h, rows = 2 * b + k, slice(P * r, P * r + P)
                        mm = pe.matmul(PB[4 + b][:, SEQ * k + P * r:SEQ * k + P * r + P], kiT[:, h, rows],
                                       qdT[:, h, rows], start=True, stop=True)
                mm.then_inc(S("gla_scored"), 1)
            pe.wait_ge(S("left"), RB)
            pe.wait_ge(S("k_decayed"), RB)
            for m in range(3 * GH):
                h, n = m // 3, m % 3
                rows = slice(CH * (n % 2), CH * (n % 2) + CH)
                bank, half = (6 + h // 2, h % 2) if n == 1 else (h, n // 2)
                mm = pe.matmul(PB[bank][:, GV * half:GV * half + GV],
                               kd[rows, n // 2, GK * h:GK * h + GK],
                               Z[rows, n // 2, Z_VG + GV * h:Z_VG + GV * h + GV], start=True, stop=True)
                mm.then_inc(S("state_add"), 1)
            for h in range(GH):
                pe.wait_ge(S("stated"), 3 * GH)
                pe.wait_ge(S("att_masked"), 2)
                for r in range(RB):
                    o = PB[h][:, GV * r:GV * r + GV]
                    pe.matmul(o, attT[:, h, r, :], Z[:, r, Z_VG + GV * h:Z_VG + GV * h + GV], start=True,
                              stop=False, skip_group_check=True)
                    for n in range(2 * r, 2 * r + 2):
                        if n:
                            q = CH * (n % 2)
                            mm = pe.matmul(PB[h][q:q + CH, GV * r:GV * r + GV], qdT[:, h, CH * n:CH * n + CH],
                                           states[:, h, n - 1, :], start=False, stop=n % 2 == 1,
                                           skip_group_check=True)
                mm.then_inc(S("gla_o"), 1)
            turn("cq", lambda r, k: Z[:, r, Z_CQ + P * k:Z_CQ + P * k + P], lambda: pe.wait_ge(S("normed"), RB * 3))
            turn("ckv", lambda r, k: Z[:, r, Z_CKV + P * k:Z_CKV + P * k + P], lambda: pe.wait_ge(S("normed"), RB * 4))
            turned_ready("cq")
            pe.wait_ge(S("gla_done"), RB * GH)
            for c in range(3):
                chunk(CHUNK0["uq"] + c, [0, 1, 2, 3], 512)
                if c == 0:
                    for _ in range(16):
                        st.next(False)
                    mod_sum(4)
            turned_ready("ckv")
            pe.wait_ge(slab_done, st.raws(1))
            pe.wait_ge(S("mod_ready"), 5)
            w = [t[:, st.lin % 2, :].rearrange("p (t n) -> p t n", t=2) for t in (wh, wl)]
            for b in range(4):
                for k in range(2):
                    h = 2 * b + k
                    o = PB[4 + b][:, SEQ * k:SEQ * k + SEQ]
                    for t in range(2):
                        cols = slice(NOPE * h, NOPE * h + NOPE)
                        pe.matmul(o, w[0][:, t, cols], XTh[:, 4 + t, :], start=t == 0, stop=False)
                        pe.matmul(o, w[0][:, t, cols], XTl[:, 4 + t, :], start=False, stop=False)
                        mm = pe.matmul(o, w[1][:, t, cols], XTh[:, 4 + t, :], start=False, stop=t == 1)
                mm.then_inc(S("kT_made") if b < 3 else slab_used, 1)
            st.next()
            pe.wait_ge(slab_done, st.raws(1))
            w = [t[:, st.lin % 2, :].rearrange("p (t n) -> p t n", t=2) for t in (wh, wl)]
            for c in range(2):
                n = CHUNK0["uv"] + c
                pe.wait_ge(chunk_out, RB * (n - 1))
                for r in range(RB):
                    o, rows = PB[2 * (n % 2) + r][:, :], slice(P * r, P * r + P)
                    for t in range(2):
                        cols = slice(512 * c, 512 * c + 512)
                        pe.matmul(o, XTh[:, 4 + t, rows], w[0][:, t, cols], start=t == 0, stop=False)
                        pe.matmul(o, XTh[:, 4 + t, rows], w[1][:, t, cols], start=False, stop=False)
                        mm = pe.matmul(o, XTl[:, 4 + t, rows], w[0][:, t, cols], start=False, stop=t == 1)
                mm.then_inc(S("v_made") if c == 0 else slab_used, 1)
            st.next()
            pe.wait_ge(S("roped"), 2 * RB)
            pe.wait_ge(S("kT_out"), 4)
            for r in range(RB):
                mm = pe.transpose(PB[4][0:ROPE, P * r:P * r + P], Z[:, r, Z_KR:Z_QG], ident)
            mm.then_inc(S("kr_turned"), 1)
            pe.wait_ge(S("kr_out"), 1)
            pe.wait_ge(chunk_out, RB * CHUNK0["wout"])
            for t in range(MH + 3):
                if t < MH:
                    if t >= 2:
                        pe.wait_ge(S("q_out"), 2 * (t - 1))
                    for r in range(RB):
                        pe.transpose(PB[4 + t % 2][:, P * r:P * r + P], qrow[r][:, t, 0:NOPE], ident)
                        mm = pe.transpose(PB[4 + t % 2][0:ROPE, SEQ + P * r:SEQ + P * r + P], qrow[r][:, t, NOPE:QKD],
                                          ident)
                    mm.then_inc(S("q_turned"), 1)
                h = t - 1
                if 0 <= h < MH:
                    pe.wait_ge(S("q_out"), 2 * (h + 1))
                    if h >= 2:
                        pe.wait_ge(S("masked"), h - 1)
                    for r in range(RB):
                        nk = P * (r + 1)
                        o = PB[6 + h % 2][:, P * r:P * r + nk]
                        pe.matmul(o, qTs[:, h % 2, P * r:P * r + P], kTn[h // 4][:, h % 4, 0:nk], start=True, stop=False)
                        mm = pe.matmul(o, qTs[0:ROPE, h % 2, SEQ + P * r:SEQ + P * r + P], krT[:, 0:nk], start=False,
                                       stop=True)
                    mm.then_inc(S("scored"), 1)
                h = t - 2
                if 0 <= h < MH:
                    pe.wait_ge(S("exped"), RB * (h + 1))
                    if h >= 2:
                        pe.wait_ge(S("pT_out"), h - 1)
                    for b in range(3):
                        mm = pe.transpose(PB[2 + h % 2][:, P * b:P * b + P], prob[:, h % 2, P * b:P * b + P], ident)
                    mm.then_inc(S("p_turned"), 1)
                h = t - 3
                if 0 <= h < MH:
                    pe.wait_ge(S("pT_out"), h + 1)
                    if h >= 2:
                        pe.wait_ge(S("mla_o"), RB * (h - 1))
                    v = [vrow[:, r, VD * h:VD * h + VD] for r in range(RB)]
                    o = PB[h % 2]
                    pe.matmul(o[:, 0:VD], probT[:, h % 2, 0:P], v[0], start=True, stop=True)
                    pe.matmul(o[:, P:P + VD], probT[:, h % 2, P:2 * P], v[0], start=True, stop=False)
                    mm = pe.matmul(o[:, P:P + VD], probT[:, h % 2, 2 * P:3 * P], v[1], start=False, stop=True)
                    mm.then_inc(S("pv_done"), 1)
            turn("o", lambda r, k: Z[:, r, Z_QG + P * k:Z_QG + P * k + P], lambda: pe.wait_ge(S("mla_o"), RB * MH))
            turned_ready("o")
            for c in range(4):
                chunk(CHUNK0["wout"] + c, ALL, 512, skip=1)
            mod_sum(5)

            def ffn(k, pre, n_normed):
                b0 = RB * FN * k
                y0 = 8 * (FN + 1) * k
                turn(pre, lambda r, q: ROWB[:, r, P * q:P * q + P], lambda: pe.wait_ge(S("normed"), RB * n_normed))
                turned_ready(pre)
                pe.wait_ge(S("y_added"), y0 + 8)

                def gate_up(j):
                    for half in range(2):
                        if not isinstance(j, int):
                            pe.wait_ge(S(("silu_out", "h_made")[half]), j * RB + b0)
                            pe.wait_ge(S("y_added"), j * 8 + (y0 - 8 + (4, 8)[half]))
                        for s in range(4):
                            slab_mm((2 * half, 2 * half + 1), ALL[4 * s:4 * s + 4], 512, s == 0, s == 3)

                def hidden_turn(j):
                    pe.wait_ge(S("h_made"), j * RB + (b0 + RB))
                    if not isinstance(j, int):
                        pe.wait_ge(S("hid_lo"), j * 2 + b0)
                    for b in range(2):
                        for q in range(2):
                            for r in range(RB):
                                mm = pe.transpose(PB[4 + b][:, SEQ * q + P * r:SEQ * q + P * r + P],
                                                  HROW[:, r, P * (2 * b + q):P * (2 * b + q) + P], ident)
                        mm.then_inc(S("h_turned"), 1)

                def down(j):
                    pe.wait_ge(S("hid_lo"), j * 2 + (b0 + 2))
                    for n in range(4):
                        banks = ((6, 7), (0, 1), (6, 7), (2, 3))[n]
                        if n == 0 and not (isinstance(j, int) and j == 0):
                            pe.wait_ge(S("y_added"), j * 8 + (y0 + 6))
                        if n == 1:
                            pe.wait_ge(S("silu_out"), (j + 2) * RB + b0 if not isinstance(j, int) else RB * FN + b0)
                        if n == 2:
                            pe.wait_ge(S("y_added"), j * 8 + (y0 + 8 + 2))
                        if n == 3 and not isinstance(j, int):
                            pe.wait_ge(S("h_made"), (j + 2) * RB + b0)
                        slab_mm(banks, [0, 1, 2, 3], 512, True, True, lhs=(HTh, HTl))

                gate_up(0)
                hidden_turn(0)
                with pe.Fori(0, FN - 1) as i, st.loop(i, FN - 1, 12, 12):
                    gate_up(i + 1)
                    down(i)
                    hidden_turn(i + 1)
                down(FN - 1)

            pe.wait_ge(S("mod_ready"), 6)
            gain_rows((6, 7))
            ffn(0, "f1", 5)
            turn("z2", lambda r, k: ROWB[:, r, P * k:P * k + P], lambda: pe.wait_ge(S("normed"), RB * 6))
            turned_ready("z2")
            with pe.Fori(0, Z2N // 2) as i, st.loop(i, Z2N // 2, 8, 8):
                for c in range(2):
                    chunk(c, ALL, Z2C, free=i * 4 + RB * (CHUNK0["zin2"] + c - 1))
            pe.wait_ge(chunk_out, RB * CHUNK0["mix"])
            for b in range(4):
                for k in range(2):
                    for r in range(RB):
                        c0 = Z2_KV + KVW * (b // 2) + HD * (2 * (b % 2) + k)
                        mm = pe.transpose(PB[b][0:HD, SEQ * k + P * r:SEQ * k + P * r + P], Z2[:, r, c0:c0 + HD], ident)
                mm.then_inc(S("raw_turned"), 1)
            pe.wait_ge(S("cmp_in"), 80)
            pe.transpose(PB[6][0:HD, 0:2 * CL], perow[:, :], ident[0:2 * CL, 0:2 * CL]).then_inc(S("pe_turned"), 1)
            pe.transpose(PB[7][0:BUCKETS, 0:NH], rb16[:, :], ident[0:NH, 0:NH]).then_inc(S("pe_turned"), 1)
            for k in range(2):
                pe.wait_ge(S("w1_in"), 16 * (k + 1))
                for l in range(CL):
                    pe.wait_ge(S("blk_made"), CL * k + l + 1)
                    mm = pe.matmul(PB[4 + k][:, 0:NG * NCMP], w1s[:, l, :],
                                   blkT[:, l % 2, :, :].rearrange("p g n -> p (g n)"), start=l == 0, stop=l == CL - 1)
                    mm.then_inc(S("blk_used"), 1)
            pe.wait_ge(S("pe_out"), 3)
            pe.wait_ge(S("onehot_in"), 16)
            pe.matmul(PB[7][0:NH, 0:SEQ], rbT[:, :], onehot[:, :], start=True, stop=True).then_inc(S("rel_made"), 1)
            pe.wait_ge(S("gelued"), 2)
            pe.matmul(PB[6][0:HD, 0:NG * NCMP], w2s[:, 0, :], hidT[:, 0, :], start=True, stop=True).then_inc(S("kc_done"), 1)
            pe.wait_ge(S("rel_row"), 1)
            for g in range(NG):
                mm = pe.matmul(PB[7][0:NCMP, HD * g:HD * g + HD], hidT[:, 1, NCMP * g:NCMP * g + NCMP], w2s[:, 1, :],
                               start=True, stop=True)
            mm.then_inc(S("kc_done"), 1)
            pe.wait_ge(S("rel_in"), 16)
            pe.wait_ge(S("raw_out"), 4)
            for k in range(8):
                if k >= 4:
                    pe.wait_ge(S("rel_done"), k - 3)
                pe.matmul(PB[k % 4][:, :], flip, relraw[:, 2 * k:2 * k + 2, :].rearrange("p h n -> p (h n)"), start=True,
                          stop=True).then_inc(S("rel_flipped"), 1)
            pe.wait_ge(S("kc_out"), 2)
            for k in range(8):
                if k >= 4:
                    pe.wait_ge(S("nq_out"), k - 3)
                for q in range(2):
                    for r in range(RB):
                        h = 2 * k + q
                        mm = pe.transpose(PB[4 + k % 4][0:HD, SEQ * q + P * r:SEQ * q + P * r + P],
                                          Z2[:, r, HD * h:HD * h + HD], ident)
                mm.then_inc(S("nq_turned"), 1)
            pe.wait_ge(S("rel_done"), 8)
            for g in range(NG):
                for b in range(2):
                    for r in range(RB):
                        c0 = Z2_KV + KVW * (2 + 2 * b) + HD * g
                        mm = pe.transpose(PB[g][0:HD, SEQ * b + P * r:SEQ * b + P * r + P], Z2[:, r, c0:c0 + HD], ident)
                mm.then_inc(S("nk_turned"), 1)
            pe.wait_ge(S("nq_out"), 8)
            pe.wait_ge(S("nk_out"), 4)
            for t in range(NH * RB + 3):
                u = t - 2
                if 0 <= u < NH * RB:
                    r = u % 2
                    nk, n_c = P * (r + 1), (NCMP0, NCMP)[r]
                    pe.wait_ge(S("n_exped"), 3 * (u + 1))
                    if u >= 2:
                        pe.wait_ge(S("npT_out"), u - 1)
                    pe.wait_ge(S("n_added"), u + 1)
                    pe.transpose(PB[2 + u % 2][0:n_c, P:2 * P], pc[:, u % 2, 0:n_c], ident)
                    for b in range(2 * (r + 1)):
                        mm = pe.transpose(PB[4 + u % 2][:, P * b:P * b + P], NSPROB(u % 2)[:, P * b:P * b + P], ident)
                    mm.then_inc(S("n_turned"), 1)
                u = t
                if u < NH * RB:
                    h, r = u // 2, u % 2
                    g, nk, n_c = h // HPG, P * (r + 1), (NCMP0, NCMP)[r]
                    if u >= 2:
                        pe.wait_ge(S("n_added"), u - 1)
                    q = QT[:, h, P * r:P * r + P]
                    for b in range(2):
                        pe.matmul(PB[u % 2][:, nk * b:nk * b + nk], q, KT2[:, g, b, 0:nk], start=True, stop=True)
                    if u >= 2:
                        pe.wait_ge(S("n_cT"), u - 1)
                    pe.matmul(PB[2 + u % 2][:, 0:n_c], q, kcT[:, g, 0:n_c], start=True, stop=True)\
                        .then_inc(S("n_scored"), 1)
                u = t - 3
                if 0 <= u < NH * RB:
                    h, r = u // 2, u % 2
                    g, n_c = h // HPG, (NCMP0, NCMP)[r]
                    pe.wait_ge(S("npT_out"), u + 1)
                    pe.wait_ge(S("n_cT"), u + 1)
                    if u >= 2:
                        pe.wait_ge(S("nsa_o"), 3 * (u - 1))
                    for b in range(2):
                        for k in range(r + 1):
                            c0 = Z2_KV + KVW * (3 + 2 * b) + HD * g
                            blk_ = b * (r + 1) + k
                            pe.matmul(PB[6 + u % 2][:, HD * b:HD * b + HD], pT[:, u % 2, P * blk_:P * blk_ + P],
                                      Z2[:, k, c0:c0 + HD], start=k == 0, stop=k == r)
                    pe.matmul(PB[6 + u % 2][:, 2 * HD:3 * HD], pcT[0:n_c, u % 2, :], vc[0:n_c, g, :], start=True, stop=True)\
                        .then_inc(S("n_pv"), 1)
            pe.wait_ge(S("band_in"), 16)
            pe.wait_ge(S("nsa_o"), 3 * NH * RB)
            for m in range(2 * PG):
                g, t = m // 2, m % 2
                c0 = Z2_U + PGW * g + P * t
                o = PB[g][:, SEQ * t:SEQ * t + SEQ]
                pe.matmul(o, Z2[:, 0, c0:c0 + P], band[:, g, 0:SEQ], start=True, stop=False, skip_group_check=True)
                pe.matmul(PB[g][:, SEQ * t + P:SEQ * t + SEQ], Z2[:, 1, c0:c0 + P], band[:, g, SEQ:], start=False,
                          stop=True, skip_group_check=True).then_inc(S("pool_mixed"), 1)
            pe.wait_ge(slab_done, st.raws(1))
            w = [t[:, st.lin % 2, :].rearrange("p (g t n) -> p g t n", g=PG, t=2) for t in (wh, wl)]
            for g in range(PG):
                pe.wait_ge(S("pool_lo"), g + 1)
                for q in range(2):
                    o, cols = PB[4 + g][:, SEQ * q:SEQ * q + SEQ], slice(P * q, P * q + P)
                    for t in range(2):
                        pe.matmul(o, w[0][:, g, t, cols], XTh[:, 2 * g + t, :], start=t == 0, stop=False)
                        pe.matmul(o, w[0][:, g, t, cols], XTl[:, 2 * g + t, :], start=False, stop=False)
                        mm = pe.matmul(o, w[1][:, g, t, cols], XTh[:, 2 * g + t, :], start=False, stop=t == 1)
                mm.then_inc(S("pool_lin") if g < PG - 1 else slab_used, 1)
            st.next()
            pe.wait_ge(S("pool_lo"), 2 * PG)
            turn("att", lambda r, k: Z2[:, r, P * k:P * k + P], lambda: None)
            turned_ready("att")
            for c in range(4):
                if c:
                    pe.wait_ge(S("merged"), 3 * RB * c)
                for half in range(2):
                    for s in range(2):
                        k = 8 * half + 4 * s
                        slab_mm((2 * half, 2 * half + 1), ALL[k:k + 4], 512, s == 0, s == 1)
            turn("y", lambda r, k: Z2[:, r, P * k:P * k + P], lambda: pe.wait_ge(S("merged"), 3 * RB * 4))
            turned_ready("y")
            for c in range(4):
                chunk(CHUNK0["mix"] + c, ALL, 512)
            turn("xq", lambda r, k: ROWB[:, r, P * k:P * k + P], lambda: pe.wait_ge(S("normed"), RB * 7))
            turned_ready("xq")
            chunk(CHUNK0["xq"], ALL, 512)
            pe.wait_ge(chunk_out, RB * CHUNK0["xo"])
            for b in range(2):
                for k in range(2):
                    for r in range(RB):
                        h = 2 * b + k
                        mm = pe.transpose(PB[6 + b][:, SEQ * k + P * r:SEQ * k + P * r + P], HROW[:, r, XD * h:XD * h + XD],
                                          ident)
                mm.then_inc(S("xq_turned"), 1)
            pe.wait_ge(S("xq_out"), 2)
            for t in range(XH + 2):
                h = t
                if h < XH:
                    if h >= 2:
                        pe.wait_ge(S("x_exped"), RB * (h - 1))
                    for r in range(RB):
                        mm = pe.matmul(PB[h % 2][:, SEQ * r:SEQ * r + SEQ], xqT[:, h, P * r:P * r + P], xkT[:, h, :],
                                       start=True, stop=True)
                    mm.then_inc(S("x_scored"), 1)
                h = t - 1
                if 0 <= h < XH:
                    pe.wait_ge(S("x_exped"), RB * (h + 1))
                    if h >= 2:
                        pe.wait_ge(S("xpT_out"), h - 1)
                    for b in range(4):
                        mm = pe.transpose(PB[4 + h % 2][:, P * b:P * b + P], xp[:, h % 2, P * b:P * b + P], ident)
                    mm.then_inc(S("xp_turned"), 1)
                h = t - 2
                if 0 <= h < XH:
                    pe.wait_ge(S("xpT_out"), h + 1)
                    if h >= 2:
                        pe.wait_ge(S("xatt_o"), RB * (h - 1))
                    for r in range(RB):
                        for k in range(RB):
                            mm = pe.matmul(PB[2 + h % 2][:, P * r:P * r + XD], xpT[:, h % 2, P * (2 * r + k):P * (2 * r + k) + P],
                                           xv[:, k, XD * h:XD * h + XD], start=k == 0, stop=k == 1)
                    mm.then_inc(S("x_pv"), 1)
            turn("xo", lambda r, k: SIL[:, r, P * k:P * k + P], lambda: pe.wait_ge(S("xatt_o"), RB * XH))
            turned_ready("xo")
            for c in range(4):
                chunk(CHUNK0["xo"] + c, [12, 13, 14, 15], 512)
            ffn(1, "f2", 8)

        @block.vector
        def _(dve):
            st = Slabs()
            link = Chain(dve, S("dve_step"))

            def tt(out_, a, b, op):
                return dve.tensor_tensor(out_, a, b, op)

            def lo(width=2048):
                dve.wait_ge(hi_made, st.lins(1))
                tt(wl[:, st.lin % 2, 0:width], raw[:, st.raw % 4, 0:width], f32(wh[:, st.lin % 2, 0:width]),
                   ALU.subtract).then_inc(slab_done, 1)
                st.next()

            def ada(k):
                dve.wait_ge(landed[st.raw % 4], st.landed())
                if st.raw or st.i is not None:
                    dve.wait_ge(slab_done, st.raws())
                w = raw[:, st.raw % 4, :]
                if k == 0:
                    ins = dve.tensor_scalar(ACC[:, :], w, cT[:, 0:1], None, ALU.mult)
                else:
                    ins = dve.scalar_tensor_tensor(ACC[:, :], w, cT[:, k:k + 1], ACC[:, :], ALU.mult, ALU.add)
                ins.then_inc(slab_done, 1)
                st.next(False)

            def mod_fin(v):
                dve.wait_ge(S("mod_sum"), v + 1)
                if v in (0, 3):
                    tt(modA[:, (0, 0, 0, 2)[v], :], PB[7][:, 0:KT], bT[:, KT * v:KT * v + KT], ALU.add)\
                        .then_inc(S("mod_ready"), 1)
                elif v in (1, 4):
                    gain = vT[:, V_PRE_MIX:V_PRE_MIX + KT] if v == 1 else vT[:, V_PRE_FFN:V_PRE_FFN + KT]
                    link(tt(mtmp[:, :], PB[7][:, 0:KT], bT[:, KT * v:KT * v + KT], ALU.add))
                    dve.scalar_tensor_tensor(modA[:, 1 if v == 1 else 3, :], mtmp[:, :], 1.0, gain, ALU.add, ALU.mult)\
                        .then_inc(S("mod_ready"), 1)
                else:
                    gain = bT[:, 96:112] if v == 2 else bT[:, 112:128]
                    link(tt(mtmp[:, :], PB[7][:, 0:KT], bT[:, KT * v:KT * v + KT], ALU.add))
                    tt(gT[:, :], mtmp[:, :], gain, ALU.mult).then_inc(S("mod_ready"), 1)

            def norm_inv(name):
                j = NORMS.index(name)
                dve.wait_ge(S("rooted"), j + 1)
                dve.reciprocal(nstat[:, j, 2, :], nstat[:, j, 1, :]).then_inc(S("rooted_inv"), 1)

            def turn_lo(name, hi_t, lo_t, gain=None, shift=None, k0=0):
                n = TURN_N[name]

                def gained(b):
                    g = TURN0[name] + b
                    dve.wait_ge(S("turned"), g + 1)
                    for k in range(2):
                        kt = 2 * b + k
                        half = slice(SEQ * k, SEQ * k + SEQ)
                        if shift is None:
                            ins = dve.tensor_scalar(TMP[:, g % 2, half], PB[4 + g % 2][:, half], gain[:, kt:kt + 1], None,
                                                    ALU.mult)
                        else:
                            ins = dve.tensor_scalar(TMP[:, g % 2, half], PB[4 + g % 2][:, half], gain[:, kt:kt + 1],
                                                    shift[:, kt:kt + 1], ALU.mult, ALU.add)
                    ins.then_inc(S("gained"), 1)

                def rest(b):
                    g = TURN0[name] + b
                    dve.wait_ge(S("turn_hi"), g + 1)
                    src = TMP[:, g % 2, :] if gain is not None else PB[4 + g % 2][:, :]
                    sl = (slice(None), slice(k0 + 2 * b, k0 + 2 * b + 2), slice(None))
                    tt(lo_t[sl].rearrange("p t n -> p (t n)"), src, f32(hi_t[sl].rearrange("p t n -> p (t n)")),
                       ALU.subtract).then_inc(S("turn_free"), 1)

                if gain is None:
                    for b in range(n):
                        rest(b)
                else:
                    for b in range(n + 1):
                        if b < n:
                            gained(b)
                        if b:
                            rest(b - 1)

            def add_normed(name, width=D):
                j = NORMS.index(name)
                norm_inv(name)
                dve.wait_ge(S("rooted_inv"), j + 1)
                for r in range(RB):
                    link(dve.scalar_tensor_tensor(ROWB[:, r, :], ROWB[:, r, :], nstat[:, j, 2, r:r + 1], G[:, :], ALU.mult,
                                                  ALU.mult))
                    tt(X[:, r, :], X[:, r, :], ROWB[:, r, :], ALU.add).then_inc(S("x_added"), 1)

            dve.memset(eps[:, :], EPS).then_inc(S("zeroed"), 1)
            dve.memset(one[:, :], 1.0).then_inc(S("zeroed"), 1)
            for k in range(2):
                dve.wait_ge(S("vec_turned"), k + 1)
                n = (126, P)[k]
                dve.tensor_copy((vT, bT)[k][:, 0:n], PB[k][:, 0:n]).then_inc(S("vec_out"), 1)
            dve.wait_ge(S("pos_in"), 16)
            link(dve.tensor_copy(posf[:, :], posi[:, :]))
            for r in range(RB):
                for k in range(2):
                    a, t, m = ropes[:, 0, :], ropes[:, 1, :], ropes[:, 2, :]
                    quarter = 0.25 if k == 0 else 0.0
                    link(dve.tensor_scalar(a, invf, posf[:, r:r + 1], None, ALU.mult))
                    link(dve.tensor_scalar(t, a, 1.0 / (2.0 * np.pi), quarter, ALU.mult, ALU.add))
                    link(dve.tensor_scalar(m, t, MAGIC, None, ALU.add))
                    link(dve.tensor_scalar(t, m, -MAGIC, None, ALU.add))
                    for q, part in enumerate(TWO_PI_PARTS):
                        src, dst = ((a, m), (m, a), (a, m))[q]
                        link(dve.scalar_tensor_tensor(dst, t, -part, src, ALU.mult, ALU.add))
                    link(dve.tensor_scalar(a, m, np.pi / 2 if k == 0 else 0.0, None, ALU.add))
                    dve.tensor_scalar(ang[:, r, k, :], a, 3.1415925, -3.1415925, ALU.min, ALU.max).then_inc(S("angle"), 1)
                    if r + k < 2:
                        dve.wait_ge(S("angle"), 2 * r + k + 1)
            norm_inv("mem")
            turn_lo("mem", XTh, XTl, gain=vT[:, V_LN_MEM:V_LN_MEM + KT])
            dve.wait_ge(S("c_gated"), 1)
            lo()
            for c in range(2):
                for s in range(4):
                    for k in range(4):
                        ada(4 * s + k)
                    if c == 0 or s < 3:
                        lo()
                if c == 0:
                    mod_fin(0)
                    dve.wait_ge(S("mod_ready"), 1)
            norm_inv("x")
            mod_fin(1)
            dve.wait_ge(S("mod_ready"), 2)
            turn_lo("x", XTh, XTl, gain=modA[:, 1, :], shift=modA[:, 0, :])
            lo(4 * ZC)
            with dve.Fori(0, 2) as i, st.loop(i, 2, 32, 16):
                for c in range(4):
                    for s in range(4):
                        ada(4 * c + s)
                        if s < 3:
                            lo(4 * ZC)
                        elif c < 3:
                            lo()
                lo()
                dve.wait_ge(S("mod_sum"), i + 3)
                dve.tensor_copy(msum[:, bass.ds(i * KT, KT)], PB[7][:, 0:KT]).then_inc(S("mod_ready"), 1)
            dve.wait_ge(S("mod_ready"), 4)
            link(tt(mtmp[:, :], msum[:, 0:KT], bT[:, 2 * KT:3 * KT], ALU.add))
            tt(gT[:, :], mtmp[:, :], bT[:, 96:112], ALU.mult).then_inc(S("gate_ready"), 1)
            tt(modA[:, 2, :], msum[:, KT:2 * KT], bT[:, 3 * KT:4 * KT], ALU.add).then_inc(S("gate_ready"), 1)
            dve.wait_ge(S("a_turned"), 1)
            dve.tensor_copy(aT[:, :], PB[6][0:GR, 0:SEQ]).then_inc(S("a_out"), 1)
            for r in range(RB):
                dve.wait_ge(S("log1p"), r + 1)
                link(dve.scalar_tensor_tensor(la[:, r, :], PB[r][:, :], 0.0, kd[:, r, :], ALU.min, ALU.subtract))
                dve.tensor_scalar(la[:, r, :], la[:, r, :], 1.0 / 16.0, None, ALU.mult).then_inc(S("log_a"), 1)
            dve.wait_ge(S("cum"), 2 * RB)
            dve.wait_ge(S("einv_out"), RB)
            for r in range(RB):
                tt(bcs[:, r, :], PB[6 + r][:, :], bcs[:, r, :], ALU.subtract).then_inc(S("left"), 1)
            for r in range(RB):
                q, k = Z[:, r, Z_QG:Z_KG], Z[:, r, Z_KG:Z_VG]
                dve.scalar_tensor_tensor(q, q, GK ** -0.5, eb[:, r, :], ALU.mult, ALU.mult).then_inc(S("decayed"), 1)
                dve.wait_ge(S("edec_out"), r + 1)
                tt(kd[:, r, :], k, kd[:, r, :], ALU.mult).then_inc(S("k_decayed"), 1)
                dve.wait_ge(S("k_decayed"), r + 1)
                tt(k, k, einv[:, r, :], ALU.mult).then_inc(S("decayed"), 1)
            link(dve.memset(attT[:, :, :, :], 0.0))
            for b in range(2):
                dve.wait_ge(S("gla_scored"), b + 1)
                for k in range(2):
                    for r in range(RB):
                        ins = dve.copy_predicated(attT[:, 2 * b + k, r, :], tri.bitcast(U32),
                                                  PB[4 + b][:, SEQ * k + P * r:SEQ * k + P * r + P])
                ins.then_inc(S("att_masked"), 1)
            for m in range(3 * GH):
                h, n = m // 3, m % 3
                dve.wait_ge(S("state_add"), 6 * (h // 2) + 6)
                bank, half = (6 + h // 2, h % 2) if n == 1 else (h, n // 2)
                src = PB[bank][:, GV * half:GV * half + GV]
                if n == 0:
                    dve.tensor_copy(states[:, h, 0, :], src).then_inc(S("stated"), 1)
                else:
                    dve.wait_ge(S("stated"), m)
                    dve.scalar_tensor_tensor(states[:, h, n, :], states[:, h, n - 1, :], decay[:, h, n:n + 1], src,
                                             ALU.mult, ALU.add).then_inc(S("stated"), 1)
            dve.wait_ge(S("gla_root"), 1)
            link(dve.reciprocal(gst[:, 2, :, :], gst[:, 1, :, :]))
            dve.wait_ge(S("r_gated"), RB)
            for h in range(GH):
                for r in range(RB):
                    v, g = Z_VG + GV * h, Z_RG + GV * h
                    link(dve.scalar_tensor_tensor(Z[:, r, v:v + GV], PB[h][:, GV * r:GV * r + GV], gst[:, 2, h, r:r + 1],
                                                  ggla[:, :], ALU.mult, ALU.mult))
                    tt(Z[:, r, v:v + GV], Z[:, r, v:v + GV], Z[:, r, g:g + GV], ALU.mult).then_inc(S("gla_done"), 1)
            norm_inv("cq")
            norm_inv("ckv")
            turn_lo("cq", XTh, XTl, gain=vT[:, V_GQ:V_GQ + 4])
            turn_lo("ckv", XTh, XTl, gain=vT[:, V_GKV:V_GKV + 2], k0=4)
            for k in range(16):
                ada(k)
            lo()
            lo()
            mod_fin(4)
            dve.wait_ge(S("mod_ready"), 5)
            lo()
            lo()
            dve.wait_ge(S("sines"), 2 * RB)
            dve.wait_ge(chunk_out, RB * CHUNK0["uv"])
            for r in range(RB):
                kr = Z[:, r, Z_KR:Z_QG].rearrange("p (h d) -> p h d", h=1)
                for x, n in ((qrow[r][:, :, NOPE:QKD], MH), (kr, 1)):
                    cos = cs[:, r, 0:1, :].broadcast_to([P, n, HALF])
                    sin = cs[:, r, 1:2, :].broadcast_to([P, n, HALF])
                    x1, x2 = x[:, :, 0:HALF], x[:, :, HALF:ROPE]
                    t = [rt[k][:, 0:n, :] for k in range(4)]
                    tt(t[0], x1, cos, ALU.mult)
                    tt(t[1], x2, sin, ALU.mult)
                    tt(t[2], x2, cos, ALU.mult)
                    link(tt(t[3], x1, sin, ALU.mult))
                    tt(x1, t[0], t[1], ALU.subtract).then_inc(S("roped_half"), 1)
                    tt(x2, t[2], t[3], ALU.add).then_inc(S("roped"), 1)
                    dve.wait_ge(S("roped"), 2 * r + (n == 1) + 1)
            lo()
            for t in range(MH + 3):
                h = t - 1
                if 0 <= h < MH:
                    dve.wait_ge(S("scored"), h + 1)
                    if h >= 2:
                        dve.wait_ge(S("p_turned"), h - 1)
                    tt(prob[:, h % 2, :], PB[6 + h % 2][:, 0:3 * P], mask3, ALU.add).then_inc(S("masked"), 1)
                    dve.wait_ge(S("masked"), h + 1)
                    for r in range(RB):
                        dve.tensor_reduce(mst[:, h % 4, 0, r:r + 1], prob[:, h % 2, P * r:P * (2 * r + 1)], AX.X, ALU.max,
                                          negate=True).then_inc(S("maxed"), 1)
                h = t - 3
                if 0 <= h < MH:
                    dve.wait_ge(S("pv_done"), h + 1)
                    link(dve.reciprocal(mst[:, h % 4, 2, :], mst[:, h % 4, 1, :]))
                    for r in range(RB):
                        dve.tensor_scalar(Z[:, r, Z_QG + VD * h:Z_QG + VD * h + VD], PB[h % 2][:, P * r:P * r + VD],
                                          mst[:, h % 4, 2, r:r + 1], None, ALU.mult).then_inc(S("mla_o"), 1)
            turn_lo("o", XTh, XTl)
            for c in range(4):
                for s in range(4):
                    ada(4 * c + s)
                    lo()
            mod_fin(5)
            add_normed("o")

            def ffn(k, pre, gain, shift, more):
                norm_inv(pre)
                turn_lo(pre, XTh, XTl, gain=gain, shift=shift)
                for n in range(4):
                    for r in range(RB):
                        dve.memset(ROWB[:, r, 512 * n:512 * n + 512], 0.0).then_inc(S("y_added"), 1)
                b0 = RB * FN * k
                y0 = 8 * (FN + 1) * k

                def hidden(j):
                    for r in range(RB):
                        dve.wait_ge(S("silu_out"), j * RB + (b0 + r + 1))
                        if not isinstance(j, int) or j or k:
                            dve.wait_ge(S("h_turned"), j * 2 + b0)
                        tt(HROW[:, r, :], SIL[:, r, :], PB[2 + r][:, :], ALU.mult).then_inc(S("h_made"), 1)

                def hidden_lo(j):
                    for b in range(2):
                        dve.wait_ge(S("hid_hi"), j * 2 + (b0 + b + 1))
                        tt(HTl[:, 2 * b:2 * b + 2, :].rearrange("p t n -> p (t n)"), PB[4 + b][:, :],
                           f32(HTh[:, 2 * b:2 * b + 2, :].rearrange("p t n -> p (t n)")), ALU.subtract)\
                            .then_inc(S("hid_lo"), 1)

                def add(n, j, used):
                    dve.wait_ge(slab_used, used)
                    dve.wait_ge(S("y_added"), j * 8 + (y0 + 2 * n + RB))
                    banks = ((6, 7), (0, 1), (6, 7), (2, 3))[n]
                    for r in range(RB):
                        y = ROWB[:, r, 512 * n:512 * n + 512]
                        tt(y, y, PB[banks[r]][:, :], ALU.add).then_inc(S("y_added"), 1)

                for _ in range(7):
                    lo()
                dve.wait_ge(slab_used, st.lins())
                hidden(0)
                lo()
                hidden_lo(0)
                with dve.Fori(0, FN - 1) as i, st.loop(i, FN - 1, 12, 12):
                    for _ in range(8):
                        lo()
                    dve.wait_ge(slab_used, st.lins(-1))
                    hidden(i + 1)
                    lo()
                    lo()
                    add(0, i, st.lins(-2))
                    lo()
                    add(1, i, st.lins(-2))
                    lo()
                    add(2, i, st.lins(-2))
                    add(3, i, st.lins(-1))
                    hidden_lo(i + 1)
                for n in range(4):
                    if n < 3 or more:
                        lo()
                    last = st.lins(-1) if n < 3 or more else st.lins()
                    add(n, FN - 1, last)
                if k:
                    dve.wait_ge(S("gain_in"), 48)
                add_normed(("y1", "y2")[k])

            ffn(0, "f1", modA[:, 3, :], modA[:, 2, :], True)
            norm_inv("z2")
            turn_lo("z2", XTh, XTl, gain=vT[:, V_LN_MIX:V_LN_MIX + KT])
            with dve.Fori(0, Z2N // 2) as i, st.loop(i, Z2N // 2, 8, 8):
                for c in range(2):
                    for s in range(3):
                        lo(4 * Z2C)
                    lo()
            for k in range(2):
                dve.wait_ge(S("pe_turned"), k + 1)
                if k == 0:
                    dve.tensor_copy(peT[:, :, :].rearrange("p k l -> p (k l)"), PB[6][0:HD, 0:2 * CL]).then_inc(S("pe_out"), 1)
                else:
                    dve.tensor_copy(rbT[:, :], PB[7][0:BUCKETS, 0:NH]).then_inc(S("pe_out"), 1)
            dve.memset(relrow[:, SEQ:384], NEG).then_inc(S("pe_out"), 1)
            dve.wait_ge(S("raw_out"), 4)
            dve.wait_ge(S("pe_out"), 2)
            for k in range(2):
                for l in range(CL):
                    m = CL * k + l
                    if m >= 2:
                        dve.wait_ge(S("blk_used"), m - 1)
                    dve.tensor_scalar(blkT[:, l % 2, :, :], rawT[:, k, :, l:l + CS * (NCMP - 1) + 1:CS],
                                      peT[:, k, l:l + 1], None, ALU.add).then_inc(S("blk_made"), 1)
            dve.wait_ge(S("rel_made"), 1)
            dve.tensor_copy(relrow[:, 0:SEQ], PB[7][0:NH, 0:SEQ]).then_inc(S("rel_row"), 1)
            dve.wait_ge(S("gates_out"), RB)
            dve.wait_ge(S("rel_done"), 8)
            for t in range(NH * RB + 3):
                u = t - 2
                if 0 <= u < NH * RB:
                    b, n_c = u % 2, (NCMP0, NCMP)[u % 2]
                    dve.wait_ge(S("n_turned"), u + 1)
                    if u >= 2:
                        dve.wait_ge(S("n_pv"), u - 1)
                    dve.tensor_copy(pcT[0:n_c, b, :], PB[2 + b][0:n_c, P:2 * P]).then_inc(S("n_cT"), 1)
                u = t
                if u < NH * RB:
                    h, r = u // 2, u % 2
                    nk, n_c = P * (r + 1), (NCMP0, NCMP)[r]
                    dve.wait_ge(S("n_scored"), u + 1)
                    if u >= 2:
                        dve.wait_ge(S("n_turned"), u - 1)
                    b = u % 2
                    off = P if r == 0 else 0
                    s3 = NSPROB(b)[:, 0:2 * nk].rearrange("p (c n) -> p c n", c=2)
                    for c in range(2):
                        tt(s3[:, c, :], PB[b][:, nk * c:nk * c + nk], REL[:, h, off:off + nk], ALU.add)
                    c0 = (P - 1 + CL if r == 0 else CL - 1)
                    tt(pc[:, b, 0:n_c], PB[2 + b][:, 0:n_c], REL[:, h, c0:c0 + CS * (n_c - 1) + 1:CS], ALU.add)\
                        .then_inc(S("n_added"), 1)
                    dve.wait_ge(S("n_added"), u + 1)
                    dve.tensor_reduce(nst[:, u % 4, 2, 0:2], s3, AX.X, ALU.max)
                    link(dve.tensor_reduce(nst[:, u % 4, 2, 2:3], pc[:, b, 0:n_c], AX.X, ALU.max))
                    dve.tensor_scalar(nst[:, u % 4, 0, :], nst[:, u % 4, 2, :], -1e29, -1.0, ALU.max, ALU.mult)\
                        .then_inc(S("n_maxed"), 1)
                u = t - 3
                if 0 <= u < NH * RB:
                    h, r, b = u // 2, u % 2, u % 2
                    link(dve.tensor_scalar(nst[:, u % 4, 1, :], nst[:, u % 4, 1, :], 1.0, None, ALU.max))
                    link(dve.reciprocal(nst[:, u % 4, 1, :], nst[:, u % 4, 1, :]))
                    gl = Z2[:, r, Z2_GL + 3 * h:Z2_GL + 3 * h + 3]
                    wt = nwt[:, u % 4, :]
                    link(tt(wt, nst[:, u % 4, 1, :], gl, ALU.mult))
                    dve.wait_ge(S("n_pv"), u + 1)
                    o = Z2[:, r, HD * h:HD * h + HD]
                    po = PB[6 + b]
                    for c, q in enumerate((1, 2, 0)):
                        src = po[:, HD * c:HD * c + HD]
                        if c == 0:
                            ins = dve.tensor_scalar(o, src, nwt[:, u % 4, q:q + 1], None, ALU.mult)
                        else:
                            ins = dve.scalar_tensor_tensor(o, src, nwt[:, u % 4, q:q + 1], o, ALU.mult, ALU.add)
                        ins.then_inc(S("nsa_o"), 1)
                        if c < 2:
                            dve.wait_ge(S("nsa_o"), 3 * u + c + 1)
            for g in range(PG):
                dve.wait_ge(S("pool_hi"), g + 1)
                sl = (slice(None), slice(2 * g, 2 * g + 2), slice(None))
                tt(XTl[sl].rearrange("p t n -> p (t n)"), PB[g][:, :], f32(XTh[sl].rearrange("p t n -> p (t n)")),
                   ALU.subtract).then_inc(S("pool_lo"), 1)
            lo()
            for g in range(PG):
                dve.wait_ge(S("pool_lin"), g + 1) if g < PG - 1 else dve.wait_ge(slab_used, st.lins(-1))
                for q in range(2):
                    k = V_PS + 2 * g + q
                    ins = dve.tensor_scalar(TMPP[:, g % 2, SEQ * q:SEQ * q + SEQ], PB[4 + g][:, SEQ * q:SEQ * q + SEQ],
                                            vT[:, k:k + 1], None, ALU.mult)
                ins.then_inc(S("pool_scaled"), 1)
                dve.wait_ge(S("pool_hi"), PG + g + 1)
                sl = (slice(None), slice(8 + 2 * g, 10 + 2 * g), slice(None))
                tt(XTl[sl].rearrange("p t n -> p (t n)"), TMPP[:, g % 2, :], f32(XTh[sl].rearrange("p t n -> p (t n)")),
                   ALU.subtract).then_inc(S("pool_lo"), 1)
            turn_lo("att", XTh, XTl)
            dve.wait_ge(S("merge_gated"), RB)
            for c in range(4):
                for s in range(4):
                    lo()
                dve.wait_ge(slab_used, st.lins(-1))
                cols = slice(512 * c, 512 * c + 512)
                for r in range(RB):
                    ga, gp = (Z2[:, r, Z2_M + D * k + 512 * c:Z2_M + D * k + 512 * c + 512] for k in range(2))
                    tt(ga, ga, PB[r][:, :], ALU.mult).then_inc(S("merged"), 1)
                    tt(gp, gp, PB[2 + r][:, :], ALU.mult).then_inc(S("merged"), 1)
                    dve.wait_ge(S("merged"), 6 * c + 3 * r + 2)
                    tt(Z2[:, r, cols], ga, gp, ALU.add).then_inc(S("merged"), 1)
            turn_lo("y", XTh, XTl)
            for c in range(16):
                lo()
            dve.wait_ge(S("gain_in"), 16)
            add_normed("mix")
            norm_inv("xq")
            turn_lo("xq", XTh, XTl, gain=vT[:, V_LN_X:V_LN_X + KT])
            for _ in range(4):
                lo()
            for t in range(XH + 2):
                h = t
                if h < XH:
                    dve.wait_ge(S("x_scored"), h + 1)
                    if h >= 2:
                        dve.wait_ge(S("x_exped"), RB * (h - 1))
                    dve.tensor_reduce(mst[:, h % 4, 0, :], PB[h % 2][:, :].rearrange("p (r n) -> p r n", r=RB), AX.X, ALU.max,
                                      negate=True).then_inc(S("x_maxed"), 1)
                h = t - 2
                if 0 <= h < XH:
                    dve.wait_ge(S("x_pv"), h + 1)
                    link(dve.reciprocal(mst[:, h % 4, 2, :], mst[:, h % 4, 1, :]))
                    for r in range(RB):
                        dve.tensor_scalar(SIL[:, r, XD * h:XD * h + XD], PB[2 + h % 2][:, P * r:P * r + XD],
                                          mst[:, h % 4, 2, r:r + 1], None, ALU.mult).then_inc(S("xatt_o"), 1)
            turn_lo("xo", XTh, XTl, k0=12)
            for c in range(4):
                lo()
            dve.wait_ge(S("gain_in"), 32)
            add_normed("xo")
            ffn(1, "f2", vT[:, V_LN_FFN:V_LN_FFN + KT], None, False)


def kernel(**inputs):
    import concourse.bacc as bacc
    from concourse.bass_utils import run_bass_kernel_spmd

    nc = bacc.Bacc("TRN2", target_bir_lowering=False, num_devices=1, dynamic_dma_scratch_size=4096)
    const, band, onehot = shape_constants()
    host = {name: np.ascontiguousarray(a) for name, a in inputs.items()}
    drop = ("w_ada", "b_ada", "g_pre_mix", "g_post_mix", "w_in", "g_q", "w_uq", "g_kv", "w_uk", "w_uv", "w_gate_up", "b_gate",
            "g_gla", "w_out", "g_pre_ffn", "g_post_ffn", "w_ffn_gate", "w_ffn_up", "w_ffn_down", "x", "c", "positions")
    for name, a in host.items():
        if name in drop or (name.endswith("_2") and name != "rel_bias_2"):
            host[name] = a[0]
    host.update(const=const, band=band, onehot=onehot)
    A = {name: nc.dram_tensor(f"in_{name}", a.shape, mybir.dt.from_np(a.dtype), kind="ExternalInput").ap()
         for name, a in host.items()}
    out = nc.dram_tensor("out_x", (SEQ, D), F32, kind="ExternalOutput").ap()
    build(nc, A, out)
    r = run_bass_kernel_spmd(nc, [{f"in_{name}": a for name, a in host.items()}], core_ids=[0])
    return r.results[0]["out_x"].reshape(1, SEQ, D)
```

```python
from contextlib import ExitStack, contextmanager

import numpy as np

import concourse.bass as bass
from concourse import mybir

F32 = mybir.dt.float32
F32R = mybir.dt.float32r
I32 = mybir.dt.int32
U32 = mybir.dt.uint32
ACT = mybir.ActivationFunctionType
ALU = mybir.AluOpType
AX = mybir.AxisListType

P = 128
SEQ, D, RB = 256, 2048, 2
KT = D // P
EPS = 1e-6
NEG = -1e30
MH, QR, KVR, NOPE, ROPE, VD = 8, 512, 256, 128, 64, 128
QKD = NOPE + ROPE
HALF = ROPE // 2
GH, GK, GV, CH = 4, 128, 256, 64
GKEY, GVAL, GR = GH * GK, GH * GV, 16
NCH = SEQ // CH
Z_CQ, Z_CKV, Z_KR = 0, QR, QR + KVR
Z_QG = Z_KR + ROPE
Z_KG = Z_QG + GKEY
Z_VG = Z_KG + GKEY
Z_AG = Z_VG + GVAL
Z_RG = Z_AG + GR
ZW = Z_RG + GVAL
ZC, ZN = ZW // 8, 8
NH, NG, HD = 16, 4, 64
HPG = NH // NG
KVW = NG * HD
CL, CS, CHID = 32, 16, 128
NCMP = (SEQ - CL) // CS + 1
NCMP0 = (P - CL) // CS + 1
POOLW = (2, 4, 8, 16)
PG, PGW = 4, 256
Z2_KV = NH * HD
Z2_GL = Z2_KV + 6 * KVW
Z2_U = Z2_GL + 3 * NH
Z2_M = Z2_U + PG * PGW
Z2W = Z2_M + 2 * D
Z2N = 8
Z2_PARTS = [(0, Z2_M // Z2N), (Z2_M, 2 * D // Z2N)]
XH, XD = 4, 128
DFF = 5632
FN = DFF // 512
BUCKETS, MAXD = 32, 2048
REL_W = SEQ + P
TWO_PI_PARTS = (6.28125, 0.0019350051879882812, 3.019916050561733e-07)
MAGIC = 12582912.0

C_ID, C_TRI, C_BLK, C_ONE, C_FLIP, C_MASK, C_INVF = 0, 128, 256, 384, 512, 640, 1024
CONST_W = C_INVF + HALF


def shape_constants():
    i = np.arange(P)
    c = np.zeros((P, CONST_W), np.float32)
    c[:, C_ID:C_ID + P] = np.eye(P)
    same = (i[:, None] // CH) == (i[None, :] // CH)
    c[:, C_TRI:C_TRI + P] = same & (i[:, None] <= i[None, :])
    c[:, C_BLK:C_BLK + P] = same
    c[:, C_ONE:C_ONE + P] = 1.0
    c[:, C_FLIP:C_FLIP + P] = np.eye(P)[::-1]
    causal = np.where(i[None, :] <= i[:, None], 0.0, NEG)
    c[:, C_MASK:C_MASK + P] = causal
    c[:, C_MASK + 2 * P:C_MASK + 3 * P] = causal
    c[:, C_INVF:] = (1.0 / (np.float32(10000.0) ** (np.arange(0, ROPE, 2, dtype=np.float32) / np.float32(ROPE))))
    t = np.arange(SEQ)
    band = np.zeros((P, PG, 3 * P), np.float32)
    for g, w in enumerate(POOLW):
        m = ((t[:, None] - t[None, :] >= 0) & (t[:, None] - t[None, :] < w)) / np.minimum(t + 1, w)[:, None]
        m = (m - np.eye(SEQ)).T
        band[:, g, :SEQ] = m[:P]
        band[:, g, SEQ:] = m[P:, P:]
    n = np.maximum(SEQ - 1 - np.arange(SEQ), 0)
    exact = BUCKETS // 2
    big = exact + (np.log(np.maximum(n, 1) / exact) / np.log(MAXD / exact) * (BUCKETS - exact)).astype(np.int64)
    bucket = np.where(n < exact, n, np.minimum(big, BUCKETS - 1))
    onehot = (np.arange(BUCKETS)[:, None] == bucket[None, :]).astype(np.float32)
    return c, band.reshape(P, PG * 3 * P), onehot


class Slabs:

    def __init__(self):
        self.raw = self.lin = 0
        self.i = None
        self.praw = self.plin = 0

    @contextmanager
    def loop(self, i, count, praw, plin):
        assert praw % 4 == 0 and plin % 2 == 0
        r, n = self.raw, self.lin
        self.i, self.praw, self.plin = i, praw, plin
        yield
        assert self.raw == r + praw and self.lin == n + plin, (self.raw - r, self.lin - n)
        self.i = None
        self.raw += praw * (count - 1)
        self.lin += plin * (count - 1)

    def plus(self, value, per):
        return value if self.i is None else self.i * per + value

    def raws(self, ahead=0):
        return self.plus(self.raw + ahead, self.praw)

    def lins(self, ahead=0):
        return self.plus(self.lin + ahead, self.plin)

    def landed(self):
        return self.plus(16 * (self.raw // 4 + 1), 4 * self.praw)

    def next(self, linear=True):
        self.raw += 1
        self.lin += linear


class Chain:

    def __init__(self, eng, sem):
        self.eng, self.sem, self.n = eng, sem, 0

    def __call__(self, ins):
        self.n += 1
        ins.then_inc(self.sem, 1)
        self.eng.wait_ge(self.sem, self.n)


TURNS = [("mem", 8, 2), ("x", 8, 1), ("cq", 2, 2), ("ckv", 1, 2), ("o", 8, 0), ("f1", 8, 1), ("z2", 8, 2),
         ("att", 4, 0), ("y", 8, 0), ("xq", 8, 2), ("xo", 2, 0), ("f2", 8, 2)]
TURN_N = {name: n for name, n, _ in TURNS}
TURN0 = {name: sum(m[1] for m in TURNS[:k]) for k, (name, _, _) in enumerate(TURNS)}
GAIN0 = {name: sum(m[1] for m in TURNS[:k] if m[2] == 1) for k, (name, _, _) in enumerate(TURNS)}
HI0 = {name: sum(m[1] * (2 if m[2] == 2 else 1) for m in TURNS[:k]) for k, (name, _, _) in enumerate(TURNS)}
GAINED = {name for name, _, kind in TURNS if kind == 1}
NORMS = ["mem", "x", "cq", "ckv", "o", "f1", "y1", "z2", "mix", "xq", "xo", "f2", "y2"]
ROWED = ["mem", "x", "cq", "ckv", "f1", "z2", "xq", "f2"]
POST = ["o", "y1", "mix", "xo", "y2"]
CHUNKS = [("xkv", 2), ("zin", ZN), ("uq", 3), ("uv", 2), ("wout", 4), ("zin2", 2 * Z2N), ("mix", 4), ("xq", 1), ("xo", 4)]
CHUNK0 = {name: sum(n for _, n in CHUNKS[:k]) for k, (name, _) in enumerate(CHUNKS)}


def build(nc, A, out):
    ctx = ExitStack()
    with ctx:
        named = {}

        def S(name):
            if name not in named:
                named[name] = ctx.enter_context(nc.semaphore(name))
            return named[name]

        base = [-(-nc.sbuf_base // 64) * 64]

        def sb(name, shape, dt=F32):
            t = nc.alloc_sbuf_tensor_at(name, shape, dt, offset=base[0])
            base[0] += -(-4 * int(np.prod(shape[1:])) // 32) * 32
            return t

        def at(name, shape, offset, dt=F32):
            return nc.alloc_sbuf_tensor_at(name, shape, dt, offset=offset)

        raw = sb("raw", [P, 4, 2048])
        wh = sb("wh", [P, 2, 2048], F32R)
        wl = sb("wl", [P, 2, 2048], F32R)
        X = sb("X", [P, RB, D])
        xt0 = base[0]
        XTh = sb("XTh", [P, KT, SEQ], F32R)
        xt1 = base[0]
        XTl = sb("XTl", [P, KT, SEQ], F32R)
        xkT = sb("xkT", [P, XH, SEQ])
        xv = sb("xv", [P, RB, XH * XD])
        zb = base[0]
        ZB = sb("ZB", [P, RB * Z2W])
        misc = base[0]
        MISC = sb("MISC", [P, 5120])
        CON = sb("CON", [P, CONST_W])
        vT = sb("vT", [P, P])
        bT = sb("bT", [P, P])
        modA = sb("modA", [P, 4, KT])
        gT = sb("gT", [P, KT])
        cT = sb("cT", [P, KT])
        nstat = sb("nstat", [P, len(NORMS), 3, RB])
        psq = sb("psq", [P, len(POST), RB, 4])
        eps = sb("eps", [P, 1])
        one = sb("one", [P, 1])
        mtmp = sb("mtmp", [P, KT])
        msum = sb("msum", [P, 2 * KT])
        nwt = sb("nwt", [P, 4, 3])
        ang = sb("ang", [P, RB, 2, HALF])
        cs = sb("cs", [P, RB, 2, HALF])
        posi = sb("posi", [P, RB], I32)
        posf = sb("posf", [P, RB])
        assert base[0] <= nc.sbuf_usable_end, (base[0], nc.sbuf_usable_end)

        Z = at("Z", [P, RB, ZW], zb)
        Z2 = at("Z2", [P, RB, Z2W], zb)
        ROWB = at("ROWB", [P, RB, D], zb)
        MEM = at("MEM", [P, RB, D], zb + 4 * 4096)
        HROW = at("HROW", [P, RB, 512], zb + 4 * 4096)
        SIL = at("SIL", [P, RB, 512], zb + 4 * 5120)
        JUNK = at("JUNK", [P, D], zb + 4 * 8192)
        TMP = at("TMP", [P, 2, 512], zb + 4 * 10240)
        HTh = at("HTh", [P, 4, SEQ], zb + 4 * 11264, F32R)
        HTl = at("HTl", [P, 4, SEQ], zb + 4 * 12288, F32R)
        ACC = at("ACC", [P, D], zb + 4 * 13408)
        wgu = at("wgu", [GR, GKEY], zb + 4 * 11264)
        bgr = at("bgr", [1, GKEY], zb + 4 * 11776)
        aT = at("aT", [GR, SEQ], zb + 4 * 12288)
        VROW = at("VROW", [P, P], zb + 4 * 12928)
        BROW = at("BROW", [P, P], zb + 4 * 13056)
        G = at("G", [P, D], misc)
        assert xt1 - xt0 == 4 * 4096 and zb + 4 * 15360 <= misc

        PB = [ctx.enter_context(nc.psum_tensor(f"bank{b}", [P, 512], F32)) for b in range(8)]

        ident = CON[:, C_ID:C_ID + P]
        tri = CON[:, C_TRI:C_TRI + P]
        blk = CON[:, C_BLK:C_BLK + P]
        ones = CON[:, C_ONE:C_ONE + P]
        flip = CON[:, C_FLIP:C_FLIP + P]
        mask3 = CON[:, C_MASK:C_MASK + 3 * P]
        invf = CON[:, C_INVF:C_INVF + HALF]
        V_PRE_MIX, V_PRE_FFN, V_LN_MIX, V_LN_X, V_LN_MEM, V_LN_FFN, V_C, V_GQ, V_GKV, V_PS = (
            0, 16, 32, 48, 64, 80, 96, 112, 116, 118)

        def f32(ap):
            return ap.bitcast(F32)

        def scr(name, off, shape):
            return at(name, shape, xt0 + 4 * off)

        la = scr("la", 0, [P, RB, GKEY])
        eb = scr("eb", 1024, [P, RB, GKEY])
        einv = scr("einv", 2048, [P, RB, GKEY])
        kd = scr("kd", 3072, [P, RB, GKEY])
        bcs = scr("bcs", 4096, [P, RB, GKEY])
        qdT = scr("qdT", 5120, [P, GH, SEQ])
        kiT = scr("kiT", 6144, [P, GH, SEQ])
        attT = scr("attT", 7168, [P, GH, RB, P])
        states = at("states", [P, GH, 3, GV], misc + 4 * 2048)
        decay = sb("decay", [P, GH, NCH])
        ggla = at("ggla", [P, GV], zb + 4 * 12544)
        gst = sb("gst", [P, 3, GH, RB])
        qrow = [at(f"qrow{r}", [P, MH, QKD], (xt0, xt1)[r] + 4 * 1536) for r in range(RB)]
        kTn = [at(f"kTn{r}", [P, 4, SEQ], (xt0, xt1)[r] + 4 * 3072) for r in range(2)]
        vrow = at("vrow", [P, RB, MH * VD], misc + 4 * 2048)
        qTs = at("qTs", [P, 2, 512], misc + 4 * 4096)
        krT = at("krT", [ROPE, SEQ], zb + 4 * 11264)
        prob = at("prob", [P, 2, 384], zb + 4 * 11520)
        probT = at("probT", [P, 2, 384], zb + 4 * 12288)
        rt = [at(f"rt{k}", [P, MH, HALF], zb + 4 * (8192 + 256 * k)) for k in range(4)]
        ropes = at("ropes", [P, 3, HALF], zb + 4 * 12800)
        mst = sb("mst", [P, 4, 3, RB])
        QT = at("QT", [HD, NH, SEQ], xt0)
        KT2 = at("KT2", [HD, NG, 2, SEQ], xt0 + 4 * 4096)
        rawT = at("rawT", [2 * HD, 2, NG, SEQ], xt0 + 4 * 6144)
        REL = at("REL", [P, NH, SEQ], misc)
        pT = at("pT", [P, 2, 512], misc + 4 * 4096)
        w1s = at("w1s", [2 * HD, 2, CS, CHID], xt0)
        w2s = at("w2s", [CHID, 2, HD], misc + 4 * 4096)
        peT = at("peT", [2 * HD, 2, CS], misc + 4 * 4224)
        perow = at("perow", [2 * CS, 2 * HD], misc + 4 * 4288)
        hidT = at("hidT", [CHID, 2, NG * NCMP], misc + 4 * 4480)
        onehot = at("onehot", [BUCKETS, SEQ], zb + 4 * 11264)
        rb16 = at("rb16", [NH, BUCKETS], zb + 4 * 11520)
        rbT = at("rbT", [BUCKETS, NH], zb + 4 * 11552)
        relrow = sb("relrow", [NH, REL_W])
        kcT = sb("kcT", [HD, NG, NCMP])
        vc = sb("vc", [NCMP, NG, HD])
        pcT = sb("pcT", [NCMP, 2, P])
        pc = sb("pc", [P, 2, 16])
        nst = sb("nst", [P, 4, 3, 3])
        band = at("band", [P, PG, 3 * P], misc)
        assert base[0] <= nc.sbuf_usable_end, (base[0], nc.sbuf_usable_end)
        NSPROB = lambda k: Z2[:, k, Z2_KV:Z2_KV + 512]
        xqT = at("xqT", [P, XH, SEQ], xt0)
        TMPP = at("TMPP", [P, 2, 512], misc + 4 * 1536)
        xp = at("xp", [P, 2, 512], xt0 + 4 * 1024)
        xpT = at("xpT", [P, 2, 512], xt0 + 4 * 2048)

        rel_d = nc.dram_tensor("rel_scratch", [NH, P, REL_W], F32, kind="Internal").ap()

        def kview(w, rows):
            return w.rearrange("(t p) n -> p t n", p=P)

        W = {k: kview(A[k], None) for k in (
            "w_ada", "w_in", "w_uq", "w_uk", "w_uv", "w_out", "w_ffn_gate", "w_ffn_up", "w_ffn_down", "w_in_2",
            "w_br_attn_2", "w_br_pool_2", "w_mix_out_2", "w_xq_2", "w_xkv_2", "w_xo_2", "w_gate_2", "w_up_2",
            "w_down_2")}
        wpool = A["w_pool_2"].rearrange("g (t p) n -> p g t n", p=P)

        block = ctx.enter_context(nc.Block())
        slab_done, hi_made, slab_used, chunk_out = S("slab_done"), S("hi_made"), S("slab_used"), S("chunk_out")
        landed = [S(f"slab_landed{k}") for k in range(4)]

        @block.sync
        def _(sp):
            st = Slabs()

            def slab(src, parts, linear=True):
                r = st.raw
                if r >= 4:
                    sp.wait_ge(slab_done, st.raws(-3))
                n = int(np.prod(parts))
                dst = raw[:, r % 4, 0:n]
                if len(parts) == 2:
                    dst = dst.rearrange("p (t n) -> p t n", t=parts[0])
                if len(parts) == 3:
                    dst = dst.rearrange("p (g t n) -> p g t n", g=parts[0], t=parts[1])
                sp.dma_start(dst, src).then_inc(landed[r % 4], 16)
                st.next(linear)

            def ada(v, k):
                slab(W["w_ada"][:, k, v * D:(v + 1) * D], (D,), False)

            def cols(w, s, c0, width):
                slab(W[w][:, 4 * s:4 * s + 4, c0:c0 + width], (4, width))

            def load(name, dst, src, **how):
                sp.dma_start(dst, src, **how).then_inc(S(name), 16)

            load("mem_in", MEM[:, :, :], A["mem_2"].rearrange("(r p) n -> p r n", p=P))
            load("con_in", CON[:, :], A["const"])
            at_row = 0
            for name, n in (("g_pre_mix", 16), ("g_pre_ffn", 16), ("ln_mix_pre_2", 16), ("ln_x_pre_2", 16),
                            ("ln_mem_2", 16), ("ln_ffn_pre_2", 16), ("c", 16), ("g_q", 4), ("g_kv", 2),
                            ("pool_scale_2", 8)):
                load("vec_in", VROW[at_row:at_row + n, :], A[name].rearrange("(t p) -> t p", p=P))
                at_row += n
            load("vec_in", BROW[0:96, :], A["b_ada"].rearrange("(t p) -> t p", p=P))
            load("vec_in", BROW[96:112, :], A["g_post_mix"].rearrange("(t p) -> t p", p=P))
            load("vec_in", BROW[112:128, :], A["g_post_ffn"].rearrange("(t p) -> t p", p=P))
            load("pos_in", posi[:, :], A["positions"].rearrange("(r p) -> p r", p=P), allow_slow_non_contiguous=True)
            load("rel_bias_in", rb16[:, :], A["rel_bias_2"])
            load("rel_bias_in", onehot[:, :], A["onehot"])
            load("x_in", X[:, :, :], A["x"].rearrange("(r p) n -> p r n", p=P))
            for k in range(KT):
                ada(0, k)
            for s in range(4):
                cols("w_xkv_2", s, 0, 512)
            for s in range(4):
                cols("w_xkv_2", s, 512, 512)
                ada(1, 2 * s)
                ada(1, 2 * s + 1)
            for k in range(8, KT):
                ada(1, k)
            with sp.Fori(0, 2) as i, st.loop(i, 2, 32, 16):
                for c in range(4):
                    for s in range(4):
                        slab(W["w_in"][:, 4 * s:4 * s + 4, bass.ds(i * (4 * ZC) + c * ZC, ZC)], (4, ZC))
                        slab(W["w_ada"][:, 4 * c + s, bass.ds(i * D + 2 * D, D)], (D,), False)
            cols("w_uq", 0, 0, 512)
            load("gla_in", wgu[:, :], A["w_gate_up"])
            load("gla_in", bgr[:, :], A["b_gate"].rearrange("(a n) -> a n", a=1))
            load("gla_in", ggla[:, :], A["g_gla"].partition_broadcast(P))
            sp.wait_ge(S("rel_row"), 2)
            load("rel_out", rel_d, relrow[:, :].unsqueeze(1).broadcast_to([NH, P, REL_W]))
            for c in (1, 2):
                cols("w_uq", 0, 512 * c, 512)
            slab(W["w_uk"], (2, 1024))
            slab(W["w_uv"], (2, 1024))
            for k in range(KT):
                ada(4, k)
            for c in range(4):
                for s in range(4):
                    cols("w_out", s, 512 * c, 512)
                    ada(5, 4 * c + s)

            def ffn(gate, up, down):
                def part(w, j):
                    for s in range(4):
                        src = bass.ds(j * 512, 512) if st.i is not None else slice(j * 512, j * 512 + 512)
                        slab(W[w][:, 4 * s:4 * s + 4, src], (4, 512))

                def part_down(j):
                    for n in range(4):
                        src = bass.ds(j * 4, 4) if st.i is not None else slice(j * 4, j * 4 + 4)
                        slab(W[down][:, src, 512 * n:512 * n + 512], (4, 512))

                part(gate, 0)
                part(up, 0)
                with sp.Fori(0, FN - 1) as i, st.loop(i, FN - 1, 12, 12):
                    part(gate, i + 1)
                    part(up, i + 1)
                    part_down(i)
                part_down(FN - 1)

            ffn("w_ffn_gate", "w_ffn_up", "w_ffn_down")
            for c0, width in Z2_PARTS:
                with sp.Fori(0, Z2N // 2) as i, st.loop(i, Z2N // 2, 8, 8):
                    for c in range(2):
                        for s in range(4):
                            slab(W["w_in_2"][:, 4 * s:4 * s + 4, bass.ds(i * (2 * width) + (c0 + c * width), width)], (4, width))
            slab(wpool, (4, 2, 256))
            sp.wait_ge(S("x_added"), 4)
            sp.wait_ge(S("rel_out"), 16)
            load("rel_in", REL[:, :, :], bass.AP(rel_d.tensor, P - 1, [[REL_W - 1, P], [P * REL_W, NH], [1, SEQ]]))
            for k in range(2):
                load("cmp_in", w2s[:, k, :], A["cmp_w2_2"][k])
                load("cmp_in", perow[CS * k:CS * k + CS, :].rearrange("l (h d) -> l h d", h=2),
                     A["cmp_pe_2"][k].rearrange("(h l) d -> l h d", h=2))
            sp.wait_ge(chunk_out, RB * CHUNK0["mix"])
            for k in range(2):
                w1 = A["cmp_w1_2"][k].rearrange("(h l d) n -> h d l n", h=2, d=HD)
                for half in range(2):
                    load(f"w1_in{k}", w1s[HD * half:HD * half + HD, k, :, :], w1[half])
            sp.wait_ge(S("nsa_o"), 3 * NH * RB)
            load("band_in", band[:, :, :], A["band"].rearrange("p (g n) -> p g n", g=PG))
            for c in range(4):
                for w in ("w_br_attn_2", "w_br_pool_2"):
                    for s in range(2):
                        cols(w, s, 512 * c, 512)
            sp.wait_ge(S("pool_lo"), 2 * PG)
            load("gain_in", G[:, :], A["ln_mix_post_2"].partition_broadcast(P))
            for c in range(4):
                for s in range(4):
                    cols("w_mix_out_2", s, 512 * c, 512)
            for s in range(4):
                cols("w_xq_2", s, 0, 512)
            sp.wait_ge(S("x_added"), 6)
            load("gain_in", G[:, :], A["ln_x_post_2"].partition_broadcast(P))
            for c in range(4):
                cols("w_xo_2", 0, 512 * c, 512)
            ffn("w_gate_2", "w_up_2", "w_down_2")
            sp.wait_ge(S("x_added"), 8)
            load("gain_in", G[:, :], A["ln_ffn_post_2"].partition_broadcast(P))
            for r in range(RB):
                sp.wait_ge(S("x_added"), 9 + r)
                load("stored", out.rearrange("(r p) n -> p r n", p=P)[:, r, :], X[:, r, :])
            sp.wait_ge(S("stored"), 16 * RB)
        @block.scalar
        def _(act):
            st = Slabs()

            def f(out_, in_, func, name, **kw):
                act.activation(out_, in_, func, **kw).then_inc(S(name), 1)

            def hi(width=2048):
                act.wait_ge(landed[st.raw % 4], st.landed())
                if st.lin >= 2:
                    act.wait_ge(slab_used, st.lins(-1))
                act.activation(wh[:, st.lin % 2, 0:width], raw[:, st.raw % 4, 0:width], ACT.Copy).then_inc(hi_made, 1)
                st.next()

            def skip(n=1):
                for _ in range(n):
                    st.next(False)

            def norm_stats(name, src, n, ready=None):
                j = NORMS.index(name)
                for r in range(RB):
                    if ready is not None:
                        act.wait_ge(S("x_added"), ready + r + 1)
                    act.wait_ge(S("squared"), RB * j + r) if j + r else None
                    f(JUNK[:, 0:n], src(r), ACT.Square, "squared", accum_out=nstat[:, j, 0, r:r + 1])
                act.wait_ge(S("squared"), RB * j + RB)
                f(nstat[:, j, 1, :], nstat[:, j, 0, :], ACT.Sqrt, "rooted", scale=1.0 / n, bias=eps[:, 0:1])

            def post_square(name, c, ready=None):
                m = 4 * RB * POST.index(name) + RB * c
                for r in range(RB):
                    ready(r)
                    if m + r >= 4:
                        act.wait_ge(S("part_sq"), m + r - 3)
                    f(JUNK[:, 512 * ((m + r) % 4):512 * ((m + r) % 4) + 512], ROWB[:, r, 512 * c:512 * c + 512], ACT.Square,
                      "part_sq", accum_out=psq[:, POST.index(name), r, c:c + 1])

            def post_root(name):
                j = NORMS.index(name)
                act.wait_ge(S("squared"), RB * j + RB)
                f(nstat[:, j, 1, :], nstat[:, j, 0, :], ACT.Sqrt, "rooted", scale=1.0 / D, bias=eps[:, 0:1])

            def norm_rows(name, src, dst, blocks=1):
                j = NORMS.index(name)
                act.wait_ge(S("rooted_inv"), j + 1)
                for r in range(blocks):
                    f(dst(r), src(r), ACT.Copy, "normed", scale=nstat[:, j, 2, r:r + 1])

            def turn_hi(name, dst, k0=0, gain=None):
                for b in range(TURN_N[name]):
                    g = TURN0[name] + b
                    if gain is not None:
                        act.wait_ge(S("turned"), g + 1)
                        for k in range(2):
                            kt = 2 * b + k
                            f(dst[:, k0 + kt, :], PB[4 + g % 2][:, SEQ * k:SEQ * k + SEQ], ACT.Copy, "turn_hi",
                              scale=gain[:, kt:kt + 1])
                        continue
                    if name in GAINED:
                        act.wait_ge(S("gained"), GAIN0[name] + b + 1)
                        src = TMP[:, g % 2, :]
                    else:
                        act.wait_ge(S("turned"), g + 1)
                        src = PB[4 + g % 2][:, :]
                    f(dst[:, k0 + 2 * b:k0 + 2 * b + 2, :].rearrange("p t n -> p (t n)"), src, ACT.Copy, "turn_hi")

            def chunk_evac(c, dst, width, scale=1.0, done=None, it=None):
                act.wait_ge(slab_used, done)
                for r in range(RB):
                    act.activation(dst(r), PB[2 * (c % 2) + r][:, 0:width], ACT.Copy, scale=scale).then_inc(chunk_out, 1)

            act.wait_ge(S("vec_out"), 2)
            f(cT[:, :], vT[:, V_C:V_C + 16], ACT.Silu, "c_gated")
            act.wait_ge(S("mem_in"), 16)
            act.wait_ge(S("zeroed"), 2)
            norm_stats("mem", lambda r: MEM[:, r, :], D)
            norm_rows("mem", lambda r: MEM[:, r, :], lambda r: ROWB[:, r, :])
            turn_hi("mem", XTh, gain=vT[:, V_LN_MEM:V_LN_MEM + KT])
            skip(16)
            for s in range(5):
                hi()
            chunk_evac(0, lambda r: HROW[:, r, :], 512, done=4)
            for b in range(2):
                act.wait_ge(S("xk_turned"), b + 1)
                f(xkT[:, 2 * b:2 * b + 2, :].rearrange("p h n -> p (h n)"), PB[6 + b][:, :], ACT.Copy, "xk_out")
            for s in range(3):
                skip(2)
                hi()
            skip(10)
            act.wait_ge(S("x_in"), 16)
            norm_stats("x", lambda r: X[:, r, :], D)
            act.wait_ge(S("turned"), TURN0["x"])
            norm_rows("x", lambda r: X[:, r, :], lambda r: ROWB[:, r, :])
            chunk_evac(1, lambda r: xv[:, r, :], 512, done=8)
            turn_hi("x", XTh)
            hi()
            with act.Fori(0, 2) as i, st.loop(i, 2, 32, 16):
                for c in range(4):
                    for s in range(3):
                        skip()
                        hi(4 * ZC)
                    skip()
                    hi()
                    act.wait_ge(slab_used, st.lins(-1))
                    for r in range(RB):
                        act.activation(Z[:, r, bass.ds(i * (4 * ZC) + c * ZC, ZC)],
                                       PB[2 * (c % 2) + r][:, 0:ZC], ACT.Copy).then_inc(chunk_out, 1)
            for b in range(4):
                act.wait_ge(S("g_wide"), b + 1)
                f(G[:, 512 * b:512 * b + 512], PB[4 + b % 2][:, :], ACT.Copy, "g_out")
            for r in range(RB):
                act.wait_ge(S("gate_in"), r + 1)
                f(eb[:, r, :], PB[r][:, :], ACT.Abs, "gla_f")
            act.wait_ge(S("gla_f"), 2)
            for r in range(RB):
                f(einv[:, r, :], eb[:, r, :], ACT.Exp, "gla_f", scale=-1.0)
            act.wait_ge(S("gla_f"), 4)
            for r in range(RB):
                f(kd[:, r, :], einv[:, r, :], ACT.Ln, "log1p", bias=one[:, 0:1])
            for r in range(RB):
                act.wait_ge(S("cum"), r + 1)
                f(bcs[:, r, :], PB[2 + r][:, :], ACT.Copy, "bc_out")
            for r in range(RB):
                f(eb[:, r, :], PB[2 + r][:, :], ACT.Exp, "eb_out")
                f(einv[:, r, :], PB[2 + r][:, :], ACT.Exp, "einv_out", scale=-1.0)
            act.wait_ge(S("cum"), 2 * RB + 1)
            f(decay[:, :, :].rearrange("p h n -> p (h n)"), PB[5][:, 0:GH * NCH], ACT.Exp, "decay_out")
            for r in range(RB):
                act.wait_ge(S("left"), r + 1)
                f(kd[:, r, :], bcs[:, r, :], ACT.Exp, "edec_out")
            for k in range(4):
                act.wait_ge(S("qk_turned"), k + 1)
                dst = (qdT, kiT)[k % 2]
                f(dst[:, 2 * (k // 2):2 * (k // 2) + 2, :].rearrange("p h n -> p (h n)"), PB[k][:, :], ACT.Copy,
                  "qk_out")
            for r in range(RB):
                f(Z[:, r, Z_RG:Z_RG + GVAL], Z[:, r, Z_RG:Z_RG + GVAL], ACT.Silu, "r_gated")
            for h in range(GH):
                act.wait_ge(S("gla_o"), h + 1)
                for r in range(RB):
                    if h + r:
                        act.wait_ge(S("gla_sq"), RB * h + r)
                    f(JUNK[:, 0:GV], PB[h][:, GV * r:GV * r + GV], ACT.Square, "gla_sq",
                      accum_out=gst[:, 0, h, r:r + 1])
            act.wait_ge(S("gla_sq"), RB * GH)
            f(gst[:, 1, :, :], gst[:, 0, :, :], ACT.Sqrt, "gla_root", scale=1.0 / GV, bias=eps[:, 0:1])
            for name, c0, n in (("cq", Z_CQ, QR), ("ckv", Z_CKV, KVR)):
                norm_stats(name, lambda r: Z[:, r, c0:c0 + n], n)
                norm_rows(name, lambda r: Z[:, r, c0:c0 + n], lambda r: Z[:, r, c0:c0 + n], RB)
            turn_hi("cq", XTh, gain=vT[:, V_GQ:V_GQ + 4])
            turn_hi("ckv", XTh, 4, gain=vT[:, V_GKV:V_GKV + 2])
            act.wait_ge(S("angle"), 2 * RB)
            for r in range(RB):
                for k in range(2):
                    f(cs[:, r, k, :], ang[:, r, k, :], ACT.Sin, "sines")
            for c in range(3):
                hi()
                chunk_evac(CHUNK0["uq"] + c, lambda r: qrow[r][:, :, :].rearrange("p h d -> p (h d)")[:, 512 * c:512 * c + 512],
                           512, scale=QKD ** -0.5, done=st.lin - 1)
            for b in range(4):
                if b == 1:
                    hi()
                act.wait_ge(S("kT_made"), b + 1) if b < 3 else act.wait_ge(slab_used, st.lins(-1))
                f(kTn[b // 2][:, 2 * (b % 2):2 * (b % 2) + 2, :].rearrange("p h n -> p (h n)"),
                  PB[(4, 5, 6, 7)[b]][:, :], ACT.Copy, "kT_out")
            for c in range(2):
                act.wait_ge(S("v_made"), c + 1) if c == 0 else act.wait_ge(slab_used, st.lins())
                for r in range(RB):
                    act.activation(vrow[:, r, 512 * c:512 * c + 512], PB[2 * ((CHUNK0["uv"] + c) % 2) + r][:, :],
                                   ACT.Copy).then_inc(chunk_out, 1)
            act.wait_ge(S("kr_turned"), 1)
            f(krT[:, :], PB[4][0:ROPE, 0:SEQ], ACT.Copy, "kr_out")
            for h in range(MH + 2):
                if h < MH:
                    act.wait_ge(S("q_turned"), h + 1)
                    if h >= 2:
                        act.wait_ge(S("scored"), h - 1)
                    f(qTs[:, h % 2, 0:SEQ], PB[4 + h % 2][:, 0:SEQ], ACT.Copy, "q_out")
                    f(qTs[0:ROPE, h % 2, SEQ:2 * SEQ], PB[4 + h % 2][0:ROPE, SEQ:2 * SEQ], ACT.Copy, "q_out")
                g = h - 1
                if 0 <= g < MH:
                    act.wait_ge(S("maxed"), RB * (g + 1))
                    for r in range(RB):
                        part = prob[:, g % 2, P * r:P * (2 * r + 1)]
                        f(part, part, ACT.Exp, "exped", bias=mst[:, g % 4, 0, r:r + 1], accum_out=mst[:, g % 4, 1, r:r + 1])
                g = h - 2
                if 0 <= g < MH:
                    act.wait_ge(S("p_turned"), g + 1)
                    if g >= 2:
                        act.wait_ge(S("pv_done"), g - 1)
                    f(probT[:, g % 2, :], PB[2 + g % 2][:, 0:3 * P], ACT.Copy, "pT_out")
            skip(16)
            hi()
            turn_hi("o", XTh)
            for c in range(4):
                for s in range(4):
                    skip()
                    hi()
                chunk_evac(CHUNK0["wout"] + c, lambda r: ROWB[:, r, 512 * c:512 * c + 512], 512,
                           done=st.lin - 1)
                post_square("o", c, lambda r: act.wait_ge(chunk_out, RB * (CHUNK0["wout"] + c) + r + 1))
            post_root("o")

            def ffn(k, pre, added, more, gain=None):
                norm_stats(pre, lambda r: X[:, r, :], D, added)
                norm_rows(pre, lambda r: X[:, r, :], lambda r: ROWB[:, r, :])
                turn_hi(pre, XTh, gain=gain)
                b0 = RB * FN * k

                def chunk(j):
                    for _ in range(4):
                        hi()
                    act.wait_ge(slab_used, st.lins(-1))
                    if not isinstance(j, int) or k or j:
                        act.wait_ge(S("h_made"), j * RB + b0)
                    for r in range(RB):
                        act.activation(SIL[:, r, :], PB[r][:, :], ACT.Silu).then_inc(S("silu_out"), 1)
                    for _ in range(3):
                        hi()

                def hidden_hi(j):
                    for b in range(2):
                        act.wait_ge(S("h_turned"), j * 2 + (b0 + b + 1))
                        act.activation(HTh[:, 2 * b:2 * b + 2, :].rearrange("p t n -> p (t n)"), PB[4 + b][:, :],
                                       ACT.Copy).then_inc(S("hid_hi"), 1)

                chunk(0)
                hi()
                hidden_hi(0)
                with act.Fori(0, FN - 1) as i, st.loop(i, FN - 1, 12, 12):
                    chunk(i + 1)
                    for _ in range(5):
                        hi()
                    hidden_hi(i + 1)
                y_all = 8 * (FN + 1) * (k + 1)
                for n in range(4):
                    if n < 3 or more:
                        hi()
                    post_square(("y1", "y2")[k], n, lambda r: act.wait_ge(S("y_added"), y_all - 8 + RB * n + r + 1))
                post_root(("y1", "y2")[k])

            act.wait_ge(S("x_added"), 2)
            for b in range(4):
                act.wait_ge(S("g_wide"), 4 + b + 1)
                f(G[:, 512 * b:512 * b + 512], PB[6 + b % 2][:, :], ACT.Copy, "g_out")
            ffn(0, "f1", 0, True)
            norm_stats("z2", lambda r: X[:, r, :], D, 2)
            norm_rows("z2", lambda r: X[:, r, :], lambda r: ROWB[:, r, :])
            turn_hi("z2", XTh, gain=vT[:, V_LN_MIX:V_LN_MIX + KT])
            for c0, width in Z2_PARTS:
                with act.Fori(0, Z2N // 2) as i, st.loop(i, Z2N // 2, 8, 8):
                    for c in range(2):
                        for s in range(3):
                            hi(4 * width)
                        hi()
                        act.wait_ge(slab_used, st.lins(-1))
                        for r in range(RB):
                            act.activation(Z2[:, r, bass.ds(i * (2 * width) + (c0 + c * width), width)],
                                           PB[2 * (c % 2) + r][:, 0:width], ACT.Copy).then_inc(chunk_out, 1)
            for k in range(2):
                act.wait_ge(S("w1_used"), k + 1)
                f(hidT[:, k, :], PB[4 + k][:, 0:NG * NCMP], ACT.Gelu_apprx_tanh, "gelued")
            act.wait_ge(S("kc_done"), 1)
            f(kcT[:, :, :].rearrange("p g n -> p (g n)"), PB[6][0:HD, 0:NG * NCMP], ACT.Copy, "kc_out")
            act.wait_ge(S("kc_done"), 2)
            f(vc[:, :, :].rearrange("p g n -> p (g n)"), PB[7][0:NCMP, 0:NG * HD], ACT.Copy, "kc_out")
            for k in range(8):
                act.wait_ge(S("nq_turned"), k + 1)
                f(QT[:, 2 * k:2 * k + 2, :].rearrange("p h n -> p (h n)"), PB[4 + k % 4][0:HD, :], ACT.Copy, "nq_out",
                  scale=HD ** -0.5)
            for k in range(4):
                act.wait_ge(S("nk_turned"), k + 1)
                f(KT2[:, k, :, :].rearrange("p b n -> p (b n)"), PB[k][0:HD, :], ACT.Copy, "nk_out")
            for r in range(RB):
                f(Z2[:, r, Z2_GL:Z2_U], Z2[:, r, Z2_GL:Z2_U], ACT.Sigmoid, "gates_out")
            for t in range(NH * RB + 2):
                u = t - 1
                if 0 <= u < NH * RB:
                    nk, nc_ = (P, NCMP0) if u % 2 == 0 else (SEQ, NCMP)
                    act.wait_ge(S("n_maxed"), u + 1)
                    for b in range(2):
                        f(NSPROB(u % 2)[:, b * nk:b * nk + nk], NSPROB(u % 2)[:, b * nk:b * nk + nk], ACT.Exp, "n_exped",
                          bias=nst[:, u % 4, 0, b:b + 1], accum_out=nst[:, u % 4, 1, b + 1:b + 2])
                    f(pc[:, u % 2, 0:nc_], pc[:, u % 2, 0:nc_], ACT.Exp, "n_exped",
                      bias=nst[:, u % 4, 0, 2:3], accum_out=nst[:, u % 4, 1, 0:1])
                u = t - 2
                if 0 <= u < NH * RB:
                    nb = 2 + 2 * (u % 2)
                    act.wait_ge(S("n_turned"), u + 1)
                    if u >= 2:
                        act.wait_ge(S("n_pv"), u - 1)
                    f(pT[:, u % 2, 0:nb * P], PB[4 + u % 2][:, 0:nb * P], ACT.Copy, "npT_out")
            for r in range(RB):
                f(Z2[:, r, Z2_M:Z2W], Z2[:, r, Z2_M:Z2W], ACT.Sigmoid, "merge_gated")
            for g in range(PG):
                act.wait_ge(S("pool_mixed"), 2 * g + 2)
                f(XTh[:, 2 * g:2 * g + 2, :].rearrange("p t n -> p (t n)"), PB[g][:, :], ACT.Copy, "pool_hi")
            hi()
            for g in range(PG):
                act.wait_ge(S("pool_scaled"), g + 1)
                f(XTh[:, 8 + 2 * g:10 + 2 * g, :].rearrange("p t n -> p (t n)"), TMPP[:, g % 2, :], ACT.Copy, "pool_hi")
            turn_hi("att", XTh)
            for c in range(4):
                for s in range(4):
                    hi()
            turn_hi("y", XTh)
            for c in range(4):
                for s in range(4):
                    hi()
                chunk_evac(CHUNK0["mix"] + c, lambda r: ROWB[:, r, 512 * c:512 * c + 512], 512,
                           done=st.lin - 1)
                post_square("mix", c, lambda r: act.wait_ge(chunk_out, RB * (CHUNK0["mix"] + c) + r + 1))
            post_root("mix")
            norm_stats("xq", lambda r: X[:, r, :], D, 4)
            norm_rows("xq", lambda r: X[:, r, :], lambda r: ROWB[:, r, :])
            turn_hi("xq", XTh, gain=vT[:, V_LN_X:V_LN_X + KT])
            for s in range(4):
                hi()
            chunk_evac(CHUNK0["xq"], lambda r: HROW[:, r, :], 512, scale=XD ** -0.5, done=st.lin - 1)
            for b in range(2):
                act.wait_ge(S("xq_turned"), b + 1)
                f(xqT[:, 2 * b:2 * b + 2, :].rearrange("p h n -> p (h n)"), PB[6 + b][:, :], ACT.Copy, "xq_out")
            for h in range(XH + 1):
                if h < XH:
                    act.wait_ge(S("x_maxed"), h + 1)
                    for r in range(RB):
                        if h >= 2:
                            act.wait_ge(S("xp_turned"), h - 1)
                        f(xp[:, h % 2, SEQ * r:SEQ * r + SEQ], PB[h % 2][:, SEQ * r:SEQ * r + SEQ], ACT.Exp, "x_exped",
                          bias=mst[:, h % 4, 0, r:r + 1], accum_out=mst[:, h % 4, 1, r:r + 1])
                g = h - 1
                if g >= 0:
                    act.wait_ge(S("xp_turned"), g + 1)
                    if g >= 2:
                        act.wait_ge(S("x_pv"), g - 1)
                    f(xpT[:, g % 2, :], PB[4 + g % 2][:, :], ACT.Copy, "xpT_out")
            turn_hi("xo", XTh, 12)
            for c in range(4):
                hi()
                chunk_evac(CHUNK0["xo"] + c, lambda r: ROWB[:, r, 512 * c:512 * c + 512], 512,
                           done=st.lin - 1)
                post_square("xo", c, lambda r: act.wait_ge(chunk_out, RB * (CHUNK0["xo"] + c) + r + 1))
            post_root("xo")
            ffn(1, "f2", 6, False, vT[:, V_LN_FFN:V_LN_FFN + KT])

        @block.tensor
        def _(pe):
            st = Slabs()

            def turn(name, src, ready):
                ready()
                for b in range(TURN_N[name]):
                    g = TURN0[name] + b
                    if g >= 2:
                        pe.wait_ge(S("turn_free"), g - 1)
                    for k in range(2):
                        for r in range(RB):
                            mm = pe.transpose(PB[4 + g % 2][:, SEQ * k + P * r:SEQ * k + P * r + P],
                                              src(r, 2 * b + k), ident)
                    mm.then_inc(S("turned"), 1)

            def turned_ready(name):
                pe.wait_ge(S("turn_free"), TURN0[name] + TURN_N[name])

            def slab_mm(banks, kts, width, first, last, lhs=None):
                hi_t, lo_t = lhs or (XTh, XTl)
                pe.wait_ge(slab_done, st.raws(1))
                n = len(kts)
                w = [t[:, st.lin % 2, 0:n * width].rearrange("p (t n) -> p t n", t=n) for t in (wh, wl)]
                for r in range(RB):
                    for q, k in enumerate(kts):
                        rows = slice(P * r, P * r + P)
                        out_ = PB[banks[r]][:, 0:width]
                        pe.matmul(out_, hi_t[:, k, rows], w[0][:, q, :], start=first and q == 0, stop=False)
                        pe.matmul(out_, hi_t[:, k, rows], w[1][:, q, :], start=False, stop=False)
                        mm = pe.matmul(out_, lo_t[:, k, rows], w[0][:, q, :], start=False, stop=last and q == n - 1)
                mm.then_inc(slab_used, 1)
                st.next()

            def chunk(c, kts, width, skip=0, free=None):
                if free is not None:
                    pe.wait_ge(chunk_out, free)
                elif c >= 2:
                    pe.wait_ge(chunk_out, RB * (c - 1))
                n = len(kts) // 4
                for s in range(n):
                    slab_mm((2 * (c % 2), 2 * (c % 2) + 1), kts[4 * s:4 * s + 4], width, s == 0, s == n - 1)
                    for _ in range(skip):
                        st.next(False)

            ALL = list(range(KT))

            def mod_sum(v):
                pe.wait_ge(slab_done, st.raws())
                if v:
                    pe.wait_ge(S("mod_ready"), v)
                for k in range(KT):
                    mm = pe.matmul(PB[7][:, k:k + 1], ACC[:, P * k:P * k + P], ones[:, 0:1], start=True, stop=True)
                mm.then_inc(S("mod_sum"), 1)

            def gain_rows(banks):
                for b in range(4):
                    if b >= 2:
                        pe.wait_ge(S("g_out"), gain_rows.n + b - 1)
                    for k in range(4):
                        mm = pe.matmul(PB[banks[b % 2]][:, P * k:P * k + P],
                                       gT[:, 4 * b + k:4 * b + k + 1].broadcast_to([P, P]), ident, start=True, stop=True)
                    mm.then_inc(S("g_wide"), 1)
                gain_rows.n += 4

            gain_rows.n = 0

            pe.wait_ge(S("con_in"), 16)
            pe.wait_ge(S("vec_in"), 16 * 13)
            pe.transpose(PB[0][:, 0:126], VROW[0:126, :], ident[0:126, 0:126]).then_inc(S("vec_turned"), 1)
            pe.transpose(PB[1][:, 0:P], BROW[:, :], ident).then_inc(S("vec_turned"), 1)
            pe.wait_ge(S("rel_bias_in"), 32)
            pe.transpose(PB[2][0:BUCKETS, 0:NH], rb16[:, :], ident[0:NH, 0:NH]).then_inc(S("rel_turned"), 1)
            pe.wait_ge(S("rel_turned_out"), 1)
            pe.matmul(PB[3][0:NH, 0:SEQ], rbT[:, :], onehot[:, :], start=True, stop=True).then_inc(S("rel_made"), 1)
            turn("mem", lambda r, k: ROWB[:, r, P * k:P * k + P], lambda: pe.wait_ge(S("normed"), RB))
            turned_ready("mem")
            pe.wait_ge(S("vec_out"), 2)
            for _ in range(KT):
                st.next(False)
            mod_sum(0)
            chunk(0, ALL, 512)
            pe.wait_ge(chunk_out, RB)
            for b in range(2):
                for k in range(2):
                    for r in range(RB):
                        h = 2 * b + k
                        mm = pe.transpose(PB[6 + b][:, SEQ * k + P * r:SEQ * k + P * r + P], HROW[:, r, XD * h:XD * h + XD],
                                          ident)
                mm.then_inc(S("xk_turned"), 1)
            pe.wait_ge(S("xk_out"), 2)
            pe.wait_ge(S("rel_row"), 1)
            chunk(1, ALL, 512, skip=2)
            for _ in range(8):
                st.next(False)
            mod_sum(1)
            turn("x", lambda r, k: ROWB[:, r, P * k:P * k + P], lambda: pe.wait_ge(S("normed"), RB * 2))
            turned_ready("x")
            with pe.Fori(0, 2) as i, st.loop(i, 2, 32, 16):
                for c in range(4):
                    chunk(c, ALL, ZC, skip=1, free=i * 8 + (RB * (c + 1) if c else RB))
                pe.wait_ge(slab_done, st.raws())
                pe.wait_ge(S("mod_ready"), i + 2)
                for k in range(KT):
                    mm = pe.matmul(PB[7][:, k:k + 1], ACC[:, P * k:P * k + P], ones[:, 0:1], start=True, stop=True)
                mm.then_inc(S("mod_sum"), 1)
            pe.wait_ge(S("gate_ready"), 1)
            gain_rows((4, 5))
            pe.wait_ge(chunk_out, RB * CHUNK0["uq"])
            for r in range(RB):
                mm = pe.transpose(PB[6][0:GR, P * r:P * r + P], Z[:, r, Z_AG:Z_RG], ident)
            mm.then_inc(S("a_turned"), 1)
            pe.wait_ge(S("gla_in"), 48)
            pe.wait_ge(S("a_out"), 1)
            for r in range(RB):
                pe.matmul(PB[r][:, :], aT[:, P * r:P * r + P], wgu[:, :], start=True, stop=False)
                pe.matmul(PB[r][:, :], ones[0:1, :], bgr[:, :], start=False, stop=True).then_inc(S("gate_in"), 1)
            pe.wait_ge(S("log_a"), RB)
            for r in range(RB):
                pe.matmul(PB[2 + r][:, :], tri, la[:, r, :], start=True, stop=True).then_inc(S("cum"), 1)
            for r in range(RB):
                pe.matmul(PB[6 + r][:, :], blk, la[:, r, :], start=True, stop=True).then_inc(S("cum"), 1)
            pe.wait_ge(S("g_out"), 4)
            for h in range(GH):
                for r in range(RB):
                    n = NCH * h + 2 * r
                    mm = pe.matmul(PB[5][:, n:n + 2], la[:, r, GK * h:GK * h + GK], blk[:, 0:CH + 1:CH], start=True, stop=True)
            mm.then_inc(S("cum"), 1)
            pe.wait_ge(S("decayed"), 2 * RB)
            pe.wait_ge(S("einv_out"), RB)
            for b in range(4):
                c0 = (Z_QG, Z_KG)[b % 2]
                for k in range(2):
                    for r in range(RB):
                        h = 2 * (b // 2) + k
                        mm = pe.transpose(PB[b][:, SEQ * k + P * r:SEQ * k + P * r + P],
                                          Z[:, r, c0 + GK * h:c0 + GK * h + GK], ident)
                mm.then_inc(S("qk_turned"), 1)
            pe.wait_ge(S("qk_out"), 4)
            pe.wait_ge(S("decay_out"), 1)
            for b in range(2):
                for k in range(2):
                    for r in range(RB):
                        h, rows = 2 * b + k, slice(P * r, P * r + P)
                        mm = pe.matmul(PB[4 + b][:, SEQ * k + P * r:SEQ * k + P * r + P], kiT[:, h, rows],
                                       qdT[:, h, rows], start=True, stop=True)
                mm.then_inc(S("gla_scored"), 1)
            pe.wait_ge(S("left"), RB)
            pe.wait_ge(S("k_decayed"), RB)
            for m in range(3 * GH):
                h, n = m // 3, m % 3
                rows = slice(CH * (n % 2), CH * (n % 2) + CH)
                bank, half = (6 + h // 2, h % 2) if n == 1 else (h, n // 2)
                mm = pe.matmul(PB[bank][:, GV * half:GV * half + GV],
                               kd[rows, n // 2, GK * h:GK * h + GK],
                               Z[rows, n // 2, Z_VG + GV * h:Z_VG + GV * h + GV], start=True, stop=True)
                mm.then_inc(S("state_add"), 1)
            for h in range(GH):
                pe.wait_ge(S("stated"), 3 * GH)
                pe.wait_ge(S("att_masked"), 2)
                for r in range(RB):
                    o = PB[h][:, GV * r:GV * r + GV]
                    pe.matmul(o, attT[:, h, r, :], Z[:, r, Z_VG + GV * h:Z_VG + GV * h + GV], start=True,
                              stop=False, skip_group_check=True)
                    for n in range(2 * r, 2 * r + 2):
                        if n:
                            q = CH * (n % 2)
                            mm = pe.matmul(PB[h][q:q + CH, GV * r:GV * r + GV], qdT[:, h, CH * n:CH * n + CH],
                                           states[:, h, n - 1, :], start=False, stop=n % 2 == 1,
                                           skip_group_check=True)
                mm.then_inc(S("gla_o"), 1)
            turn("cq", lambda r, k: Z[:, r, Z_CQ + P * k:Z_CQ + P * k + P], lambda: pe.wait_ge(S("normed"), RB * 3))
            turn("ckv", lambda r, k: Z[:, r, Z_CKV + P * k:Z_CKV + P * k + P], lambda: pe.wait_ge(S("normed"), RB * 4))
            turned_ready("cq")
            pe.wait_ge(S("gla_done"), RB * GH)
            for c in range(3):
                chunk(CHUNK0["uq"] + c, [0, 1, 2, 3], 512)
            turned_ready("ckv")
            pe.wait_ge(slab_done, st.raws(1))
            w = [t[:, st.lin % 2, :].rearrange("p (t n) -> p t n", t=2) for t in (wh, wl)]
            for b in range(4):
                for k in range(2):
                    h = 2 * b + k
                    o = PB[4 + b][:, SEQ * k:SEQ * k + SEQ]
                    for t in range(2):
                        cols = slice(NOPE * h, NOPE * h + NOPE)
                        pe.matmul(o, w[0][:, t, cols], XTh[:, 4 + t, :], start=t == 0, stop=False)
                        pe.matmul(o, w[0][:, t, cols], XTl[:, 4 + t, :], start=False, stop=False)
                        mm = pe.matmul(o, w[1][:, t, cols], XTh[:, 4 + t, :], start=False, stop=t == 1)
                mm.then_inc(S("kT_made") if b < 3 else slab_used, 1)
            st.next()
            pe.wait_ge(slab_done, st.raws(1))
            w = [t[:, st.lin % 2, :].rearrange("p (t n) -> p t n", t=2) for t in (wh, wl)]
            for c in range(2):
                n = CHUNK0["uv"] + c
                pe.wait_ge(chunk_out, RB * (n - 1))
                for r in range(RB):
                    o, rows = PB[2 * (n % 2) + r][:, :], slice(P * r, P * r + P)
                    for t in range(2):
                        cols = slice(512 * c, 512 * c + 512)
                        pe.matmul(o, XTh[:, 4 + t, rows], w[0][:, t, cols], start=t == 0, stop=False)
                        pe.matmul(o, XTh[:, 4 + t, rows], w[1][:, t, cols], start=False, stop=False)
                        mm = pe.matmul(o, XTl[:, 4 + t, rows], w[0][:, t, cols], start=False, stop=t == 1)
                mm.then_inc(S("v_made") if c == 0 else slab_used, 1)
            st.next()
            pe.wait_ge(S("roped"), 2 * RB)
            pe.wait_ge(S("kT_out"), 4)
            for r in range(RB):
                mm = pe.transpose(PB[4][0:ROPE, P * r:P * r + P], Z[:, r, Z_KR:Z_QG], ident)
            mm.then_inc(S("kr_turned"), 1)
            pe.wait_ge(S("kr_out"), 1)
            pe.wait_ge(chunk_out, RB * CHUNK0["wout"])
            for t in range(MH + 3):
                if t < MH:
                    if t >= 2:
                        pe.wait_ge(S("q_out"), 2 * (t - 1))
                    for r in range(RB):
                        pe.transpose(PB[4 + t % 2][:, P * r:P * r + P], qrow[r][:, t, 0:NOPE], ident)
                        mm = pe.transpose(PB[4 + t % 2][0:ROPE, SEQ + P * r:SEQ + P * r + P], qrow[r][:, t, NOPE:QKD],
                                          ident)
                    mm.then_inc(S("q_turned"), 1)
                h = t - 1
                if 0 <= h < MH:
                    pe.wait_ge(S("q_out"), 2 * (h + 1))
                    if h >= 2:
                        pe.wait_ge(S("masked"), h - 1)
                    for r in range(RB):
                        nk = P * (r + 1)
                        o = PB[6 + h % 2][:, P * r:P * r + nk]
                        pe.matmul(o, qTs[:, h % 2, P * r:P * r + P], kTn[h // 4][:, h % 4, 0:nk], start=True, stop=False)
                        mm = pe.matmul(o, qTs[0:ROPE, h % 2, SEQ + P * r:SEQ + P * r + P], krT[:, 0:nk], start=False,
                                       stop=True)
                    mm.then_inc(S("scored"), 1)
                h = t - 2
                if 0 <= h < MH:
                    pe.wait_ge(S("exped"), RB * (h + 1))
                    if h >= 2:
                        pe.wait_ge(S("pT_out"), h - 1)
                    for b in range(3):
                        mm = pe.transpose(PB[2 + h % 2][:, P * b:P * b + P], prob[:, h % 2, P * b:P * b + P], ident)
                    mm.then_inc(S("p_turned"), 1)
                h = t - 3
                if 0 <= h < MH:
                    pe.wait_ge(S("pT_out"), h + 1)
                    if h >= 2:
                        pe.wait_ge(S("mla_o"), RB * (h - 1))
                    v = [vrow[:, r, VD * h:VD * h + VD] for r in range(RB)]
                    o = PB[h % 2]
                    pe.matmul(o[:, 0:VD], probT[:, h % 2, 0:P], v[0], start=True, stop=True)
                    pe.matmul(o[:, P:P + VD], probT[:, h % 2, P:2 * P], v[0], start=True, stop=False)
                    mm = pe.matmul(o[:, P:P + VD], probT[:, h % 2, 2 * P:3 * P], v[1], start=False, stop=True)
                    mm.then_inc(S("pv_done"), 1)
            for _ in range(16):
                st.next(False)
            mod_sum(4)
            turn("o", lambda r, k: Z[:, r, Z_QG + P * k:Z_QG + P * k + P], lambda: pe.wait_ge(S("mla_o"), RB * MH))
            turned_ready("o")
            for c in range(4):
                chunk(CHUNK0["wout"] + c, ALL, 512, skip=1)
            mod_sum(5)

            def ffn(k, pre, n_normed):
                b0 = RB * FN * k
                y0 = 8 * (FN + 1) * k
                turn(pre, lambda r, q: ROWB[:, r, P * q:P * q + P], lambda: pe.wait_ge(S("normed"), RB * n_normed))
                turned_ready(pre)
                pe.wait_ge(S("y_added"), y0 + 8)

                def gate_up(j):
                    for half in range(2):
                        if not isinstance(j, int):
                            pe.wait_ge(S(("silu_out", "h_made")[half]), j * RB + b0)
                            pe.wait_ge(S("y_added"), j * 8 + (y0 - 8 + (4, 8)[half]))
                        for s in range(4):
                            slab_mm((2 * half, 2 * half + 1), ALL[4 * s:4 * s + 4], 512, s == 0, s == 3)

                def hidden_turn(j):
                    pe.wait_ge(S("h_made"), j * RB + (b0 + RB))
                    if not isinstance(j, int):
                        pe.wait_ge(S("hid_lo"), j * 2 + b0)
                    for b in range(2):
                        for q in range(2):
                            for r in range(RB):
                                mm = pe.transpose(PB[4 + b][:, SEQ * q + P * r:SEQ * q + P * r + P],
                                                  HROW[:, r, P * (2 * b + q):P * (2 * b + q) + P], ident)
                        mm.then_inc(S("h_turned"), 1)

                def down(j):
                    pe.wait_ge(S("hid_lo"), j * 2 + (b0 + 2))
                    for n in range(4):
                        banks = ((6, 7), (0, 1), (6, 7), (2, 3))[n]
                        if n == 0 and not (isinstance(j, int) and j == 0):
                            pe.wait_ge(S("y_added"), j * 8 + (y0 + 6))
                        if n == 1:
                            pe.wait_ge(S("silu_out"), (j + 2) * RB + b0 if not isinstance(j, int) else RB * FN + b0)
                        if n == 2:
                            pe.wait_ge(S("y_added"), j * 8 + (y0 + 8 + 2))
                        if n == 3 and not isinstance(j, int):
                            pe.wait_ge(S("h_made"), (j + 2) * RB + b0)
                        slab_mm(banks, [0, 1, 2, 3], 512, True, True, lhs=(HTh, HTl))

                gate_up(0)
                hidden_turn(0)
                with pe.Fori(0, FN - 1) as i, st.loop(i, FN - 1, 12, 12):
                    gate_up(i + 1)
                    down(i)
                    hidden_turn(i + 1)
                down(FN - 1)

            pe.wait_ge(S("mod_ready"), 6)
            gain_rows((6, 7))
            ffn(0, "f1", 5)
            turn("z2", lambda r, k: ROWB[:, r, P * k:P * k + P], lambda: pe.wait_ge(S("normed"), RB * 6))
            turned_ready("z2")
            for part, (_, width) in enumerate(Z2_PARTS):
                with pe.Fori(0, Z2N // 2) as i, st.loop(i, Z2N // 2, 8, 8):
                    for c in range(2):
                        chunk(c, ALL, width, free=i * 4 + RB * (CHUNK0["zin2"] + Z2N * part + c - 1))
            pe.wait_ge(S("cmp_in"), 64)
            pe.wait_ge(chunk_out, RB * CHUNK0["mix"])
            pe.transpose(PB[6][:, 0:2 * CS], perow[:, :], ident[0:2 * CS, 0:2 * CS]).then_inc(S("pe_turned"), 1)
            for b in range(4):
                for k in range(2):
                    for r in range(RB):
                        c0 = Z2_KV + KVW * (b // 2) + HD * (2 * (b % 2) + k)
                        cols = slice(SEQ * k + P * r, SEQ * k + P * r + P)
                        pe.transpose(PB[b][0:HD, cols], Z2[:, r, c0:c0 + HD], ident)
                        mm = pe.matmul(PB[b][HD:2 * HD, cols], Z2[:, r, c0:c0 + HD], ident, start=True, stop=True)
                mm.then_inc(S("raw_turned"), 1)
            for k in range(2):
                pe.wait_ge(S(f"w1_in{k}"), 32)
                pe.wait_ge(S("raw_out"), 2 * k + 2)
                for l in range(CS):
                    mm = pe.matmul(PB[4 + k][:, 0:NG * NCMP].rearrange("p (g n) -> p g n", g=NG), w1s[:, k, l, :],
                                   rawT[:, k, :, l:l + CS * (NCMP - 1) + 1:CS], start=l == 0, stop=l == CS - 1)
                mm.then_inc(S("w1_used"), 1)
            pe.wait_ge(S("gelued"), 2)
            pe.matmul(PB[6][0:HD, 0:NG * NCMP], w2s[:, 0, :], hidT[:, 0, :], start=True, stop=True).then_inc(S("kc_done"), 1)
            for g in range(NG):
                mm = pe.matmul(PB[7][0:NCMP, HD * g:HD * g + HD], hidT[:, 1, NCMP * g:NCMP * g + NCMP], w2s[:, 1, :],
                               start=True, stop=True)
            mm.then_inc(S("kc_done"), 1)
            pe.wait_ge(S("kc_out"), 2)
            for k in range(8):
                if k >= 4:
                    pe.wait_ge(S("nq_out"), k - 3)
                for q in range(2):
                    for r in range(RB):
                        h = 2 * k + q
                        mm = pe.transpose(PB[4 + k % 4][0:HD, SEQ * q + P * r:SEQ * q + P * r + P],
                                          Z2[:, r, HD * h:HD * h + HD], ident)
                mm.then_inc(S("nq_turned"), 1)
            for g in range(NG):
                for b in range(2):
                    for r in range(RB):
                        c0 = Z2_KV + KVW * (2 + 2 * b) + HD * g
                        mm = pe.transpose(PB[g][0:HD, SEQ * b + P * r:SEQ * b + P * r + P], Z2[:, r, c0:c0 + HD], ident)
                mm.then_inc(S("nk_turned"), 1)
            pe.wait_ge(S("nq_out"), 8)
            pe.wait_ge(S("nk_out"), 4)
            for t in range(NH * RB + 3):
                u = t - 2
                if 0 <= u < NH * RB:
                    r = u % 2
                    nk, n_c = P * (r + 1), (NCMP0, NCMP)[r]
                    pe.wait_ge(S("n_exped"), 3 * (u + 1))
                    if u >= 2:
                        pe.wait_ge(S("npT_out"), u - 1)
                    pe.wait_ge(S("n_added"), u + 1)
                    pe.transpose(PB[2 + u % 2][0:n_c, P:2 * P], pc[:, u % 2, 0:n_c], ident)
                    for b in range(2 * (r + 1)):
                        mm = pe.transpose(PB[4 + u % 2][:, P * b:P * b + P], NSPROB(u % 2)[:, P * b:P * b + P], ident)
                    mm.then_inc(S("n_turned"), 1)
                u = t
                if u < NH * RB:
                    h, r = u // 2, u % 2
                    g, nk, n_c = h // HPG, P * (r + 1), (NCMP0, NCMP)[r]
                    if u >= 2:
                        pe.wait_ge(S("n_added"), u - 1)
                    q = QT[:, h, P * r:P * r + P]
                    for b in range(2):
                        pe.matmul(PB[u % 2][:, nk * b:nk * b + nk], q, KT2[:, g, b, 0:nk], start=True, stop=True)
                    if u >= 2:
                        pe.wait_ge(S("n_cT"), u - 1)
                    pe.matmul(PB[2 + u % 2][:, 0:n_c], q, kcT[:, g, 0:n_c], start=True, stop=True)\
                        .then_inc(S("n_scored"), 1)
                u = t - 3
                if 0 <= u < NH * RB:
                    h, r = u // 2, u % 2
                    g, n_c = h // HPG, (NCMP0, NCMP)[r]
                    pe.wait_ge(S("npT_out"), u + 1)
                    pe.wait_ge(S("n_cT"), u + 1)
                    if u >= 2:
                        pe.wait_ge(S("nsa_o"), 3 * (u - 1))
                    for b in range(2):
                        for k in range(r + 1):
                            c0 = Z2_KV + KVW * (3 + 2 * b) + HD * g
                            blk_ = b * (r + 1) + k
                            pe.matmul(PB[6 + u % 2][:, HD * b:HD * b + HD], pT[:, u % 2, P * blk_:P * blk_ + P],
                                      Z2[:, k, c0:c0 + HD], start=k == 0, stop=k == r)
                    pe.matmul(PB[6 + u % 2][:, 2 * HD:3 * HD], pcT[0:n_c, u % 2, :], vc[0:n_c, g, :], start=True, stop=True)\
                        .then_inc(S("n_pv"), 1)
            pe.wait_ge(S("band_in"), 16)
            pe.wait_ge(S("nsa_o"), 3 * NH * RB)
            for m in range(2 * PG):
                g, t = m // 2, m % 2
                c0 = Z2_U + PGW * g + P * t
                o = PB[g][:, SEQ * t:SEQ * t + SEQ]
                pe.matmul(o, Z2[:, 0, c0:c0 + P], band[:, g, 0:SEQ], start=True, stop=False, skip_group_check=True)
                pe.matmul(PB[g][:, SEQ * t + P:SEQ * t + SEQ], Z2[:, 1, c0:c0 + P], band[:, g, SEQ:], start=False,
                          stop=True, skip_group_check=True).then_inc(S("pool_mixed"), 1)
            pe.wait_ge(slab_done, st.raws(1))
            w = [t[:, st.lin % 2, :].rearrange("p (g t n) -> p g t n", g=PG, t=2) for t in (wh, wl)]
            for g in range(PG):
                pe.wait_ge(S("pool_lo"), g + 1)
                for q in range(2):
                    o, cols = PB[4 + g][:, SEQ * q:SEQ * q + SEQ], slice(P * q, P * q + P)
                    for t in range(2):
                        pe.matmul(o, w[0][:, g, t, cols], XTh[:, 2 * g + t, :], start=t == 0, stop=False)
                        pe.matmul(o, w[0][:, g, t, cols], XTl[:, 2 * g + t, :], start=False, stop=False)
                        mm = pe.matmul(o, w[1][:, g, t, cols], XTh[:, 2 * g + t, :], start=False, stop=t == 1)
                mm.then_inc(S("pool_lin") if g < PG - 1 else slab_used, 1)
            st.next()
            pe.wait_ge(S("pool_lo"), 2 * PG)
            turn("att", lambda r, k: Z2[:, r, P * k:P * k + P], lambda: None)
            turned_ready("att")
            for c in range(4):
                if c:
                    pe.wait_ge(S("merged"), 3 * RB * c)
                for half in range(2):
                    for s in range(2):
                        k = 8 * half + 4 * s
                        slab_mm((2 * half, 2 * half + 1), ALL[k:k + 4], 512, s == 0, s == 1)
            turn("y", lambda r, k: Z2[:, r, P * k:P * k + P], lambda: pe.wait_ge(S("merged"), 3 * RB * 4))
            turned_ready("y")
            for c in range(4):
                chunk(CHUNK0["mix"] + c, ALL, 512)
            turn("xq", lambda r, k: ROWB[:, r, P * k:P * k + P], lambda: pe.wait_ge(S("normed"), RB * 7))
            turned_ready("xq")
            chunk(CHUNK0["xq"], ALL, 512)
            pe.wait_ge(chunk_out, RB * CHUNK0["xo"])
            for b in range(2):
                for k in range(2):
                    for r in range(RB):
                        h = 2 * b + k
                        mm = pe.transpose(PB[6 + b][:, SEQ * k + P * r:SEQ * k + P * r + P], HROW[:, r, XD * h:XD * h + XD],
                                          ident)
                mm.then_inc(S("xq_turned"), 1)
            pe.wait_ge(S("xq_out"), 2)
            for t in range(XH + 2):
                h = t
                if h < XH:
                    if h >= 2:
                        pe.wait_ge(S("x_exped"), RB * (h - 1))
                    for r in range(RB):
                        mm = pe.matmul(PB[h % 2][:, SEQ * r:SEQ * r + SEQ], xqT[:, h, P * r:P * r + P], xkT[:, h, :],
                                       start=True, stop=True)
                    mm.then_inc(S("x_scored"), 1)
                h = t - 1
                if 0 <= h < XH:
                    pe.wait_ge(S("x_exped"), RB * (h + 1))
                    if h >= 2:
                        pe.wait_ge(S("xpT_out"), h - 1)
                    for b in range(4):
                        mm = pe.transpose(PB[4 + h % 2][:, P * b:P * b + P], xp[:, h % 2, P * b:P * b + P], ident)
                    mm.then_inc(S("xp_turned"), 1)
                h = t - 2
                if 0 <= h < XH:
                    pe.wait_ge(S("xpT_out"), h + 1)
                    if h >= 2:
                        pe.wait_ge(S("xatt_o"), RB * (h - 1))
                    for r in range(RB):
                        for k in range(RB):
                            mm = pe.matmul(PB[2 + h % 2][:, P * r:P * r + XD], xpT[:, h % 2, P * (2 * r + k):P * (2 * r + k) + P],
                                           xv[:, k, XD * h:XD * h + XD], start=k == 0, stop=k == 1)
                    mm.then_inc(S("x_pv"), 1)
            turn("xo", lambda r, k: SIL[:, r, P * k:P * k + P], lambda: pe.wait_ge(S("xatt_o"), RB * XH))
            turned_ready("xo")
            for c in range(4):
                chunk(CHUNK0["xo"] + c, [12, 13, 14, 15], 512)
            ffn(1, "f2", 8)

        @block.vector
        def _(dve):
            st = Slabs()
            link = Chain(dve, S("dve_step"))

            def tt(out_, a, b, op):
                return dve.tensor_tensor(out_, a, b, op)

            def lo(width=2048):
                dve.wait_ge(hi_made, st.lins(1))
                tt(wl[:, st.lin % 2, 0:width], raw[:, st.raw % 4, 0:width], f32(wh[:, st.lin % 2, 0:width]),
                   ALU.subtract).then_inc(slab_done, 1)
                st.next()

            def ada(k):
                dve.wait_ge(landed[st.raw % 4], st.landed())
                if st.raw or st.i is not None:
                    dve.wait_ge(slab_done, st.raws())
                w = raw[:, st.raw % 4, :]
                if k == 0:
                    ins = dve.tensor_scalar(ACC[:, :], w, cT[:, 0:1], None, ALU.mult)
                else:
                    ins = dve.scalar_tensor_tensor(ACC[:, :], w, cT[:, k:k + 1], ACC[:, :], ALU.mult, ALU.add)
                ins.then_inc(slab_done, 1)
                st.next(False)

            def mod_fin(v):
                dve.wait_ge(S("mod_sum"), v + 1)
                if v in (0, 3):
                    tt(modA[:, (0, 0, 0, 2)[v], :], PB[7][:, 0:KT], bT[:, KT * v:KT * v + KT], ALU.add)\
                        .then_inc(S("mod_ready"), 1)
                elif v in (1, 4):
                    gain = vT[:, V_PRE_MIX:V_PRE_MIX + KT] if v == 1 else vT[:, V_PRE_FFN:V_PRE_FFN + KT]
                    link(tt(mtmp[:, :], PB[7][:, 0:KT], bT[:, KT * v:KT * v + KT], ALU.add))
                    dve.scalar_tensor_tensor(modA[:, 1 if v == 1 else 3, :], mtmp[:, :], 1.0, gain, ALU.add, ALU.mult)\
                        .then_inc(S("mod_ready"), 1)
                else:
                    gain = bT[:, 96:112] if v == 2 else bT[:, 112:128]
                    link(tt(mtmp[:, :], PB[7][:, 0:KT], bT[:, KT * v:KT * v + KT], ALU.add))
                    tt(gT[:, :], mtmp[:, :], gain, ALU.mult).then_inc(S("mod_ready"), 1)

            def norm_inv(name):
                j = NORMS.index(name)
                dve.wait_ge(S("rooted"), j + 1)
                dve.reciprocal(nstat[:, j, 2, :], nstat[:, j, 1, :]).then_inc(S("rooted_inv"), 1)

            def turn_lo(name, hi_t, lo_t, gain=None, shift=None, k0=0):
                n = TURN_N[name]

                def gained(b):
                    g = TURN0[name] + b
                    dve.wait_ge(S("turned"), g + 1)
                    for k in range(2):
                        kt = 2 * b + k
                        half = slice(SEQ * k, SEQ * k + SEQ)
                        ins = dve.tensor_scalar(TMP[:, g % 2, half], PB[4 + g % 2][:, half], gain[:, kt:kt + 1],
                                                shift[:, kt:kt + 1], ALU.mult, ALU.add)
                    ins.then_inc(S("gained"), 1)

                def rest(b):
                    g = TURN0[name] + b
                    dve.wait_ge(S("turn_hi"), HI0[name] + b + 1)
                    src = TMP[:, g % 2, :] if shift is not None else PB[4 + g % 2][:, :]
                    sl = (slice(None), slice(k0 + 2 * b, k0 + 2 * b + 2), slice(None))
                    tt(lo_t[sl].rearrange("p t n -> p (t n)"), src, f32(hi_t[sl].rearrange("p t n -> p (t n)")),
                       ALU.subtract).then_inc(S("turn_free"), 1)

                def gained_rest(b):
                    g = TURN0[name] + b
                    dve.wait_ge(S("turn_hi"), HI0[name] + 2 * b + 2)
                    for k in range(2):
                        kt = 2 * b + k
                        ins = dve.scalar_tensor_tensor(lo_t[:, k0 + kt, :], PB[4 + g % 2][:, SEQ * k:SEQ * k + SEQ],
                                                       gain[:, kt:kt + 1], f32(hi_t[:, k0 + kt, :]), ALU.mult, ALU.subtract)
                    ins.then_inc(S("turn_free"), 1)

                if shift is not None:
                    for b in range(n + 1):
                        if b < n:
                            gained(b)
                        if b:
                            rest(b - 1)
                else:
                    for b in range(n):
                        rest(b) if gain is None else gained_rest(b)

            def norm_row2(name):
                j = NORMS.index(name)
                norm_inv(name)
                dve.wait_ge(S("rooted_inv"), j + 1)
                src = MEM if name == "mem" else X
                dve.tensor_scalar(ROWB[:, 1, :], src[:, 1, :], nstat[:, j, 2, 1:2], None, ALU.mult).then_inc(S("normed"), 1)

            def weigh(name, c):
                m = 4 * RB * POST.index(name) + RB * c
                for r in range(RB):
                    dve.wait_ge(S("part_sq"), m + r + 1)
                    y = ROWB[:, r, 512 * c:512 * c + 512]
                    tt(y, y, G[:, 512 * c:512 * c + 512], ALU.mult).then_inc(S("weighed"), 1)

            def add_normed(name):
                j, q = NORMS.index(name), POST.index(name)
                dve.wait_ge(S("part_sq"), 4 * RB * (q + 1))
                dve.tensor_reduce(nstat[:, j, 0, :], psq[:, q, :, :], AX.X, ALU.add).then_inc(S("squared"), RB)
                weigh(name, 3)
                norm_inv(name)
                dve.wait_ge(S("rooted_inv"), j + 1)
                dve.wait_ge(S("weighed"), 4 * RB * (q + 1))
                for r in range(RB):
                    dve.scalar_tensor_tensor(X[:, r, :], ROWB[:, r, :], nstat[:, j, 2, r:r + 1], X[:, r, :], ALU.mult,
                                             ALU.add).then_inc(S("x_added"), 1)

            dve.memset(eps[:, :], EPS).then_inc(S("zeroed"), 1)
            dve.memset(one[:, :], 1.0).then_inc(S("zeroed"), 1)
            for k in range(2):
                dve.wait_ge(S("vec_turned"), k + 1)
                n = (126, P)[k]
                dve.tensor_copy((vT, bT)[k][:, 0:n], PB[k][:, 0:n]).then_inc(S("vec_out"), 1)
            dve.wait_ge(S("rel_turned"), 1)
            dve.tensor_copy(rbT[:, :], PB[2][0:BUCKETS, 0:NH]).then_inc(S("rel_turned_out"), 1)
            dve.wait_ge(S("rel_made"), 1)
            dve.tensor_copy(relrow[:, 0:SEQ], PB[3][0:NH, 0:SEQ]).then_inc(S("rel_row"), 1)
            dve.memset(relrow[:, SEQ:REL_W], NEG).then_inc(S("rel_row"), 1)
            dve.wait_ge(S("c_gated"), 1)
            for k in range(8):
                ada(k)
            norm_row2("mem")
            for k in range(8, KT):
                ada(k)
            turn_lo("mem", XTh, XTl, gain=vT[:, V_LN_MEM:V_LN_MEM + KT])
            lo()
            lo()
            mod_fin(0)
            dve.wait_ge(S("mod_ready"), 1)
            for s in range(2):
                lo()
            for s in range(4):
                lo()
                ada(2 * s)
                ada(2 * s + 1)
            for k in range(8, KT):
                ada(k)
            dve.wait_ge(S("turned"), TURN0["x"])
            norm_row2("x")
            mod_fin(1)
            dve.wait_ge(S("mod_ready"), 2)
            turn_lo("x", XTh, XTl, gain=modA[:, 1, :], shift=modA[:, 0, :])
            lo(4 * ZC)
            with dve.Fori(0, 2) as i, st.loop(i, 2, 32, 16):
                for c in range(4):
                    for s in range(4):
                        ada(4 * c + s)
                        if s < 3:
                            lo(4 * ZC)
                        elif c < 3:
                            lo()
                lo()
                dve.wait_ge(S("mod_sum"), i + 3)
                dve.tensor_copy(msum[:, bass.ds(i * KT, KT)], PB[7][:, 0:KT]).then_inc(S("mod_ready"), 1)
            dve.wait_ge(S("mod_ready"), 4)
            link(tt(mtmp[:, :], msum[:, 0:KT], bT[:, 2 * KT:3 * KT], ALU.add))
            tt(gT[:, :], mtmp[:, :], bT[:, 96:112], ALU.mult).then_inc(S("gate_ready"), 1)
            tt(modA[:, 2, :], msum[:, KT:2 * KT], bT[:, 3 * KT:4 * KT], ALU.add).then_inc(S("gate_ready"), 1)
            dve.wait_ge(S("a_turned"), 1)
            dve.tensor_copy(aT[:, :], PB[6][0:GR, 0:SEQ]).then_inc(S("a_out"), 1)
            dve.wait_ge(S("pos_in"), 16)
            link(dve.tensor_copy(posf[:, :], posi[:, :]))
            for r in range(RB):
                for k in range(2):
                    a, t, m = ropes[:, 0, :], ropes[:, 1, :], ropes[:, 2, :]
                    quarter = 0.25 if k == 0 else 0.0
                    link(dve.tensor_scalar(a, invf, posf[:, r:r + 1], None, ALU.mult))
                    link(dve.tensor_scalar(t, a, 1.0 / (2.0 * np.pi), quarter, ALU.mult, ALU.add))
                    link(dve.tensor_scalar(m, t, MAGIC, None, ALU.add))
                    link(dve.tensor_scalar(t, m, -MAGIC, None, ALU.add))
                    for q, part in enumerate(TWO_PI_PARTS):
                        src, dst = ((a, m), (m, a), (a, m))[q]
                        link(dve.scalar_tensor_tensor(dst, t, -part, src, ALU.mult, ALU.add))
                    link(dve.tensor_scalar(a, m, np.pi / 2 if k == 0 else 0.0, None, ALU.add))
                    dve.tensor_scalar(ang[:, r, k, :], a, 3.1415925, -3.1415925, ALU.min, ALU.max).then_inc(S("angle"), 1)
                    if r + k < 2:
                        dve.wait_ge(S("angle"), 2 * r + k + 1)
            for r in range(RB):
                dve.wait_ge(S("log1p"), r + 1)
                link(dve.scalar_tensor_tensor(la[:, r, :], PB[r][:, :], 0.0, kd[:, r, :], ALU.min, ALU.subtract))
                dve.tensor_scalar(la[:, r, :], la[:, r, :], 1.0 / 16.0, None, ALU.mult).then_inc(S("log_a"), 1)
            dve.wait_ge(S("cum"), 2 * RB)
            dve.wait_ge(S("einv_out"), RB)
            for r in range(RB):
                tt(bcs[:, r, :], PB[6 + r][:, :], bcs[:, r, :], ALU.subtract).then_inc(S("left"), 1)
            for r in range(RB):
                q, k = Z[:, r, Z_QG:Z_KG], Z[:, r, Z_KG:Z_VG]
                dve.scalar_tensor_tensor(q, q, GK ** -0.5, eb[:, r, :], ALU.mult, ALU.mult).then_inc(S("decayed"), 1)
                dve.wait_ge(S("edec_out"), r + 1)
                tt(kd[:, r, :], k, kd[:, r, :], ALU.mult).then_inc(S("k_decayed"), 1)
                dve.wait_ge(S("k_decayed"), r + 1)
                tt(k, k, einv[:, r, :], ALU.mult).then_inc(S("decayed"), 1)
            link(dve.memset(attT[:, :, :, :], 0.0))
            for b in range(2):
                dve.wait_ge(S("gla_scored"), b + 1)
                for k in range(2):
                    for r in range(RB):
                        ins = dve.copy_predicated(attT[:, 2 * b + k, r, :], tri.bitcast(U32),
                                                  PB[4 + b][:, SEQ * k + P * r:SEQ * k + P * r + P])
                ins.then_inc(S("att_masked"), 1)
            for m in range(3 * GH):
                h, n = m // 3, m % 3
                dve.wait_ge(S("state_add"), 6 * (h // 2) + 6)
                bank, half = (6 + h // 2, h % 2) if n == 1 else (h, n // 2)
                src = PB[bank][:, GV * half:GV * half + GV]
                if n == 0:
                    dve.tensor_copy(states[:, h, 0, :], src).then_inc(S("stated"), 1)
                else:
                    dve.wait_ge(S("stated"), m)
                    dve.scalar_tensor_tensor(states[:, h, n, :], states[:, h, n - 1, :], decay[:, h, n:n + 1], src,
                                             ALU.mult, ALU.add).then_inc(S("stated"), 1)
            dve.wait_ge(S("gla_root"), 1)
            link(dve.reciprocal(gst[:, 2, :, :], gst[:, 1, :, :]))
            dve.wait_ge(S("r_gated"), RB)
            for h in range(GH):
                for r in range(RB):
                    v, g = Z_VG + GV * h, Z_RG + GV * h
                    link(dve.scalar_tensor_tensor(Z[:, r, v:v + GV], PB[h][:, GV * r:GV * r + GV], gst[:, 2, h, r:r + 1],
                                                  ggla[:, :], ALU.mult, ALU.mult))
                    tt(Z[:, r, v:v + GV], Z[:, r, v:v + GV], Z[:, r, g:g + GV], ALU.mult).then_inc(S("gla_done"), 1)
            norm_inv("cq")
            norm_inv("ckv")
            turn_lo("cq", XTh, XTl, gain=vT[:, V_GQ:V_GQ + 4])
            turn_lo("ckv", XTh, XTl, gain=vT[:, V_GKV:V_GKV + 2], k0=4)
            for _ in range(4):
                lo()
            dve.wait_ge(S("sines"), 2 * RB)
            dve.wait_ge(chunk_out, RB * CHUNK0["uv"])
            for r in range(RB):
                kr = Z[:, r, Z_KR:Z_QG].rearrange("p (h d) -> p h d", h=1)
                for x, n in ((qrow[r][:, :, NOPE:QKD], MH), (kr, 1)):
                    cos = cs[:, r, 0:1, :].broadcast_to([P, n, HALF])
                    sin = cs[:, r, 1:2, :].broadcast_to([P, n, HALF])
                    x1, x2 = x[:, :, 0:HALF], x[:, :, HALF:ROPE]
                    t = [rt[k][:, 0:n, :] for k in range(4)]
                    tt(t[0], x1, cos, ALU.mult)
                    tt(t[1], x2, sin, ALU.mult)
                    tt(t[2], x2, cos, ALU.mult)
                    link(tt(t[3], x1, sin, ALU.mult))
                    tt(x1, t[0], t[1], ALU.subtract).then_inc(S("roped_half"), 1)
                    tt(x2, t[2], t[3], ALU.add).then_inc(S("roped"), 1)
                    dve.wait_ge(S("roped"), 2 * r + (n == 1) + 1)
            for t in range(MH + 3):
                if t < MH:
                    ada(2 * t)
                    ada(2 * t + 1)
                h = t - 1
                if 0 <= h < MH:
                    dve.wait_ge(S("scored"), h + 1)
                    if h >= 2:
                        dve.wait_ge(S("p_turned"), h - 1)
                    tt(prob[:, h % 2, :], PB[6 + h % 2][:, 0:3 * P], mask3, ALU.add).then_inc(S("masked"), 1)
                    dve.wait_ge(S("masked"), h + 1)
                    for r in range(RB):
                        dve.tensor_reduce(mst[:, h % 4, 0, r:r + 1], prob[:, h % 2, P * r:P * (2 * r + 1)], AX.X, ALU.max,
                                          negate=True).then_inc(S("maxed"), 1)
                h = t - 3
                if 0 <= h < MH:
                    dve.wait_ge(S("pv_done"), h + 1)
                    link(dve.reciprocal(mst[:, h % 4, 2, :], mst[:, h % 4, 1, :]))
                    for r in range(RB):
                        dve.tensor_scalar(Z[:, r, Z_QG + VD * h:Z_QG + VD * h + VD], PB[h % 2][:, P * r:P * r + VD],
                                          mst[:, h % 4, 2, r:r + 1], None, ALU.mult).then_inc(S("mla_o"), 1)
            lo()
            mod_fin(4)
            dve.wait_ge(S("mod_ready"), 5)
            turn_lo("o", XTh, XTl)
            for c in range(4):
                for s in range(4):
                    ada(4 * c + s)
                    lo()
                    if c and s == 1:
                        weigh("o", c - 1)
            mod_fin(5)
            add_normed("o")

            def ffn(k, pre, gain, shift, more):
                norm_row2(pre)
                turn_lo(pre, XTh, XTl, gain=gain, shift=shift)
                for n in range(4):
                    for r in range(RB):
                        dve.memset(ROWB[:, r, 512 * n:512 * n + 512], 0.0).then_inc(S("y_added"), 1)
                b0 = RB * FN * k
                y0 = 8 * (FN + 1) * k

                def hidden(j):
                    for r in range(RB):
                        dve.wait_ge(S("silu_out"), j * RB + (b0 + r + 1))
                        if not isinstance(j, int) or j or k:
                            dve.wait_ge(S("h_turned"), j * 2 + b0)
                        tt(HROW[:, r, :], SIL[:, r, :], PB[2 + r][:, :], ALU.mult).then_inc(S("h_made"), 1)

                def hidden_lo(j):
                    for b in range(2):
                        dve.wait_ge(S("hid_hi"), j * 2 + (b0 + b + 1))
                        tt(HTl[:, 2 * b:2 * b + 2, :].rearrange("p t n -> p (t n)"), PB[4 + b][:, :],
                           f32(HTh[:, 2 * b:2 * b + 2, :].rearrange("p t n -> p (t n)")), ALU.subtract)\
                            .then_inc(S("hid_lo"), 1)

                def add(n, j, used):
                    dve.wait_ge(slab_used, used)
                    dve.wait_ge(S("y_added"), j * 8 + (y0 + 2 * n + RB))
                    banks = ((6, 7), (0, 1), (6, 7), (2, 3))[n]
                    for r in range(RB):
                        y = ROWB[:, r, 512 * n:512 * n + 512]
                        tt(y, y, PB[banks[r]][:, :], ALU.add).then_inc(S("y_added"), 1)

                for _ in range(7):
                    lo()
                dve.wait_ge(slab_used, st.lins())
                hidden(0)
                lo()
                hidden_lo(0)
                with dve.Fori(0, FN - 1) as i, st.loop(i, FN - 1, 12, 12):
                    for _ in range(8):
                        lo()
                    dve.wait_ge(slab_used, st.lins(-1))
                    hidden(i + 1)
                    lo()
                    lo()
                    add(0, i, st.lins(-2))
                    lo()
                    add(1, i, st.lins(-2))
                    lo()
                    add(2, i, st.lins(-2))
                    add(3, i, st.lins(-1))
                    hidden_lo(i + 1)
                for n in range(4):
                    if n < 3 or more:
                        lo()
                    last = st.lins(-1) if n < 3 or more else st.lins()
                    add(n, FN - 1, last)
                    if n == 0 and k:
                        dve.wait_ge(S("gain_in"), 48)
                    if n:
                        weigh(("y1", "y2")[k], n - 1)
                add_normed(("y1", "y2")[k])

            ffn(0, "f1", modA[:, 3, :], modA[:, 2, :], True)
            norm_row2("z2")
            turn_lo("z2", XTh, XTl, gain=vT[:, V_LN_MIX:V_LN_MIX + KT])
            for _, width in Z2_PARTS:
                with dve.Fori(0, Z2N // 2) as i, st.loop(i, Z2N // 2, 8, 8):
                    for c in range(2):
                        for s in range(3):
                            lo(4 * width)
                        lo()
            dve.wait_ge(S("pe_turned"), 1)
            dve.tensor_copy(peT[:, :, :].rearrange("p k l -> p (k l)"), PB[6][:, 0:2 * CS]).then_inc(S("pe_out"), 1)
            dve.wait_ge(S("pe_out"), 1)
            for b in range(4):
                dve.wait_ge(S("raw_turned"), b + 1)
                k, g, n = b // 2, 2 * (b % 2), SEQ // CS

                def tokens(ap):
                    return ap.rearrange("p (m l) -> p m l", l=CS)

                tt(tokens(rawT[0:HD, k, g:g + 2, :].rearrange("p g n -> p (g n)")), tokens(PB[b][0:HD, :]),
                   peT[0:HD, k:k + 1, :].broadcast_to([HD, 2 * n, CS]), ALU.add)
                for q in range(2):
                    ins = tt(tokens(rawT[HD:2 * HD, k, g + q, 0:SEQ - CS]), tokens(PB[b][HD:2 * HD, SEQ * q + CS:SEQ * q + SEQ]),
                             peT[HD:2 * HD, k:k + 1, :].broadcast_to([HD, n - 1, CS]), ALU.add)
                ins.then_inc(S("raw_out"), 1)
            dve.wait_ge(S("gates_out"), RB)
            dve.wait_ge(S("rel_in"), 16)
            for t in range(NH * RB + 3):
                u = t - 2
                if 0 <= u < NH * RB:
                    b, n_c = u % 2, (NCMP0, NCMP)[u % 2]
                    dve.wait_ge(S("n_turned"), u + 1)
                    if u >= 2:
                        dve.wait_ge(S("n_pv"), u - 1)
                    dve.tensor_copy(pcT[0:n_c, b, :], PB[2 + b][0:n_c, P:2 * P]).then_inc(S("n_cT"), 1)
                u = t
                if u < NH * RB:
                    h, r = u // 2, u % 2
                    nk, n_c = P * (r + 1), (NCMP0, NCMP)[r]
                    dve.wait_ge(S("n_scored"), u + 1)
                    if u >= 2:
                        dve.wait_ge(S("n_turned"), u - 1)
                    b = u % 2
                    off = P if r == 0 else 0
                    s3 = NSPROB(b)[:, 0:2 * nk].rearrange("p (c n) -> p c n", c=2)
                    for c in range(2):
                        tt(s3[:, c, :], PB[b][:, nk * c:nk * c + nk], REL[:, h, off:off + nk], ALU.add)
                    c0 = (P - 1 + CL if r == 0 else CL - 1)
                    tt(pc[:, b, 0:n_c], PB[2 + b][:, 0:n_c], REL[:, h, c0:c0 + CS * (n_c - 1) + 1:CS], ALU.add)\
                        .then_inc(S("n_added"), 1)
                    dve.wait_ge(S("n_added"), u + 1)
                    dve.tensor_reduce(nst[:, u % 4, 2, 0:2], s3, AX.X, ALU.max)
                    link(dve.tensor_reduce(nst[:, u % 4, 2, 2:3], pc[:, b, 0:n_c], AX.X, ALU.max))
                    dve.tensor_scalar(nst[:, u % 4, 0, :], nst[:, u % 4, 2, :], -1e29, -1.0, ALU.max, ALU.mult)\
                        .then_inc(S("n_maxed"), 1)
                u = t - 3
                if 0 <= u < NH * RB:
                    h, r, b = u // 2, u % 2, u % 2
                    link(dve.tensor_scalar(nst[:, u % 4, 1, :], nst[:, u % 4, 1, :], 1.0, None, ALU.max))
                    link(dve.reciprocal(nst[:, u % 4, 1, :], nst[:, u % 4, 1, :]))
                    gl = Z2[:, r, Z2_GL + 3 * h:Z2_GL + 3 * h + 3]
                    wt = nwt[:, u % 4, :]
                    link(tt(wt, nst[:, u % 4, 1, :], gl, ALU.mult))
                    dve.wait_ge(S("n_pv"), u + 1)
                    o = Z2[:, r, HD * h:HD * h + HD]
                    po = PB[6 + b]
                    for c, q in enumerate((1, 2, 0)):
                        src = po[:, HD * c:HD * c + HD]
                        if c == 0:
                            ins = dve.tensor_scalar(o, src, nwt[:, u % 4, q:q + 1], None, ALU.mult)
                        else:
                            ins = dve.scalar_tensor_tensor(o, src, nwt[:, u % 4, q:q + 1], o, ALU.mult, ALU.add)
                        ins.then_inc(S("nsa_o"), 1)
                        if c < 2:
                            dve.wait_ge(S("nsa_o"), 3 * u + c + 1)
            for g in range(PG):
                dve.wait_ge(S("pool_hi"), g + 1)
                sl = (slice(None), slice(2 * g, 2 * g + 2), slice(None))
                tt(XTl[sl].rearrange("p t n -> p (t n)"), PB[g][:, :], f32(XTh[sl].rearrange("p t n -> p (t n)")),
                   ALU.subtract).then_inc(S("pool_lo"), 1)
            lo()
            for g in range(PG):
                dve.wait_ge(S("pool_lin"), g + 1) if g < PG - 1 else dve.wait_ge(slab_used, st.lins(-1))
                for q in range(2):
                    k = V_PS + 2 * g + q
                    ins = dve.tensor_scalar(TMPP[:, g % 2, SEQ * q:SEQ * q + SEQ], PB[4 + g][:, SEQ * q:SEQ * q + SEQ],
                                            vT[:, k:k + 1], None, ALU.mult)
                ins.then_inc(S("pool_scaled"), 1)
                dve.wait_ge(S("pool_hi"), PG + g + 1)
                sl = (slice(None), slice(8 + 2 * g, 10 + 2 * g), slice(None))
                tt(XTl[sl].rearrange("p t n -> p (t n)"), TMPP[:, g % 2, :], f32(XTh[sl].rearrange("p t n -> p (t n)")),
                   ALU.subtract).then_inc(S("pool_lo"), 1)
            turn_lo("att", XTh, XTl)
            dve.wait_ge(S("merge_gated"), RB)
            for c in range(4):
                for s in range(4):
                    lo()
                dve.wait_ge(slab_used, st.lins(-1))
                cols = slice(512 * c, 512 * c + 512)
                for r in range(RB):
                    ga, gp = (Z2[:, r, Z2_M + D * k + 512 * c:Z2_M + D * k + 512 * c + 512] for k in range(2))
                    tt(ga, ga, PB[r][:, :], ALU.mult).then_inc(S("merged"), 1)
                    tt(gp, gp, PB[2 + r][:, :], ALU.mult).then_inc(S("merged"), 1)
                    dve.wait_ge(S("merged"), 6 * c + 3 * r + 2)
                    tt(Z2[:, r, cols], ga, gp, ALU.add).then_inc(S("merged"), 1)
            turn_lo("y", XTh, XTl)
            for c in range(4):
                for s in range(4):
                    lo()
                    if c and s == 1:
                        dve.wait_ge(S("gain_in"), 16)
                        weigh("mix", c - 1)
            add_normed("mix")
            norm_row2("xq")
            turn_lo("xq", XTh, XTl, gain=vT[:, V_LN_X:V_LN_X + KT])
            for _ in range(4):
                lo()
            for t in range(XH + 2):
                h = t
                if h < XH:
                    dve.wait_ge(S("x_scored"), h + 1)
                    if h >= 2:
                        dve.wait_ge(S("x_exped"), RB * (h - 1))
                    dve.tensor_reduce(mst[:, h % 4, 0, :], PB[h % 2][:, :].rearrange("p (r n) -> p r n", r=RB), AX.X, ALU.max,
                                      negate=True).then_inc(S("x_maxed"), 1)
                h = t - 2
                if 0 <= h < XH:
                    dve.wait_ge(S("x_pv"), h + 1)
                    link(dve.reciprocal(mst[:, h % 4, 2, :], mst[:, h % 4, 1, :]))
                    for r in range(RB):
                        dve.tensor_scalar(SIL[:, r, XD * h:XD * h + XD], PB[2 + h % 2][:, P * r:P * r + XD],
                                          mst[:, h % 4, 2, r:r + 1], None, ALU.mult).then_inc(S("xatt_o"), 1)
            turn_lo("xo", XTh, XTl, k0=12)
            for c in range(4):
                lo()
                if c:
                    dve.wait_ge(S("gain_in"), 32)
                    weigh("xo", c - 1)
            add_normed("xo")
            ffn(1, "f2", vT[:, V_LN_FFN:V_LN_FFN + KT], None, False)


def kernel(**inputs):
    import concourse.bacc as bacc
    from concourse.bass_utils import run_bass_kernel_spmd

    nc = bacc.Bacc("TRN2", target_bir_lowering=False, num_devices=1, dynamic_dma_scratch_size=4096)
    const, band, onehot = shape_constants()
    host = {name: np.ascontiguousarray(a) for name, a in inputs.items()}
    drop = ("w_ada", "b_ada", "g_pre_mix", "g_post_mix", "w_in", "g_q", "w_uq", "g_kv", "w_uk", "w_uv", "w_gate_up", "b_gate",
            "g_gla", "w_out", "g_pre_ffn", "g_post_ffn", "w_ffn_gate", "w_ffn_up", "w_ffn_down", "x", "c", "positions")
    for name, a in host.items():
        if name in drop or (name.endswith("_2") and name != "rel_bias_2"):
            host[name] = a[0]
    host.update(const=const, band=band, onehot=onehot)
    A = {name: nc.dram_tensor(f"in_{name}", a.shape, mybir.dt.from_np(a.dtype), kind="ExternalInput").ap()
         for name, a in host.items()}
    out = nc.dram_tensor("out_x", (SEQ, D), F32, kind="ExternalOutput").ap()
    build(nc, A, out)
    r = run_bass_kernel_spmd(nc, [{f"in_{name}": a for name, a in host.items()}], core_ids=[0])
    return r.results[0]["out_x"].reshape(1, SEQ, D)
```

```python
from contextlib import ExitStack, contextmanager

import numpy as np

import concourse.bass as bass
from concourse import mybir

F32 = mybir.dt.float32
F32R = mybir.dt.float32r
I32 = mybir.dt.int32
U32 = mybir.dt.uint32
ACT = mybir.ActivationFunctionType
ALU = mybir.AluOpType
AX = mybir.AxisListType

P = 128
SEQ, D, RB = 256, 2048, 2
KT = D // P
EPS = 1e-6
NEG = -1e30
MH, QR, KVR, NOPE, ROPE, VD = 8, 512, 256, 128, 64, 128
QKD = NOPE + ROPE
HALF = ROPE // 2
GH, GK, GV, CH = 4, 128, 256, 64
GKEY, GVAL, GR = GH * GK, GH * GV, 16
NCH = SEQ // CH
Z_CQ, Z_CKV, Z_KR = 0, QR, QR + KVR
Z_QG = Z_KR + ROPE
Z_KG = Z_QG + GKEY
Z_VG = Z_KG + GKEY
Z_AG = Z_VG + GVAL
Z_RG = Z_AG + GR
ZW = Z_RG + GVAL
ZC, ZN = ZW // 8, 8
NH, NG, HD = 16, 4, 64
HPG = NH // NG
KVW = NG * HD
CL, CS, CHID = 32, 16, 128
NCMP = (SEQ - CL) // CS + 1
NCMP0 = (P - CL) // CS + 1
POOLW = (2, 4, 8, 16)
PG, PGW = 4, 256
Z2_KV = NH * HD
Z2_GL = Z2_KV + 6 * KVW
Z2_U = Z2_GL + 3 * NH
Z2_M = Z2_U + PG * PGW
Z2W = Z2_M + 2 * D
Z2N = 8
Z2_PARTS = [(0, Z2_M // Z2N), (Z2_M, 2 * D // Z2N)]
XH, XD = 4, 128
DFF = 5632
FN = DFF // 512
FN_ADA = KT // 4
BUCKETS, MAXD = 32, 2048
REL_W = SEQ + P
TWO_PI_PARTS = (6.28125, 0.0019350051879882812, 3.019916050561733e-07)
MAGIC = 12582912.0

C_ID, C_TRI, C_BLK, C_ONE, C_MASK, C_INVF = 0, 128, 256, 384, 512, 896
CONST_W = C_INVF + HALF


def shape_constants():
    i = np.arange(P)
    c = np.zeros((P, CONST_W), np.float32)
    c[:, C_ID:C_ID + P] = np.eye(P)
    same = (i[:, None] // CH) == (i[None, :] // CH)
    c[:, C_TRI:C_TRI + P] = same & (i[:, None] <= i[None, :])
    c[:, C_BLK:C_BLK + P] = same
    c[:, C_ONE:C_ONE + P] = 1.0
    causal = np.where(i[None, :] <= i[:, None], 0.0, NEG)
    c[:, C_MASK:C_MASK + P] = causal
    c[:, C_MASK + 2 * P:C_MASK + 3 * P] = causal
    c[:, C_INVF:] = (1.0 / (np.float32(10000.0) ** (np.arange(0, ROPE, 2, dtype=np.float32) / np.float32(ROPE))))
    t = np.arange(SEQ)
    band = np.zeros((P, PG, 3 * P), np.float32)
    for g, w in enumerate(POOLW):
        m = ((t[:, None] - t[None, :] >= 0) & (t[:, None] - t[None, :] < w)) / np.minimum(t + 1, w)[:, None]
        m = (m - np.eye(SEQ)).T
        band[:, g, :SEQ] = m[:P]
        band[:, g, SEQ:] = m[P:, P:]
    n = np.maximum(SEQ - 1 - np.arange(SEQ), 0)
    exact = BUCKETS // 2
    big = exact + (np.log(np.maximum(n, 1) / exact) / np.log(MAXD / exact) * (BUCKETS - exact)).astype(np.int64)
    bucket = np.where(n < exact, n, np.minimum(big, BUCKETS - 1))
    onehot = (np.arange(BUCKETS)[:, None] == bucket[None, :]).astype(np.float32)
    return c, band.reshape(P, PG * 3 * P), onehot


class Slabs:

    def __init__(self):
        self.raw = self.lin = 0
        self.i = None
        self.i0 = self.praw = self.plin = 0

    @contextmanager
    def loop(self, i, count, praw, plin, i0=0):
        assert praw % 4 == 0 and plin % 2 == 0
        r, n = self.raw, self.lin
        self.i, self.i0, self.praw, self.plin = i, i0, praw, plin
        yield
        assert self.raw == r + praw and self.lin == n + plin, (self.raw - r, self.lin - n)
        self.i = None
        self.praw = self.plin = 0
        self.raw += praw * (count - 1)
        self.lin += plin * (count - 1)

    def plus(self, value, per):
        return value if self.i is None else self.i * per + (value - self.i0 * per)

    def raws(self, ahead=0):
        return self.plus(self.raw + ahead, self.praw)

    def lins(self, ahead=0):
        return self.plus(self.lin + ahead, self.plin)

    def landed(self):
        return self.plus(16 * (self.raw // 4 + 1), 4 * self.praw)

    def next(self, linear=True):
        self.raw += 1
        self.lin += linear


class Chain:

    def __init__(self, eng, sem):
        self.eng, self.sem, self.n = eng, sem, 0

    def __call__(self, ins):
        self.n += 1
        ins.then_inc(self.sem, 1)
        self.eng.wait_ge(self.sem, self.n)


TURNS = [("mem", 8, 2), ("x", 8, 1), ("cq", 2, 2), ("ckv", 1, 2), ("o", 8, 0), ("f1", 8, 1), ("z2", 8, 2),
         ("att", 4, 0), ("y", 8, 0), ("xq", 8, 2), ("xo", 2, 0), ("f2", 8, 2)]
TURN_N = {name: n for name, n, _ in TURNS}
TURN0 = {name: sum(m[1] for m in TURNS[:k]) for k, (name, _, _) in enumerate(TURNS)}
GAIN0 = {name: sum(m[1] for m in TURNS[:k] if m[2] == 1) for k, (name, _, _) in enumerate(TURNS)}
HI0 = {name: sum(m[1] * (2 if m[2] == 2 else 1) for m in TURNS[:k]) for k, (name, _, _) in enumerate(TURNS)}
GAINED = {name for name, _, kind in TURNS if kind == 1}
NORMS = ["mem", "x", "cq", "ckv", "o", "f1", "y1", "z2", "mix", "xq", "xo", "f2", "y2"]
POST = ["o", "y1", "mix", "xo", "y2"]
CHUNKS = [("xkv", 2), ("zin", ZN), ("uq", 3), ("uv", 2), ("wout", 4), ("zin2", 2 * Z2N), ("mix", 4), ("xq", 1), ("xo", 4)]
CHUNK0 = {name: sum(n for _, n in CHUNKS[:k]) for k, (name, _) in enumerate(CHUNKS)}


def added(name, chunk=3, blocks=RB):
    return 4 * RB * POST.index(name) + RB * chunk + blocks


def build(nc, A, out):
    ctx = ExitStack()
    with ctx:
        named = {}

        def S(name):
            if name not in named:
                named[name] = ctx.enter_context(nc.semaphore(name))
            return named[name]

        base = [-(-nc.sbuf_base // 64) * 64]

        def sb(name, shape, dt=F32):
            t = nc.alloc_sbuf_tensor_at(name, shape, dt, offset=base[0])
            base[0] += -(-4 * int(np.prod(shape[1:])) // 32) * 32
            return t

        def at(name, shape, offset, dt=F32):
            return nc.alloc_sbuf_tensor_at(name, shape, dt, offset=offset)

        raw = sb("raw", [P, 4, 2048])
        wh = sb("wh", [P, 2, 2048], F32R)
        wl = sb("wl", [P, 2, 2048], F32R)
        X = sb("X", [P, RB, D])
        xt0 = base[0]
        XTh = sb("XTh", [P, KT, SEQ], F32R)
        xt1 = base[0]
        XTl = sb("XTl", [P, KT, SEQ], F32R)
        xkT = sb("xkT", [P, XH, SEQ])
        xv = sb("xv", [P, RB, XH * XD])
        zb = base[0]
        ZB = sb("ZB", [P, RB * Z2W])
        misc = base[0]
        MISC = sb("MISC", [P, 5120])
        CON = sb("CON", [P, CONST_W])
        vT = sb("vT", [P, P])
        bT = sb("bT", [P, P])
        modA = sb("modA", [P, 4, KT])
        gT = sb("gT", [P, KT])
        cT = sb("cT", [P, KT])
        nstat = sb("nstat", [P, len(NORMS), 3, RB])
        psq = sb("psq", [P, len(POST), RB, 4])
        eps = sb("eps", [P, 1])
        one = sb("one", [P, 1])
        mtmp = sb("mtmp", [P, KT])
        nwt = sb("nwt", [P, 8, 3])
        ang = sb("ang", [P, RB, 2, HALF])
        cs = sb("cs", [P, RB, 2, HALF])
        posi = sb("posi", [P, RB], I32)
        posf = sb("posf", [P, RB])
        assert base[0] <= nc.sbuf_usable_end, (base[0], nc.sbuf_usable_end)

        Z = at("Z", [P, RB, ZW], zb)
        Z2 = at("Z2", [P, RB, Z2W], zb)
        ROWB = at("ROWB", [P, RB, D], zb)
        MEM = at("MEM", [P, RB, D], zb + 4 * 4096)
        XS = at("XS", [P, KT, SEQ], zb + 4 * 4096)
        HROW = at("HROW", [P, RB, 512], zb + 4 * 4096)
        SIL = at("SIL", [P, RB, 512], zb + 4 * 5120)
        JUNK = at("JUNK", [P, D], zb + 4 * 8192)
        TMP = at("TMP", [P, 2, 512], zb + 4 * 10240)
        HTh = at("HTh", [P, 4, SEQ], zb + 4 * 11264, F32R)
        HTl = at("HTl", [P, 4, SEQ], zb + 4 * 12288, F32R)
        ACC = at("ACC", [P, D], zb + 4 * 13408)
        wgu = at("wgu", [GR, GKEY], zb + 4 * 11264)
        bgr = at("bgr", [1, GKEY], zb + 4 * 11776)
        aT = at("aT", [GR, SEQ], zb + 4 * 12288)
        VROW = at("VROW", [P, P], zb + 4 * 12928)
        BROW = at("BROW", [P, P], zb + 4 * 13056)
        G = at("G", [P, D], misc)
        assert xt1 - xt0 == 4 * 4096 and zb + 4 * 15360 <= misc

        PB = [ctx.enter_context(nc.psum_tensor(f"bank{b}", [P, 512], F32)) for b in range(8)]

        ident = CON[:, C_ID:C_ID + P]
        tri = CON[:, C_TRI:C_TRI + P]
        blk = CON[:, C_BLK:C_BLK + P]
        ones = CON[:, C_ONE:C_ONE + P]
        mask3 = CON[:, C_MASK:C_MASK + 3 * P]
        invf = CON[:, C_INVF:C_INVF + HALF]
        V_PRE_MIX, V_PRE_FFN, V_LN_MIX, V_LN_X, V_LN_MEM, V_LN_FFN, V_C, V_GQ, V_GKV, V_PS = (
            0, 16, 32, 48, 64, 80, 96, 112, 116, 118)

        def f32(ap):
            return ap.bitcast(F32)

        def scr(name, off, shape):
            return at(name, shape, xt0 + 4 * off)

        la = scr("la", 0, [P, RB, GKEY])
        eb = scr("eb", 1024, [P, RB, GKEY])
        einv = scr("einv", 2048, [P, RB, GKEY])
        kd = scr("kd", 3072, [P, RB, GKEY])
        bcs = scr("bcs", 4096, [P, RB, GKEY])
        qdT = scr("qdT", 5120, [P, GH, SEQ])
        kiT = scr("kiT", 6144, [P, GH, SEQ])
        attT = scr("attT", 7168, [P, GH, RB, P])
        states = at("states", [P, GH, 3, GV], misc + 4 * 2048)
        decay = sb("decay", [P, GH, NCH])
        ggla = at("ggla", [P, GV], zb + 4 * 12544)
        gst = sb("gst", [P, 3, GH, RB])
        qrow = [at(f"qrow{r}", [P, MH, QKD], (xt0, xt1)[r] + 4 * 1536) for r in range(RB)]
        kTn = [at(f"kTn{r}", [P, 4, SEQ], (xt0, xt1)[r] + 4 * 3072) for r in range(2)]
        vrow = at("vrow", [P, RB, MH * VD], misc + 4 * 2048)
        qTs = at("qTs", [P, 2, 512], misc + 4 * 4096)
        krT = at("krT", [ROPE, SEQ], zb + 4 * 11264)
        prob = at("prob", [P, 2, 384], zb + 4 * 11520)
        probT = at("probT", [P, 2, 384], zb + 4 * 12288)
        rt = [at(f"rt{k}", [P, MH, HALF], zb + 4 * (8192 + 256 * k)) for k in range(4)]
        ropes = at("ropes", [P, 3, HALF], zb + 4 * 12800)
        mst = sb("mst", [P, 4, 3, RB])
        QT = at("QT", [HD, NH, SEQ], xt0)
        KT2 = at("KT2", [HD, NG, 2, SEQ], xt0 + 4 * 4096)
        rawT = at("rawT", [2 * HD, 2, NG, SEQ], xt0 + 4 * 6144)
        REL = at("REL", [P, NH, SEQ], misc)
        pT = at("pT", [P, 2, 512], misc + 4 * 4096)
        w1s = at("w1s", [2 * HD, 2, CS, CHID], xt0)
        w2s = at("w2s", [CHID, 2, HD], misc + 4 * 4096)
        peT = at("peT", [2 * HD, 2, CS], misc + 4 * 4224)
        perow = at("perow", [2 * CS, 2 * HD], misc + 4 * 4288)
        hidT = at("hidT", [CHID, 2, NG * NCMP], misc + 4 * 4480)
        onehot = at("onehot", [BUCKETS, SEQ], zb + 4 * 11264)
        rb16 = at("rb16", [NH, BUCKETS], zb + 4 * 11520)
        rbT = at("rbT", [BUCKETS, NH], zb + 4 * 11552)
        relrow = sb("relrow", [NH, REL_W])
        kcT = sb("kcT", [HD, NG, NCMP])
        vc = sb("vc", [NCMP, NG, HD])
        pcT = sb("pcT", [NCMP, 2, P])
        pc = sb("pc", [P, 4, 16])
        nst = sb("nst", [P, 8, 3, 3])
        nprob = sb("nprob", [P, 2, 512])
        band = at("band", [P, PG, 3 * P], misc)
        assert base[0] <= nc.sbuf_usable_end, (base[0], nc.sbuf_usable_end)

        def NSPROB(k):
            return Z2[:, k, Z2_KV:Z2_KV + 512] if k < 2 else nprob[:, k - 2, :]

        xqT = at("xqT", [P, XH, SEQ], xt0)
        TMPP = at("TMPP", [P, 2, 512], misc + 4 * 1536)
        xp = at("xp", [P, 2, 512], xt0 + 4 * 1024)
        xpT = at("xpT", [P, 2, 512], xt0 + 4 * 2048)

        rel_d = nc.dram_tensor("rel_scratch", [NH, P, REL_W], F32, kind="Internal").ap()

        def kview(w, rows):
            return w.rearrange("(t p) n -> p t n", p=P)

        W = {k: kview(A[k], None) for k in (
            "w_ada", "w_in", "w_uq", "w_uk", "w_uv", "w_out", "w_ffn_gate", "w_ffn_up", "w_ffn_down", "w_in_2",
            "w_br_attn_2", "w_br_pool_2", "w_mix_out_2", "w_xq_2", "w_xkv_2", "w_xo_2", "w_gate_2", "w_up_2",
            "w_down_2")}
        wpool = A["w_pool_2"].rearrange("g (t p) n -> p g t n", p=P)

        block = ctx.enter_context(nc.Block())
        slab_done, hi_made, slab_used, chunk_out = S("slab_done"), S("hi_made"), S("slab_used"), S("chunk_out")
        landed = [S(f"slab_landed{k}") for k in range(4)]

        @block.sync
        def _(sp):
            st = Slabs()

            def slab(src, parts, linear=True):
                r = st.raw
                if r >= 4:
                    sp.wait_ge(slab_done, st.raws(-3))
                n = int(np.prod(parts))
                dst = raw[:, r % 4, 0:n]
                if len(parts) == 2:
                    dst = dst.rearrange("p (t n) -> p t n", t=parts[0])
                if len(parts) == 3:
                    dst = dst.rearrange("p (g t n) -> p g t n", g=parts[0], t=parts[1])
                sp.dma_start(dst, src).then_inc(landed[r % 4], 16)
                st.next(linear)

            def ada(v, k):
                slab(W["w_ada"][:, k, v * D:(v + 1) * D], (D,), False)

            def cols(w, s, c0, width):
                slab(W[w][:, 4 * s:4 * s + 4, c0:c0 + width], (4, width))

            def load(name, dst, src, **how):
                sp.dma_start(dst, src, **how).then_inc(S(name), 16)

            load("mem_in", MEM[:, :, :], A["mem_2"].rearrange("(r p) n -> p r n", p=P))
            load("con_in", CON[:, :], A["const"])
            at_row = 0
            for name, n in (("g_pre_mix", 16), ("g_pre_ffn", 16), ("ln_mix_pre_2", 16), ("ln_x_pre_2", 16),
                            ("ln_mem_2", 16), ("ln_ffn_pre_2", 16), ("c", 16), ("g_q", 4), ("g_kv", 2),
                            ("pool_scale_2", 8)):
                load("vec_in", VROW[at_row:at_row + n, :], A[name].rearrange("(t p) -> t p", p=P))
                at_row += n
            load("vec_in", BROW[0:96, :], A["b_ada"].rearrange("(t p) -> t p", p=P))
            load("vec_in", BROW[96:112, :], A["g_post_mix"].rearrange("(t p) -> t p", p=P))
            load("vec_in", BROW[112:128, :], A["g_post_ffn"].rearrange("(t p) -> t p", p=P))
            load("pos_in", posi[:, :], A["positions"].rearrange("(r p) -> p r", p=P), allow_slow_non_contiguous=True)
            load("rel_bias_in", rb16[:, :], A["rel_bias_2"])
            load("rel_bias_in", onehot[:, :], A["onehot"])
            load("x_in", X[:, :, :], A["x"].rearrange("(r p) n -> p r n", p=P))
            for k in range(8):
                ada(0, k)
            for c in range(2):
                for s in range(4):
                    cols("w_xkv_2", s, 512 * c, 512)
                    for k in range(8 + 2 * s, 10 + 2 * s) if c == 0 else range(3 * s, 3 * s + 3):
                        ada(c, k)
            for k in range(12, KT):
                ada(1, k)
            with sp.Fori(0, 2) as i, st.loop(i, 2, 24, 16):
                for c in range(4):
                    for s in range(4):
                        slab(W["w_in"][:, 4 * s:4 * s + 4, bass.ds(i * (4 * ZC) + c * ZC, ZC)], (4, ZC))
                        if s % 2:
                            slab(W["w_ada"][:, bass.ds(i * 8 + (2 * c + s // 2), 1), 2 * D:3 * D], (1, D), False)
            cols("w_uq", 0, 0, 512)
            load("gla_in", wgu[:, :], A["w_gate_up"])
            load("gla_in", bgr[:, :], A["b_gate"].rearrange("(a n) -> a n", a=1))
            load("gla_in", ggla[:, :], A["g_gla"].partition_broadcast(P))
            sp.wait_ge(S("rel_row"), 2)
            load("rel_out", rel_d, relrow[:, :].unsqueeze(1).broadcast_to([NH, P, REL_W]))
            for k in range(KT):
                ada(3, k)
            for c in (1, 2):
                cols("w_uq", 0, 512 * c, 512)
            slab(W["w_uk"], (2, 1024))
            slab(W["w_uv"], (2, 1024))
            for c in range(4):
                for s in range(4):
                    cols("w_out", s, 512 * c, 512)
                    ada(4, 4 * c + s)

            def ffn(gate, up, down, extra):
                def ada_row(q):
                    if extra and st.i is not None and st.praw == 16:
                        slab(W["w_ada"][:, bass.ds(st.i * 4 + q, 1), 5 * D:6 * D], (1, D), False)

                def part(w, j):
                    for s in range(4):
                        src = bass.ds(j * 512, 512) if st.i is not None else slice(j * 512, j * 512 + 512)
                        slab(W[w][:, 4 * s:4 * s + 4, src], (4, 512))

                def part_down(j):
                    for n in range(4):
                        src = bass.ds(j * 4, 4) if st.i is not None else slice(j * 4, j * 4 + 4)
                        slab(W[down][:, src, 512 * n:512 * n + 512], (4, 512))
                        if n % 2:
                            ada_row(2 + n // 2)

                part(gate, 0)
                part(up, 0)
                for first, last, per in ((0, FN_ADA, 16), (FN_ADA, FN - 1, 12)) if extra else ((0, FN - 1, 12),):
                    with sp.Fori(first, last) as i, st.loop(i, last - first, per, 12, first):
                        part(gate, i + 1)
                        ada_row(0)
                        part(up, i + 1)
                        ada_row(1)
                        part_down(i)
                part_down(FN - 1)

            ffn("w_ffn_gate", "w_ffn_up", "w_ffn_down", True)
            for c0, width in Z2_PARTS:
                with sp.Fori(0, Z2N // 2) as i, st.loop(i, Z2N // 2, 8, 8):
                    for c in range(2):
                        for s in range(4):
                            slab(W["w_in_2"][:, 4 * s:4 * s + 4, bass.ds(i * (2 * width) + (c0 + c * width), width)], (4, width))
            slab(wpool, (4, 2, 256))
            cols("w_br_attn_2", 0, 0, 512)
            sp.wait_ge(S("x_added"), added("y1"))
            sp.wait_ge(S("rel_out"), 16)
            load("rel_in", REL[:, :, :], bass.AP(rel_d.tensor, P - 1, [[REL_W - 1, P], [P * REL_W, NH], [1, SEQ]]))
            for k in range(2):
                load("cmp_in", w2s[:, k, :], A["cmp_w2_2"][k])
                load("cmp_in", perow[CS * k:CS * k + CS, :].rearrange("l (h d) -> l h d", h=2),
                     A["cmp_pe_2"][k].rearrange("(h l) d -> l h d", h=2))
            sp.wait_ge(chunk_out, RB * CHUNK0["mix"])
            for k in range(2):
                w1 = A["cmp_w1_2"][k].rearrange("(h l d) n -> h d l n", h=2, d=HD)
                for half in range(2):
                    load(f"w1_in{k}", w1s[HD * half:HD * half + HD, k, :, :], w1[half])
            sp.wait_ge(S("nsa_o"), 3 * NH * RB)
            load("band_in", band[:, :, :], A["band"].rearrange("p (g n) -> p g n", g=PG))
            for c in range(4):
                for w in ("w_br_attn_2", "w_br_pool_2"):
                    for s in range(2):
                        if (c, w, s) != (0, "w_br_attn_2", 0):
                            cols(w, s, 512 * c, 512)
            sp.wait_ge(S("pool_lo"), 2 * PG)
            load("gain_in", G[:, :], A["ln_mix_post_2"].partition_broadcast(P))
            for c in range(4):
                for s in range(4):
                    cols("w_mix_out_2", s, 512 * c, 512)
            for s in range(4):
                cols("w_xq_2", s, 0, 512)
            sp.wait_ge(S("x_added"), added("mix"))
            load("gain_in", G[:, :], A["ln_x_post_2"].partition_broadcast(P))
            for c in range(4):
                cols("w_xo_2", 0, 512 * c, 512)
            ffn("w_gate_2", "w_up_2", "w_down_2", False)
            sp.wait_ge(S("x_added"), added("xo"))
            load("gain_in", G[:, :], A["ln_ffn_post_2"].partition_broadcast(P))
            rows = out.rearrange("(r p) n -> p r n", p=P)
            for c in range(4):
                sp.wait_ge(S("x_added"), added("y2", c))
                load("stored", rows[:, :, 512 * c:512 * c + 512], X[:, :, 512 * c:512 * c + 512])
            sp.wait_ge(S("stored"), 16 * 4)
        @block.scalar
        def _(act):
            st = Slabs()

            def f(out_, in_, func, name, **kw):
                act.activation(out_, in_, func, **kw).then_inc(S(name), 1)

            def hi(width=2048):
                act.wait_ge(landed[st.raw % 4], st.landed())
                if st.lin >= 2:
                    act.wait_ge(slab_used, st.lins(-1))
                act.activation(wh[:, st.lin % 2, 0:width], raw[:, st.raw % 4, 0:width], ACT.Copy).then_inc(hi_made, 1)
                st.next()

            def skip(n=1):
                for _ in range(n):
                    st.next(False)

            def norm_stats(name, src, n, ready=None):
                j = NORMS.index(name)
                for r in range(RB):
                    if ready is not None:
                        act.wait_ge(S("x_added"), added(ready, blocks=r + 1))
                    act.wait_ge(S("squared"), RB * j + r) if j + r else None
                    f(JUNK[:, 0:n], src(r), ACT.Square, "squared", accum_out=nstat[:, j, 0, r:r + 1])
                act.wait_ge(S("squared"), RB * j + RB)
                f(nstat[:, j, 1, :], nstat[:, j, 0, :], ACT.Sqrt, "rooted", scale=1.0 / n, bias=eps[:, 0:1])

            def post_square(name, c, ready=None):
                m = 4 * RB * POST.index(name) + RB * c
                for r in range(RB):
                    ready(r)
                    if m + r >= 4:
                        act.wait_ge(S("part_sq"), m + r - 3)
                    f(JUNK[:, 512 * ((m + r) % 4):512 * ((m + r) % 4) + 512], ROWB[:, r, 512 * c:512 * c + 512], ACT.Square,
                      "part_sq", accum_out=psq[:, POST.index(name), r, c:c + 1])

            def post_root(name):
                j = NORMS.index(name)
                act.wait_ge(S("squared"), RB * j + RB)
                f(nstat[:, j, 1, :], nstat[:, j, 0, :], ACT.Sqrt, "rooted", scale=1.0 / D, bias=eps[:, 0:1])

            def norm_rows(name, src, dst, blocks=1):
                j = NORMS.index(name)
                act.wait_ge(S("rooted_inv"), j + 1)
                for r in range(blocks):
                    f(dst(r), src(r), ACT.Copy, "normed", scale=nstat[:, j, 2, r:r + 1])

            def turn_hi(name, dst, k0=0, gain=None, between=None):
                for b in range(TURN_N[name]):
                    g = TURN0[name] + b
                    if between and b in (4, 6):
                        between()
                    if gain is not None:
                        act.wait_ge(S("turned"), g + 1)
                        for k in range(2):
                            kt = 2 * b + k
                            f(dst[:, k0 + kt, :], PB[4 + g % 2][:, SEQ * k:SEQ * k + SEQ], ACT.Copy, "turn_hi",
                              scale=gain[:, kt:kt + 1])
                        continue
                    if name in GAINED:
                        act.wait_ge(S("gained"), GAIN0[name] + b + 1)
                        src = TMP[:, g % 2, :] if name != "x" else XS[:, 2 * b:2 * b + 2, :].rearrange("p t n -> p (t n)")
                    else:
                        act.wait_ge(S("turned"), g + 1)
                        src = PB[4 + g % 2][:, :]
                    f(dst[:, k0 + 2 * b:k0 + 2 * b + 2, :].rearrange("p t n -> p (t n)"), src, ACT.Copy, "turn_hi")
                if between:
                    between()

            def chunk_evac(c, dst, width, scale=1.0, done=None):
                act.wait_ge(slab_used, done)
                for r in range(RB):
                    by = scale(r) if callable(scale) else scale
                    act.activation(dst(r), PB[2 * (c % 2) + r][:, 0:width], ACT.Copy, scale=by).then_inc(chunk_out, 1)

            act.wait_ge(S("vec_out"), 2)
            f(cT[:, :], vT[:, V_C:V_C + 16], ACT.Silu, "c_gated")
            act.wait_ge(S("mem_in"), 16)
            act.wait_ge(S("zeroed"), 2)
            norm_stats("mem", lambda r: MEM[:, r, :], D)
            norm_rows("mem", lambda r: MEM[:, r, :], lambda r: ROWB[:, r, :])
            turn_hi("mem", XTh, gain=vT[:, V_LN_MEM:V_LN_MEM + KT])
            skip(8)
            hi()
            for s in range(4):
                skip(2)
                hi()
            act.wait_ge(S("x_in"), 16)
            norm_stats("x", lambda r: X[:, r, :], D)
            act.wait_ge(S("turned"), TURN0["x"])
            norm_rows("x", lambda r: X[:, r, :], lambda r: ROWB[:, r, :])
            chunk_evac(0, lambda r: TMP[:, r, :], 512, done=4)
            for b in range(2):
                act.wait_ge(S("xk_turned"), b + 1)
                f(xkT[:, 2 * b:2 * b + 2, :].rearrange("p h n -> p (h n)"), PB[4 + b][:, :], ACT.Copy, "xk_out")
            for s in range(3):
                skip(3)
                hi()
            skip(7)
            chunk_evac(1, lambda r: xv[:, r, :], 512, done=8)
            for b in range(TURN_N["x"]):
                g = TURN0["x"] + b
                act.wait_ge(S("turned"), g + 1)
                f(XS[:, 2 * b:2 * b + 2, :].rearrange("p t n -> p (t n)"), PB[4 + g % 2][:, :], ACT.Copy, "turn_free")
            hi()
            turn_hi("x", XTh)
            with act.Fori(0, 2) as i, st.loop(i, 2, 24, 16):
                for c in range(4):
                    hi(4 * ZC)
                    skip()
                    hi(4 * ZC)
                    hi(4 * ZC)
                    skip()
                    hi()
                    act.wait_ge(slab_used, st.lins(-1))
                    for r in range(RB):
                        act.activation(Z[:, r, bass.ds(i * (4 * ZC) + c * ZC, ZC)],
                                       PB[2 * (c % 2) + r][:, 0:ZC], ACT.Copy).then_inc(chunk_out, 1)
            for b in range(4):
                act.wait_ge(S("g_wide"), b + 1)
                f(G[:, 512 * b:512 * b + 512], PB[4 + b % 2][:, :], ACT.Copy, "g_out")
            for r in range(RB):
                act.wait_ge(S("gate_in"), r + 1)
                f(eb[:, r, :], PB[r][:, :], ACT.Abs, "gla_f")
            act.wait_ge(S("gla_f"), 2)
            for r in range(RB):
                f(einv[:, r, :], eb[:, r, :], ACT.Exp, "gla_f", scale=-1.0)
            act.wait_ge(S("gla_f"), 4)
            for r in range(RB):
                f(kd[:, r, :], einv[:, r, :], ACT.Ln, "log1p", bias=one[:, 0:1])
            for r in range(RB):
                act.wait_ge(S("cum"), r + 1)
                f(bcs[:, r, :], PB[2 + r][:, :], ACT.Copy, "bc_out")
            for r in range(RB):
                f(eb[:, r, :], PB[2 + r][:, :], ACT.Exp, "eb_out")
                f(einv[:, r, :], PB[2 + r][:, :], ACT.Exp, "einv_out", scale=-1.0)
            act.wait_ge(S("cum"), 2 * RB + 1)
            f(decay[:, :, :].rearrange("p h n -> p (h n)"), PB[5][:, 0:GH * NCH], ACT.Exp, "decay_out")
            for r in range(RB):
                act.wait_ge(S("left"), r + 1)
                f(kd[:, r, :], bcs[:, r, :], ACT.Exp, "edec_out")
            for k in range(4):
                act.wait_ge(S("qk_turned"), k + 1)
                dst = (qdT, kiT)[k % 2]
                f(dst[:, 2 * (k // 2):2 * (k // 2) + 2, :].rearrange("p h n -> p (h n)"), PB[k][:, :], ACT.Copy,
                  "qk_out")
            for r in range(RB):
                f(Z[:, r, Z_RG:Z_RG + GVAL], Z[:, r, Z_RG:Z_RG + GVAL], ACT.Silu, "r_gated")
            for h in range(GH):
                act.wait_ge(S("gla_o"), h + 1)
                for r in range(RB):
                    if h + r:
                        act.wait_ge(S("gla_sq"), RB * h + r)
                    f(JUNK[:, 0:GV], PB[h][:, GV * r:GV * r + GV], ACT.Square, "gla_sq",
                      accum_out=gst[:, 0, h, r:r + 1])
            act.wait_ge(S("gla_sq"), RB * GH)
            f(gst[:, 1, :, :], gst[:, 0, :, :], ACT.Sqrt, "gla_root", scale=1.0 / GV, bias=eps[:, 0:1])
            for name, c0, n in (("cq", Z_CQ, QR), ("ckv", Z_CKV, KVR)):
                norm_stats(name, lambda r: Z[:, r, c0:c0 + n], n)
                norm_rows(name, lambda r: Z[:, r, c0:c0 + n], lambda r: Z[:, r, c0:c0 + n], RB)
            turn_hi("cq", XTh, gain=vT[:, V_GQ:V_GQ + 4])
            turn_hi("ckv", XTh, 4, gain=vT[:, V_GKV:V_GKV + 2])
            act.wait_ge(S("angle"), 2 * RB)
            for r in range(RB):
                for k in range(2):
                    f(cs[:, r, k, :], ang[:, r, k, :], ACT.Sin, "sines")
            skip(16)
            for c in range(3):
                hi()
                chunk_evac(CHUNK0["uq"] + c, lambda r: qrow[r][:, :, :].rearrange("p h d -> p (h d)")[:, 512 * c:512 * c + 512],
                           512, scale=QKD ** -0.5, done=st.lin - 1)
            for b in range(4):
                if b == 1:
                    hi()
                act.wait_ge(S("kT_made"), b + 1) if b < 3 else act.wait_ge(slab_used, st.lins(-1))
                f(kTn[b // 2][:, 2 * (b % 2):2 * (b % 2) + 2, :].rearrange("p h n -> p (h n)"),
                  PB[(4, 5, 6, 7)[b]][:, :], ACT.Copy, "kT_out")
            for c in range(2):
                act.wait_ge(S("v_made"), c + 1) if c == 0 else act.wait_ge(slab_used, st.lins())
                for r in range(RB):
                    act.activation(vrow[:, r, 512 * c:512 * c + 512], PB[2 * ((CHUNK0["uv"] + c) % 2) + r][:, :],
                                   ACT.Copy).then_inc(chunk_out, 1)
            act.wait_ge(S("kr_turned"), 1)
            f(krT[:, :], PB[4][0:ROPE, 0:SEQ], ACT.Copy, "kr_out")
            for h in range(MH + 2):
                if h < MH:
                    act.wait_ge(S("q_turned"), h + 1)
                    if h >= 2:
                        act.wait_ge(S("scored"), h - 1)
                    f(qTs[:, h % 2, 0:SEQ], PB[4 + h % 2][:, 0:SEQ], ACT.Copy, "q_out")
                    f(qTs[0:ROPE, h % 2, SEQ:2 * SEQ], PB[4 + h % 2][0:ROPE, SEQ:2 * SEQ], ACT.Copy, "q_out")
                g = h - 1
                if 0 <= g < MH:
                    act.wait_ge(S("maxed"), RB * (g + 1))
                    for r in range(RB):
                        part = prob[:, g % 2, P * r:P * (2 * r + 1)]
                        f(part, part, ACT.Exp, "exped", bias=mst[:, g % 4, 0, r:r + 1], accum_out=mst[:, g % 4, 1, r:r + 1])
                g = h - 2
                if 0 <= g < MH:
                    act.wait_ge(S("p_turned"), g + 1)
                    if g >= 2:
                        act.wait_ge(S("pv_done"), g - 1)
                    f(probT[:, g % 2, :], PB[2 + g % 2][:, 0:3 * P], ACT.Copy, "pT_out")
            hi()

            def ada_hi():
                skip()
                hi()

            def chunk_squared(name, layer, c, done):
                chunk_evac(CHUNK0[layer] + c, lambda r: ROWB[:, r, 512 * c:512 * c + 512], 512, done=done)
                post_square(name, c, lambda r: act.wait_ge(chunk_out, RB * (CHUNK0[layer] + c) + r + 1))

            turn_hi("o", XTh, between=ada_hi)
            for c in range(4):
                for s in range(4):
                    if c or s == 3:
                        ada_hi()
                    if c and s == 0:
                        chunk_squared("o", "wout", c - 1, st.lin - 2)
            chunk_squared("o", "wout", 3, st.lin - 1)
            post_root("o")

            def ffn(k, pre, after, more, gain=None):
                if k == 0:
                    norm_stats(pre, lambda r: X[:, r, :], D, after)
                    norm_rows(pre, lambda r: X[:, r, :], lambda r: ROWB[:, r, :])
                turn_hi(pre, XTh, gain=gain, between=hi)
                if k:
                    norm_stats(pre, lambda r: X[:, r, :], D, after)
                    act.wait_ge(S("rooted_inv"), NORMS.index(pre) + 1)
                b0 = RB * FN * k

                def chunk(j):
                    for _ in range(0 if isinstance(j, int) else 3):
                        hi()
                    skip(st.praw == 16)
                    hi()
                    hi()
                    act.wait_ge(slab_used, st.lins(-2))
                    if not isinstance(j, int) or k or j:
                        act.wait_ge(S("h_made"), j * RB + b0)
                    for r in range(RB):
                        act.activation(SIL[:, r, :], PB[r][:, :], ACT.Silu,
                                       scale=nstat[:, NORMS.index(pre), 2, r:r + 1] if k else 1.0).then_inc(S("silu_out"), 1)
                    for _ in range(2):
                        hi()

                def hidden_hi(j):
                    for b in range(2):
                        act.wait_ge(S("h_turned"), j * 2 + (b0 + b + 1))
                        act.activation(HTh[:, 2 * b:2 * b + 2, :].rearrange("p t n -> p (t n)"), PB[4 + b][:, :],
                                       ACT.Copy).then_inc(S("hid_hi"), 1)

                chunk(0)
                hi()
                hidden_hi(0)
                for first, last, per in ((0, FN_ADA, 16), (FN_ADA, FN - 1, 12)) if k == 0 else ((0, FN - 1, 12),):
                    with act.Fori(first, last) as i, st.loop(i, last - first, per, 12, first):
                        chunk(i + 1)
                        for n in range(5):
                            if n in (0, 2, 4):
                                skip(per == 16)
                            hi()
                        hidden_hi(i + 1)
                    if per == 16:
                        for b in range(4):
                            act.wait_ge(S("g_wide"), 4 + b + 1)
                            f(G[:, 512 * b:512 * b + 512], PB[6 + b % 2][:, :], ACT.Copy, "g_out")
                y_all = 8 * (FN + 1) * (k + 1)
                for n in range(4):
                    if n < 3 or more:
                        hi()
                    post_square(("y1", "y2")[k], n, lambda r: act.wait_ge(S("y_added"), y_all - 8 + RB * n + r + 1))
                post_root(("y1", "y2")[k])

            ffn(0, "f1", "o", True)
            turn_hi("z2", XTh, gain=vT[:, V_LN_MIX:V_LN_MIX + KT])
            norm_stats("z2", lambda r: X[:, r, :], D, "y1")
            act.wait_ge(S("rooted_inv"), NORMS.index("z2") + 1)
            hi(4 * Z2_PARTS[0][1])
            for c0, width in Z2_PARTS:
                with act.Fori(0, Z2N // 2) as i, st.loop(i, Z2N // 2, 8, 8):
                    for c in range(2):
                        hi(4 * width)
                        hi(4 * width)
                        hi()
                        hi()
                        act.wait_ge(slab_used, st.lins(-2))
                        for r in range(RB):
                            act.activation(Z2[:, r, bass.ds(i * (2 * width) + (c0 + c * width), width)],
                                           PB[2 * (c % 2) + r][:, 0:width], ACT.Copy,
                                           scale=nstat[:, NORMS.index("z2"), 2, r:r + 1]).then_inc(chunk_out, 1)
            for k in range(2):
                act.wait_ge(S("w1_used"), k + 1)
                f(hidT[:, k, :], PB[4 + k][:, 0:NG * NCMP], ACT.Gelu_apprx_tanh, "gelued")
            act.wait_ge(S("kc_done"), 1)
            f(kcT[:, :, :].rearrange("p g n -> p (g n)"), PB[6][0:HD, 0:NG * NCMP], ACT.Copy, "kc_out")
            act.wait_ge(S("kc_done"), 2)
            f(vc[:, :, :].rearrange("p g n -> p (g n)"), PB[7][0:NCMP, 0:NG * HD], ACT.Copy, "kc_out")
            for k in range(8):
                act.wait_ge(S("nq_turned"), k + 1)
                f(QT[:, 2 * k:2 * k + 2, :].rearrange("p h n -> p (h n)"), PB[4 + k % 4][0:HD, :], ACT.Copy, "nq_out",
                  scale=HD ** -0.5)
            for k in range(4):
                act.wait_ge(S("nk_turned"), k + 1)
                f(KT2[:, k, :, :].rearrange("p b n -> p (b n)"), PB[k][0:HD, :], ACT.Copy, "nk_out")
            for r in range(RB):
                f(Z2[:, r, Z2_GL:Z2_U], Z2[:, r, Z2_GL:Z2_U], ACT.Sigmoid, "gates_out")
            for t in range(NH * RB + 3):
                u = t - 1
                if 0 <= u < NH * RB:
                    nk, nc_ = (P, NCMP0) if u % 2 == 0 else (SEQ, NCMP)
                    act.wait_ge(S("n_maxed"), u + 1)
                    for b in range(2):
                        f(NSPROB(u % 4)[:, b * nk:b * nk + nk], NSPROB(u % 4)[:, b * nk:b * nk + nk], ACT.Exp, "n_exped",
                          bias=nst[:, u % 8, 0, b:b + 1], accum_out=nst[:, u % 8, 1, b + 1:b + 2])
                    f(pc[:, u % 4, 0:nc_], pc[:, u % 4, 0:nc_], ACT.Exp, "n_exped",
                      bias=nst[:, u % 8, 0, 2:3], accum_out=nst[:, u % 8, 1, 0:1])
                u = t - 3
                if 0 <= u < NH * RB:
                    nb = 2 + 2 * (u % 2)
                    act.wait_ge(S("n_turned"), u + 1)
                    if u >= 2:
                        act.wait_ge(S("n_pv"), u - 1)
                    f(pT[:, u % 2, 0:nb * P], PB[4 + u % 2][:, 0:nb * P], ACT.Copy, "npT_out")
            for r in range(RB):
                f(Z2[:, r, Z2_M:Z2W], Z2[:, r, Z2_M:Z2W], ACT.Sigmoid, "merge_gated")
            for g in range(PG):
                act.wait_ge(S("pool_mixed"), 2 * g + 2)
                f(XTh[:, 2 * g:2 * g + 2, :].rearrange("p t n -> p (t n)"), PB[g][:, :], ACT.Copy, "pool_hi")
            for g in range(PG):
                act.wait_ge(S("pool_scaled"), g + 1)
                f(XTh[:, 8 + 2 * g:10 + 2 * g, :].rearrange("p t n -> p (t n)"), TMPP[:, g % 2, :], ACT.Copy, "pool_hi")
            turn_hi("att", XTh)
            for c in range(4):
                for s in range(4):
                    hi()
            turn_hi("y", XTh, between=hi)
            for c in range(4):
                for s in range(4):
                    if c or s == 3:
                        hi()
                    if c and s == 0:
                        chunk_squared("mix", "mix", c - 1, st.lin - 2)
            chunk_squared("mix", "mix", 3, st.lin - 1)
            post_root("mix")
            turn_hi("xq", XTh, gain=vT[:, V_LN_X:V_LN_X + KT], between=hi)
            norm_stats("xq", lambda r: X[:, r, :], D, "mix")
            act.wait_ge(S("rooted_inv"), NORMS.index("xq") + 1)
            hi()
            chunk_evac(CHUNK0["xq"], lambda r: HROW[:, r, :], 512, scale=lambda r: nstat[:, NORMS.index("xq"), 2, r:r + 1],
                       done=st.lin - 1)
            for b in range(2):
                act.wait_ge(S("xq_turned"), b + 1)
                f(xqT[:, 2 * b:2 * b + 2, :].rearrange("p h n -> p (h n)"), PB[6 + b][:, :], ACT.Copy, "xq_out",
                  scale=XD ** -0.5)
            for h in range(XH + 1):
                if h < XH:
                    act.wait_ge(S("x_maxed"), h + 1)
                    for r in range(RB):
                        if h >= 2:
                            act.wait_ge(S("xp_turned"), h - 1)
                        f(xp[:, h % 2, SEQ * r:SEQ * r + SEQ], PB[h % 2][:, SEQ * r:SEQ * r + SEQ], ACT.Exp, "x_exped",
                          bias=mst[:, h % 4, 0, r:r + 1], accum_out=mst[:, h % 4, 1, r:r + 1])
                g = h - 1
                if g >= 0:
                    act.wait_ge(S("xp_turned"), g + 1)
                    if g >= 2:
                        act.wait_ge(S("x_pv"), g - 1)
                    f(xpT[:, g % 2, :], PB[4 + g % 2][:, :], ACT.Copy, "xpT_out")
            turn_hi("xo", XTh, 12)
            for c in range(4):
                hi()
                if c:
                    chunk_squared("xo", "xo", c - 1, st.lin - 2)
            chunk_squared("xo", "xo", 3, st.lin - 1)
            post_root("xo")
            ffn(1, "f2", "xo", False, vT[:, V_LN_FFN:V_LN_FFN + KT])

        @block.tensor
        def _(pe):
            st = Slabs()

            def turn(name, src, ready, groups=None, after=None):
                ready()
                for b in groups or range(TURN_N[name]):
                    g = TURN0[name] + b
                    if g >= 2:
                        pe.wait_ge(S("turn_free"), g - 1)
                    if after:
                        pe.wait_ge(S("x_added"), added(after, b // 2))
                    for k in range(2):
                        for r in range(RB):
                            mm = pe.transpose(PB[4 + g % 2][:, SEQ * k + P * r:SEQ * k + P * r + P],
                                              src(r, 2 * b + k), ident)
                    mm.then_inc(S("turned"), 1)

            def turn_into(name, src, ready, first_slab, after=None):
                turn(name, src, ready, range(4), after)
                for s in range(4):
                    pe.wait_ge(S("turn_free"), TURN0[name] + 2 * s + 2)
                    first_slab(s)
                    if s < 2:
                        turn(name, src, lambda: None, range(4 + 2 * s, 6 + 2 * s), after)

            def turned_ready(name):
                pe.wait_ge(S("turn_free"), TURN0[name] + TURN_N[name])

            def slab_mm(banks, kts, width, first, last, lhs=None):
                hi_t, lo_t = lhs or (XTh, XTl)
                pe.wait_ge(slab_done, st.raws(1))
                n = len(kts)
                w = [t[:, st.lin % 2, 0:n * width].rearrange("p (t n) -> p t n", t=n) for t in (wh, wl)]
                for r in range(RB):
                    for q, k in enumerate(kts):
                        rows = slice(P * r, P * r + P)
                        out_ = PB[banks[r]][:, 0:width]
                        pe.matmul(out_, hi_t[:, k, rows], w[0][:, q, :], start=first and q == 0, stop=False)
                        pe.matmul(out_, hi_t[:, k, rows], w[1][:, q, :], start=False, stop=False)
                        mm = pe.matmul(out_, lo_t[:, k, rows], w[0][:, q, :], start=False, stop=last and q == n - 1)
                mm.then_inc(slab_used, 1)
                st.next()

            def chunk(c, kts, width, skip=(0, 0, 0, 0), free=None, turning=None, ready=None):
                if free is not None:
                    pe.wait_ge(chunk_out, free)
                elif c >= 2:
                    pe.wait_ge(chunk_out, RB * (c - 1))
                n = len(kts) // 4

                def part(s):
                    if ready:
                        ready(s)
                    slab_mm((2 * (c % 2), 2 * (c % 2) + 1), kts[4 * s:4 * s + 4], width, s == 0, s == n - 1)
                    for _ in range(skip[s]):
                        st.next(False)

                if turning:
                    turn_into(*turning[:3], part, *turning[3:])
                else:
                    for s in range(n):
                        part(s)

            ALL = list(range(KT))

            def mod_sum(v):
                pe.wait_ge(slab_done, st.raws())
                if v:
                    pe.wait_ge(S("mod_ready"), v)
                for k in range(KT):
                    mm = pe.matmul(PB[7][:, k:k + 1], ACC[:, P * k:P * k + P], ones[:, 0:1], start=True, stop=True)
                mm.then_inc(S("mod_sum"), 1)

            def gain_rows(banks):
                for b in range(4):
                    if b >= 2:
                        pe.wait_ge(S("g_out"), gain_rows.n + b - 1)
                    for k in range(4):
                        mm = pe.matmul(PB[banks[b % 2]][:, P * k:P * k + P],
                                       gT[:, 4 * b + k:4 * b + k + 1].broadcast_to([P, P]), ident, start=True, stop=True)
                    mm.then_inc(S("g_wide"), 1)
                gain_rows.n += 4

            gain_rows.n = 0

            pe.wait_ge(S("con_in"), 16)
            pe.wait_ge(S("vec_in"), 16 * 13)
            pe.transpose(PB[0][:, 0:126], VROW[0:126, :], ident[0:126, 0:126]).then_inc(S("vec_turned"), 1)
            pe.transpose(PB[1][:, 0:P], BROW[:, :], ident).then_inc(S("vec_turned"), 1)
            pe.wait_ge(S("rel_bias_in"), 32)
            pe.transpose(PB[2][0:BUCKETS, 0:NH], rb16[:, :], ident[0:NH, 0:NH]).then_inc(S("rel_turned"), 1)
            pe.wait_ge(S("rel_turned_out"), 1)
            pe.matmul(PB[3][0:NH, 0:SEQ], rbT[:, :], onehot[:, :], start=True, stop=True).then_inc(S("rel_made"), 1)
            turn("mem", lambda r, k: ROWB[:, r, P * k:P * k + P], lambda: pe.wait_ge(S("normed"), RB))
            turned_ready("mem")
            pe.wait_ge(S("vec_out"), 2)
            for _ in range(8):
                st.next(False)
            chunk(0, ALL, 512, skip=(2, 2, 2, 2))
            mod_sum(0)
            pe.wait_ge(chunk_out, RB)
            for b in range(2):
                for k in range(2):
                    for r in range(RB):
                        h = 2 * b + k
                        mm = pe.transpose(PB[4 + b][:, SEQ * k + P * r:SEQ * k + P * r + P], TMP[:, r, XD * h:XD * h + XD],
                                          ident)
                mm.then_inc(S("xk_turned"), 1)
            pe.wait_ge(S("xk_out"), 2)
            pe.wait_ge(S("rel_row"), 1)
            chunk(1, ALL, 512, skip=(3, 3, 3, 3))
            turn("x", lambda r, k: ROWB[:, r, P * k:P * k + P], lambda: pe.wait_ge(S("normed"), RB * 2))
            for _ in range(4):
                st.next(False)
            mod_sum(1)
            with pe.Fori(0, 2) as i, st.loop(i, 2, 24, 16):
                for c in range(4):
                    chunk(c, ALL, ZC, skip=(0, 1, 0, 1), free=i * 8 + (RB * (c + 1) if c else RB),
                          ready=None if c else lambda s: pe.wait_ge(S("x_lo"), 2 * s + 2))
            mod_sum(2)
            pe.wait_ge(S("mod_ready"), 3)
            gain_rows((4, 5))
            pe.wait_ge(chunk_out, RB * CHUNK0["uq"])
            for r in range(RB):
                mm = pe.transpose(PB[6][0:GR, P * r:P * r + P], Z[:, r, Z_AG:Z_RG], ident)
            mm.then_inc(S("a_turned"), 1)
            pe.wait_ge(S("gla_in"), 48)
            pe.wait_ge(S("a_out"), 1)
            for r in range(RB):
                pe.matmul(PB[r][:, :], aT[:, P * r:P * r + P], wgu[:, :], start=True, stop=False)
                pe.matmul(PB[r][:, :], ones[0:1, :], bgr[:, :], start=False, stop=True).then_inc(S("gate_in"), 1)
            pe.wait_ge(S("log_a"), RB)
            for r in range(RB):
                pe.matmul(PB[2 + r][:, :], tri, la[:, r, :], start=True, stop=True).then_inc(S("cum"), 1)
            for r in range(RB):
                pe.matmul(PB[6 + r][:, :], blk, la[:, r, :], start=True, stop=True).then_inc(S("cum"), 1)
            pe.wait_ge(S("g_out"), 4)
            for h in range(GH):
                for r in range(RB):
                    n = NCH * h + 2 * r
                    mm = pe.matmul(PB[5][:, n:n + 2], la[:, r, GK * h:GK * h + GK], blk[:, 0:CH + 1:CH], start=True, stop=True)
            mm.then_inc(S("cum"), 1)
            pe.wait_ge(S("decayed"), 2 * RB)
            pe.wait_ge(S("einv_out"), RB)
            for b in range(4):
                c0 = (Z_QG, Z_KG)[b % 2]
                for k in range(2):
                    for r in range(RB):
                        h = 2 * (b // 2) + k
                        mm = pe.transpose(PB[b][:, SEQ * k + P * r:SEQ * k + P * r + P],
                                          Z[:, r, c0 + GK * h:c0 + GK * h + GK], ident)
                mm.then_inc(S("qk_turned"), 1)
            pe.wait_ge(S("qk_out"), 4)
            pe.wait_ge(S("decay_out"), 1)
            for b in range(2):
                for k in range(2):
                    for r in range(RB):
                        h, rows = 2 * b + k, slice(P * r, P * r + P)
                        mm = pe.matmul(PB[4 + b][:, SEQ * k + P * r:SEQ * k + P * r + P], kiT[:, h, rows],
                                       qdT[:, h, rows], start=True, stop=True)
                mm.then_inc(S("gla_scored"), 1)
            pe.wait_ge(S("left"), RB)
            pe.wait_ge(S("k_decayed"), RB)
            for m in range(3 * GH):
                h, n = m // 3, m % 3
                rows = slice(CH * (n % 2), CH * (n % 2) + CH)
                bank, half = (6 + h // 2, h % 2) if n == 1 else (h, n // 2)
                mm = pe.matmul(PB[bank][:, GV * half:GV * half + GV],
                               kd[rows, n // 2, GK * h:GK * h + GK],
                               Z[rows, n // 2, Z_VG + GV * h:Z_VG + GV * h + GV], start=True, stop=True)
                mm.then_inc(S("state_add"), 1)
            for h in range(GH):
                pe.wait_ge(S("stated"), 3 * GH)
                pe.wait_ge(S("att_masked"), 2)
                for r in range(RB):
                    o = PB[h][:, GV * r:GV * r + GV]
                    pe.matmul(o, attT[:, h, r, :], Z[:, r, Z_VG + GV * h:Z_VG + GV * h + GV], start=True,
                              stop=False, skip_group_check=True)
                    for n in range(2 * r, 2 * r + 2):
                        if n:
                            q = CH * (n % 2)
                            mm = pe.matmul(PB[h][q:q + CH, GV * r:GV * r + GV], qdT[:, h, CH * n:CH * n + CH],
                                           states[:, h, n - 1, :], start=False, stop=n % 2 == 1,
                                           skip_group_check=True)
                mm.then_inc(S("gla_o"), 1)
            turn("cq", lambda r, k: Z[:, r, Z_CQ + P * k:Z_CQ + P * k + P], lambda: pe.wait_ge(S("normed"), RB * 3))
            turn("ckv", lambda r, k: Z[:, r, Z_CKV + P * k:Z_CKV + P * k + P], lambda: pe.wait_ge(S("normed"), RB * 4))
            turned_ready("cq")
            pe.wait_ge(S("gla_done"), RB * GH)
            for c in range(3):
                chunk(CHUNK0["uq"] + c, [0, 1, 2, 3], 512)
                if c == 0:
                    for _ in range(KT):
                        st.next(False)
                    mod_sum(3)
            turned_ready("ckv")
            pe.wait_ge(S("mod_ready"), 4)
            pe.wait_ge(slab_done, st.raws(1))
            w = [t[:, st.lin % 2, :].rearrange("p (t n) -> p t n", t=2) for t in (wh, wl)]
            for b in range(4):
                for k in range(2):
                    h = 2 * b + k
                    o = PB[4 + b][:, SEQ * k:SEQ * k + SEQ]
                    for t in range(2):
                        cols = slice(NOPE * h, NOPE * h + NOPE)
                        pe.matmul(o, w[0][:, t, cols], XTh[:, 4 + t, :], start=t == 0, stop=False)
                        pe.matmul(o, w[0][:, t, cols], XTl[:, 4 + t, :], start=False, stop=False)
                        mm = pe.matmul(o, w[1][:, t, cols], XTh[:, 4 + t, :], start=False, stop=t == 1)
                mm.then_inc(S("kT_made") if b < 3 else slab_used, 1)
            st.next()
            pe.wait_ge(slab_done, st.raws(1))
            w = [t[:, st.lin % 2, :].rearrange("p (t n) -> p t n", t=2) for t in (wh, wl)]
            for c in range(2):
                n = CHUNK0["uv"] + c
                pe.wait_ge(chunk_out, RB * (n - 1))
                for r in range(RB):
                    o, rows = PB[2 * (n % 2) + r][:, :], slice(P * r, P * r + P)
                    for t in range(2):
                        cols = slice(512 * c, 512 * c + 512)
                        pe.matmul(o, XTh[:, 4 + t, rows], w[0][:, t, cols], start=t == 0, stop=False)
                        pe.matmul(o, XTh[:, 4 + t, rows], w[1][:, t, cols], start=False, stop=False)
                        mm = pe.matmul(o, XTl[:, 4 + t, rows], w[0][:, t, cols], start=False, stop=t == 1)
                mm.then_inc(S("v_made") if c == 0 else slab_used, 1)
            st.next()
            pe.wait_ge(S("roped"), 2 * RB)
            pe.wait_ge(S("kT_out"), 4)
            for r in range(RB):
                mm = pe.transpose(PB[4][0:ROPE, P * r:P * r + P], Z[:, r, Z_KR:Z_QG], ident)
            mm.then_inc(S("kr_turned"), 1)
            pe.wait_ge(S("kr_out"), 1)
            pe.wait_ge(chunk_out, RB * CHUNK0["wout"])
            for t in range(MH + 3):
                if t < MH:
                    if t >= 2:
                        pe.wait_ge(S("q_out"), 2 * (t - 1))
                    for r in range(RB):
                        pe.transpose(PB[4 + t % 2][:, P * r:P * r + P], qrow[r][:, t, 0:NOPE], ident)
                        mm = pe.transpose(PB[4 + t % 2][0:ROPE, SEQ + P * r:SEQ + P * r + P], qrow[r][:, t, NOPE:QKD],
                                          ident)
                    mm.then_inc(S("q_turned"), 1)
                h = t - 1
                if 0 <= h < MH:
                    pe.wait_ge(S("q_out"), 2 * (h + 1))
                    if h >= 2:
                        pe.wait_ge(S("masked"), h - 1)
                    for r in range(RB):
                        nk = P * (r + 1)
                        o = PB[6 + h % 2][:, P * r:P * r + nk]
                        pe.matmul(o, qTs[:, h % 2, P * r:P * r + P], kTn[h // 4][:, h % 4, 0:nk], start=True, stop=False)
                        mm = pe.matmul(o, qTs[0:ROPE, h % 2, SEQ + P * r:SEQ + P * r + P], krT[:, 0:nk], start=False,
                                       stop=True)
                    mm.then_inc(S("scored"), 1)
                h = t - 2
                if 0 <= h < MH:
                    pe.wait_ge(S("exped"), RB * (h + 1))
                    if h >= 2:
                        pe.wait_ge(S("pT_out"), h - 1)
                    for b in range(3):
                        mm = pe.transpose(PB[2 + h % 2][:, P * b:P * b + P], prob[:, h % 2, P * b:P * b + P], ident)
                    mm.then_inc(S("p_turned"), 1)
                h = t - 3
                if 0 <= h < MH:
                    pe.wait_ge(S("pT_out"), h + 1)
                    if h >= 2:
                        pe.wait_ge(S("mla_o"), RB * (h - 1))
                    v = [vrow[:, r, VD * h:VD * h + VD] for r in range(RB)]
                    o = PB[h % 2]
                    pe.matmul(o[:, 0:VD], probT[:, h % 2, 0:P], v[0], start=True, stop=True)
                    pe.matmul(o[:, P:P + VD], probT[:, h % 2, P:2 * P], v[0], start=True, stop=False)
                    mm = pe.matmul(o[:, P:P + VD], probT[:, h % 2, 2 * P:3 * P], v[1], start=False, stop=True)
                    mm.then_inc(S("pv_done"), 1)
            for c in range(4):
                chunk(CHUNK0["wout"] + c, ALL, 512, skip=(1, 1, 1, 1), turning=None if c else (
                    "o", lambda r, k: Z[:, r, Z_QG + P * k:Z_QG + P * k + P], lambda: pe.wait_ge(S("mla_o"), RB * MH)))
            mod_sum(4)

            def ffn(k, pre):
                b0 = RB * FN * k
                y0 = 8 * (FN + 1) * k

                def gate_up(j):
                    for half in range(2):
                        if isinstance(j, int) and half == 0:
                            rows = X if k else ROWB
                            turn_into(pre, lambda r, q: rows[:, r, P * q:P * q + P],
                                      lambda: None if k else pe.wait_ge(S("normed"), RB * 5),
                                      lambda s: slab_mm((0, 1), ALL[4 * s:4 * s + 4], 512, s == 0, s == 3), "xo" if k else None)
                            continue
                        if not isinstance(j, int):
                            pe.wait_ge(S(("silu_out", "h_made")[half]), j * RB + b0)
                            pe.wait_ge(S("y_added"), j * 8 + (y0 - 8 + (4, 8)[half]))
                        for s in range(4):
                            slab_mm((2 * half, 2 * half + 1), ALL[4 * s:4 * s + 4], 512, s == 0, s == 3)
                        if st.praw == 16:
                            st.next(False)

                def hidden_turn(j):
                    pe.wait_ge(S("h_made"), j * RB + (b0 + RB))
                    if not isinstance(j, int):
                        pe.wait_ge(S("hid_lo"), j * 2 + b0)
                    for b in range(2):
                        for q in range(2):
                            for r in range(RB):
                                mm = pe.transpose(PB[4 + b][:, SEQ * q + P * r:SEQ * q + P * r + P],
                                                  HROW[:, r, P * (2 * b + q):P * (2 * b + q) + P], ident)
                        mm.then_inc(S("h_turned"), 1)

                def down(j):
                    pe.wait_ge(S("hid_lo"), j * 2 + (b0 + 2))
                    for n in range(4):
                        banks = ((6, 7), (0, 1), (6, 7), (2, 3))[n]
                        if n == 0 and not (isinstance(j, int) and j == 0):
                            pe.wait_ge(S("y_added"), j * 8 + (y0 + 6))
                        if n == 1:
                            pe.wait_ge(S("silu_out"), (j + 2) * RB + b0 if not isinstance(j, int) else RB * FN + b0)
                        if n == 2:
                            pe.wait_ge(S("y_added"), j * 8 + (y0 + 8 + 2))
                        if n == 3 and not isinstance(j, int):
                            pe.wait_ge(S("h_made"), (j + 2) * RB + b0)
                        slab_mm(banks, [0, 1, 2, 3], 512, True, True, lhs=(HTh, HTl))
                        if st.praw == 16 and n % 2:
                            st.next(False)

                gate_up(0)
                hidden_turn(0)
                for first, last, per in ((0, FN_ADA, 16), (FN_ADA, FN - 1, 12)) if k == 0 else ((0, FN - 1, 12),):
                    with pe.Fori(first, last) as i, st.loop(i, last - first, per, 12, first):
                        gate_up(i + 1)
                        down(i)
                        hidden_turn(i + 1)
                    if per == 16:
                        pe.wait_ge(S("y_added"), y0 + 8 + 8 * (last - 1) + 6)
                        mod_sum(5)
                        pe.wait_ge(S("mod_ready"), 6)
                        gain_rows((6, 7))
                        pe.wait_ge(S("g_out"), 8)
                down(FN - 1)

            pe.wait_ge(S("mod_ready"), 5)
            ffn(0, "f1")
            turn("z2", lambda r, k: X[:, r, P * k:P * k + P], lambda: None, after="y1")
            turned_ready("z2")
            for part, (_, width) in enumerate(Z2_PARTS):
                with pe.Fori(0, Z2N // 2) as i, st.loop(i, Z2N // 2, 8, 8):
                    for c in range(2):
                        chunk(c, ALL, width, free=i * 4 + RB * (CHUNK0["zin2"] + Z2N * part + c - 1))
            pe.wait_ge(S("cmp_in"), 64)
            pe.wait_ge(chunk_out, RB * CHUNK0["mix"])
            pe.transpose(PB[6][:, 0:2 * CS], perow[:, :], ident[0:2 * CS, 0:2 * CS]).then_inc(S("pe_turned"), 1)
            for b in range(4):
                for k in range(2):
                    for r in range(RB):
                        c0 = Z2_KV + KVW * (b // 2) + HD * (2 * (b % 2) + k)
                        cols = slice(SEQ * k + P * r, SEQ * k + P * r + P)
                        pe.transpose(PB[b][0:HD, cols], Z2[:, r, c0:c0 + HD], ident)
                        mm = pe.matmul(PB[b][HD:2 * HD, cols], Z2[:, r, c0:c0 + HD], ident, start=True, stop=True)
                mm.then_inc(S("raw_turned"), 1)
            for k in range(2):
                pe.wait_ge(S(f"w1_in{k}"), 32)
                pe.wait_ge(S("raw_out"), 2 * k + 2)
                for l in range(CS):
                    mm = pe.matmul(PB[4 + k][:, 0:NG * NCMP].rearrange("p (g n) -> p g n", g=NG), w1s[:, k, l, :],
                                   rawT[:, k, :, l:l + CS * (NCMP - 1) + 1:CS], start=l == 0, stop=l == CS - 1)
                mm.then_inc(S("w1_used"), 1)
            pe.wait_ge(S("gelued"), 2)
            pe.matmul(PB[6][0:HD, 0:NG * NCMP], w2s[:, 0, :], hidT[:, 0, :], start=True, stop=True).then_inc(S("kc_done"), 1)
            for g in range(NG):
                mm = pe.matmul(PB[7][0:NCMP, HD * g:HD * g + HD], hidT[:, 1, NCMP * g:NCMP * g + NCMP], w2s[:, 1, :],
                               start=True, stop=True)
            mm.then_inc(S("kc_done"), 1)
            pe.wait_ge(S("kc_out"), 2)
            for k in range(8):
                if k >= 4:
                    pe.wait_ge(S("nq_out"), k - 3)
                for q in range(2):
                    for r in range(RB):
                        h = 2 * k + q
                        mm = pe.transpose(PB[4 + k % 4][0:HD, SEQ * q + P * r:SEQ * q + P * r + P],
                                          Z2[:, r, HD * h:HD * h + HD], ident)
                mm.then_inc(S("nq_turned"), 1)
            for g in range(NG):
                for b in range(2):
                    for r in range(RB):
                        c0 = Z2_KV + KVW * (2 + 2 * b) + HD * g
                        mm = pe.transpose(PB[g][0:HD, SEQ * b + P * r:SEQ * b + P * r + P], Z2[:, r, c0:c0 + HD], ident)
                mm.then_inc(S("nk_turned"), 1)
            pe.wait_ge(S("nq_out"), 8)
            pe.wait_ge(S("nk_out"), 4)
            for t in range(NH * RB + 4):
                u = t
                if u < NH * RB:
                    h, r = u // 2, u % 2
                    g, nk, n_c = h // HPG, P * (r + 1), (NCMP0, NCMP)[r]
                    if u >= 2:
                        pe.wait_ge(S("n_added"), u - 1)
                    q = QT[:, h, P * r:P * r + P]
                    for b in range(2):
                        pe.matmul(PB[u % 2][:, nk * b:nk * b + nk], q, KT2[:, g, b, 0:nk], start=True, stop=True)
                    if u >= 4:
                        pe.wait_ge(S("n_cT"), u - 3)
                    pe.matmul(PB[2 + u % 2][:, 0:n_c], q, kcT[:, g, 0:n_c], start=True, stop=True)\
                        .then_inc(S("n_scored"), 1)
                u = t - 3
                if 0 <= u < NH * RB:
                    r = u % 2
                    nk, n_c = P * (r + 1), (NCMP0, NCMP)[r]
                    pe.wait_ge(S("n_exped"), 3 * (u + 1))
                    if u >= 2:
                        pe.wait_ge(S("npT_out"), u - 1)
                    for b in range(2 * (r + 1)):
                        pe.transpose(PB[4 + u % 2][:, P * b:P * b + P], NSPROB(u % 4)[:, P * b:P * b + P], ident)
                    pe.wait_ge(S("n_added"), min(u + 3, NH * RB))
                    pe.transpose(PB[2 + u % 2][0:n_c, P:2 * P], pc[:, u % 4, 0:n_c], ident).then_inc(S("n_turned"), 1)
                u = t - 4
                if 0 <= u < NH * RB:
                    h, r = u // 2, u % 2
                    g, n_c = h // HPG, (NCMP0, NCMP)[r]
                    pe.wait_ge(S("npT_out"), u + 1)
                    pe.wait_ge(S("n_cT"), u + 1)
                    if u >= 2:
                        pe.wait_ge(S("nsa_o"), 3 * (u - 1))
                    for b in range(2):
                        for k in range(r + 1):
                            c0 = Z2_KV + KVW * (3 + 2 * b) + HD * g
                            blk_ = b * (r + 1) + k
                            pe.matmul(PB[6 + u % 2][:, HD * b:HD * b + HD], pT[:, u % 2, P * blk_:P * blk_ + P],
                                      Z2[:, k, c0:c0 + HD], start=k == 0, stop=k == r)
                    pe.matmul(PB[6 + u % 2][:, 2 * HD:3 * HD], pcT[0:n_c, u % 2, :], vc[0:n_c, g, :], start=True, stop=True)\
                        .then_inc(S("n_pv"), 1)
            pe.wait_ge(S("band_in"), 16)
            pe.wait_ge(S("nsa_o"), 3 * NH * RB)
            for m in range(2 * PG):
                g, t = m // 2, m % 2
                c0 = Z2_U + PGW * g + P * t
                o = PB[g][:, SEQ * t:SEQ * t + SEQ]
                pe.matmul(o, Z2[:, 0, c0:c0 + P], band[:, g, 0:SEQ], start=True, stop=False, skip_group_check=True)
                pe.matmul(PB[g][:, SEQ * t + P:SEQ * t + SEQ], Z2[:, 1, c0:c0 + P], band[:, g, SEQ:], start=False,
                          stop=True, skip_group_check=True).then_inc(S("pool_mixed"), 1)
            pe.wait_ge(slab_done, st.raws(1))
            w = [t[:, st.lin % 2, :].rearrange("p (g t n) -> p g t n", g=PG, t=2) for t in (wh, wl)]
            for g in range(PG):
                pe.wait_ge(S("pool_lo"), g + 1)
                for q in range(2):
                    o, cols = PB[4 + g][:, SEQ * q:SEQ * q + SEQ], slice(P * q, P * q + P)
                    for t in range(2):
                        pe.matmul(o, w[0][:, g, t, cols], XTh[:, 2 * g + t, :], start=t == 0, stop=False)
                        pe.matmul(o, w[0][:, g, t, cols], XTl[:, 2 * g + t, :], start=False, stop=False)
                        mm = pe.matmul(o, w[1][:, g, t, cols], XTh[:, 2 * g + t, :], start=False, stop=t == 1)
                mm.then_inc(S("pool_lin") if g < PG - 1 else slab_used, 1)
            st.next()
            pe.wait_ge(S("pool_lo"), 2 * PG)
            turn("att", lambda r, k: Z2[:, r, P * k:P * k + P], lambda: None)
            turned_ready("att")
            for c in range(4):
                if c >= 2:
                    pe.wait_ge(S("merged"), 3 * RB * (c - 1))
                for half in range(2):
                    for s in range(2):
                        k = 8 * half + 4 * s
                        slab_mm((4 * (c % 2) + 2 * half, 4 * (c % 2) + 2 * half + 1), ALL[k:k + 4], 512, s == 0, s == 1)
            for c in range(4):
                chunk(CHUNK0["mix"] + c, ALL, 512, turning=None if c else (
                    "y", lambda r, k: Z2[:, r, P * k:P * k + P], lambda: pe.wait_ge(S("merged"), 3 * RB * 4)))
            chunk(CHUNK0["xq"], ALL, 512, turning=(
                "xq", lambda r, k: X[:, r, P * k:P * k + P], lambda: None, "mix"))
            pe.wait_ge(chunk_out, RB * CHUNK0["xo"])
            for b in range(2):
                for k in range(2):
                    for r in range(RB):
                        h = 2 * b + k
                        mm = pe.transpose(PB[6 + b][:, SEQ * k + P * r:SEQ * k + P * r + P], HROW[:, r, XD * h:XD * h + XD],
                                          ident)
                mm.then_inc(S("xq_turned"), 1)
            pe.wait_ge(S("xq_out"), 2)
            for t in range(XH + 2):
                h = t
                if h < XH:
                    if h >= 2:
                        pe.wait_ge(S("x_exped"), RB * (h - 1))
                    for r in range(RB):
                        mm = pe.matmul(PB[h % 2][:, SEQ * r:SEQ * r + SEQ], xqT[:, h, P * r:P * r + P], xkT[:, h, :],
                                       start=True, stop=True)
                    mm.then_inc(S("x_scored"), 1)
                h = t - 1
                if 0 <= h < XH:
                    pe.wait_ge(S("x_exped"), RB * (h + 1))
                    if h >= 2:
                        pe.wait_ge(S("xpT_out"), h - 1)
                    for b in range(4):
                        mm = pe.transpose(PB[4 + h % 2][:, P * b:P * b + P], xp[:, h % 2, P * b:P * b + P], ident)
                    mm.then_inc(S("xp_turned"), 1)
                h = t - 2
                if 0 <= h < XH:
                    pe.wait_ge(S("xpT_out"), h + 1)
                    if h >= 2:
                        pe.wait_ge(S("xatt_o"), RB * (h - 1))
                    for r in range(RB):
                        for k in range(RB):
                            mm = pe.matmul(PB[2 + h % 2][:, P * r:P * r + XD], xpT[:, h % 2, P * (2 * r + k):P * (2 * r + k) + P],
                                           xv[:, k, XD * h:XD * h + XD], start=k == 0, stop=k == 1)
                    mm.then_inc(S("x_pv"), 1)
            turn("xo", lambda r, k: SIL[:, r, P * k:P * k + P], lambda: pe.wait_ge(S("xatt_o"), RB * XH))
            turned_ready("xo")
            for c in range(4):
                chunk(CHUNK0["xo"] + c, [12, 13, 14, 15], 512)
            ffn(1, "f2")

        @block.vector
        def _(dve):
            st = Slabs()
            link = Chain(dve, S("dve_step"))

            def tt(out_, a, b, op):
                return dve.tensor_tensor(out_, a, b, op)

            def lo(width=2048):
                dve.wait_ge(hi_made, st.lins(1))
                tt(wl[:, st.lin % 2, 0:width], raw[:, st.raw % 4, 0:width], f32(wh[:, st.lin % 2, 0:width]),
                   ALU.subtract).then_inc(slab_done, 1)
                st.next()

            def ada(k, k0=None):
                dve.wait_ge(landed[st.raw % 4], st.landed())
                if st.raw or st.i is not None:
                    dve.wait_ge(slab_done, st.raws())
                w = raw[:, st.raw % 4, :]
                if k0 is not None:
                    ins = dve.scalar_tensor_tensor(ACC[:, :], w, cT[:, bass.ds(k0 + k, 1)], ACC[:, :], ALU.mult, ALU.add)
                elif k == 0:
                    ins = dve.tensor_scalar(ACC[:, :], w, cT[:, 0:1], None, ALU.mult)
                else:
                    ins = dve.scalar_tensor_tensor(ACC[:, :], w, cT[:, k:k + 1], ACC[:, :], ALU.mult, ALU.add)
                ins.then_inc(slab_done, 1)
                st.next(False)

            def mod_fin(v):
                dve.wait_ge(S("mod_sum"), v + 1)
                if v in (0, 3):
                    tt(modA[:, (0, 0, 0, 2)[v], :], PB[7][:, 0:KT], bT[:, KT * v:KT * v + KT], ALU.add)\
                        .then_inc(S("mod_ready"), 1)
                elif v in (1, 4):
                    gain = vT[:, V_PRE_MIX:V_PRE_MIX + KT] if v == 1 else vT[:, V_PRE_FFN:V_PRE_FFN + KT]
                    link(tt(mtmp[:, :], PB[7][:, 0:KT], bT[:, KT * v:KT * v + KT], ALU.add))
                    dve.scalar_tensor_tensor(modA[:, 1 if v == 1 else 3, :], mtmp[:, :], 1.0, gain, ALU.add, ALU.mult)\
                        .then_inc(S("mod_ready"), 1)
                else:
                    gain = bT[:, 96:112] if v == 2 else bT[:, 112:128]
                    link(tt(mtmp[:, :], PB[7][:, 0:KT], bT[:, KT * v:KT * v + KT], ALU.add))
                    tt(gT[:, :], mtmp[:, :], gain, ALU.mult).then_inc(S("mod_ready"), 1)

            def norm_inv(name):
                j = NORMS.index(name)
                dve.wait_ge(S("rooted"), j + 1)
                dve.reciprocal(nstat[:, j, 2, :], nstat[:, j, 1, :]).then_inc(S("rooted_inv"), 1)

            def turn_lo(name, hi_t, lo_t, gain=None, shift=None, k0=0, between=None):
                n = TURN_N[name]

                def gained(b):
                    g = TURN0[name] + b
                    dve.wait_ge(S("turned"), g + 1)
                    for k in range(2):
                        kt = 2 * b + k
                        half = slice(SEQ * k, SEQ * k + SEQ)
                        ins = dve.tensor_scalar(TMP[:, g % 2, half], PB[4 + g % 2][:, half], gain[:, kt:kt + 1],
                                                shift[:, kt:kt + 1], ALU.mult, ALU.add)
                    ins.then_inc(S("gained"), 1)

                def rest(b):
                    g = TURN0[name] + b
                    dve.wait_ge(S("turn_hi"), HI0[name] + b + 1)
                    src = TMP[:, g % 2, :] if shift is not None else PB[4 + g % 2][:, :]
                    sl = (slice(None), slice(k0 + 2 * b, k0 + 2 * b + 2), slice(None))
                    tt(lo_t[sl].rearrange("p t n -> p (t n)"), src, f32(hi_t[sl].rearrange("p t n -> p (t n)")),
                       ALU.subtract).then_inc(S("turn_free"), 1)

                def gained_rest(b):
                    g = TURN0[name] + b
                    dve.wait_ge(S("turn_hi"), HI0[name] + 2 * b + 2)
                    for k in range(2):
                        kt = 2 * b + k
                        ins = dve.scalar_tensor_tensor(lo_t[:, k0 + kt, :], PB[4 + g % 2][:, SEQ * k:SEQ * k + SEQ],
                                                       gain[:, kt:kt + 1], f32(hi_t[:, k0 + kt, :]), ALU.mult, ALU.subtract)
                    ins.then_inc(S("turn_free"), 1)

                if shift is not None:
                    for b in range(n + 1):
                        if b < n:
                            gained(b)
                        if b:
                            rest(b - 1)
                        if between and b in (4, 6, 8):
                            between()
                else:
                    for b in range(n):
                        rest(b) if gain is None else gained_rest(b)
                        if between and b in (3, 5, 7):
                            between()

            def norm_row2(name):
                j = NORMS.index(name)
                norm_inv(name)
                dve.wait_ge(S("rooted_inv"), j + 1)
                src = MEM if name == "mem" else X
                dve.tensor_scalar(ROWB[:, 1, :], src[:, 1, :], nstat[:, j, 2, 1:2], None, ALU.mult).then_inc(S("normed"), 1)

            def weigh(name, c):
                m = 4 * RB * POST.index(name) + RB * c
                for r in range(RB):
                    dve.wait_ge(S("part_sq"), m + r + 1)
                    y = ROWB[:, r, 512 * c:512 * c + 512]
                    tt(y, y, G[:, 512 * c:512 * c + 512], ALU.mult).then_inc(S("weighed"), 1)

            def add_normed(name):
                j, q = NORMS.index(name), POST.index(name)
                dve.wait_ge(S("part_sq"), 4 * RB * (q + 1))
                dve.tensor_reduce(nstat[:, j, 0, :], psq[:, q, :, :], AX.X, ALU.add).then_inc(S("squared"), RB)
                weigh(name, 3)
                norm_inv(name)
                dve.wait_ge(S("rooted_inv"), j + 1)
                dve.wait_ge(S("weighed"), 4 * RB * (q + 1))
                for c in range(4):
                    for r in range(RB):
                        x, y = (t[:, r, 512 * c:512 * c + 512] for t in (X, ROWB))
                        dve.scalar_tensor_tensor(x, y, nstat[:, j, 2, r:r + 1], x, ALU.mult, ALU.add).then_inc(S("x_added"), 1)

            dve.memset(eps[:, :], EPS).then_inc(S("zeroed"), 1)
            dve.memset(one[:, :], 1.0).then_inc(S("zeroed"), 1)
            for k in range(2):
                dve.wait_ge(S("vec_turned"), k + 1)
                n = (126, P)[k]
                dve.tensor_copy((vT, bT)[k][:, 0:n], PB[k][:, 0:n]).then_inc(S("vec_out"), 1)
            dve.wait_ge(S("rel_turned"), 1)
            dve.tensor_copy(rbT[:, :], PB[2][0:BUCKETS, 0:NH]).then_inc(S("rel_turned_out"), 1)
            dve.wait_ge(S("rel_made"), 1)
            dve.tensor_copy(relrow[:, 0:SEQ], PB[3][0:NH, 0:SEQ]).then_inc(S("rel_row"), 1)
            dve.memset(relrow[:, SEQ:REL_W], NEG).then_inc(S("rel_row"), 1)
            dve.wait_ge(S("c_gated"), 1)
            for k in range(4):
                ada(k)
            norm_row2("mem")
            for k in range(4, 8):
                ada(k)
            turn_lo("mem", XTh, XTl, gain=vT[:, V_LN_MEM:V_LN_MEM + KT])
            for c in range(2):
                for s in range(4):
                    lo()
                    for k in range(8 + 2 * s, 10 + 2 * s) if c == 0 else range(3 * s, 3 * s + 3):
                        ada(k)
                if c == 0:
                    mod_fin(0)
                    dve.wait_ge(S("mod_ready"), 1)
                    dve.wait_ge(S("turned"), TURN0["x"])
                    norm_row2("x")
            for k in range(12, KT):
                ada(k)
            lo(4 * ZC)
            mod_fin(1)
            dve.wait_ge(S("mod_ready"), 2)
            dve.wait_ge(S("turn_free"), TURN0["x"] + TURN_N["x"])
            for b in range(TURN_N["x"] + 1):
                if b < TURN_N["x"]:
                    for kt in (2 * b, 2 * b + 1):
                        ins = dve.tensor_scalar(XS[:, kt, :], XS[:, kt, :], modA[:, 1, kt:kt + 1], modA[:, 0, kt:kt + 1],
                                                ALU.mult, ALU.add)
                    ins.then_inc(S("gained"), 1)
                if b:
                    dve.wait_ge(S("turn_hi"), HI0["x"] + b)
                    part = slice(2 * b - 2, 2 * b)
                    tt(XTl[:, part, :], XS[:, part, :], f32(XTh[:, part, :]), ALU.subtract).then_inc(S("x_lo"), 1)
            link(dve.memset(ACC[:, :], 0.0))
            with dve.Fori(0, 2) as i, st.loop(i, 2, 24, 16):
                for c in range(4):
                    lo(4 * ZC)
                    ada(2 * c, i * 8)
                    lo(4 * ZC)
                    lo(4 * ZC)
                    ada(2 * c + 1, i * 8)
                    lo()
            dve.wait_ge(S("pos_in"), 16)
            link(dve.tensor_copy(posf[:, :], posi[:, :]))
            for r in range(RB):
                for k in range(2):
                    a, t, m = ropes[:, 0, :], ropes[:, 1, :], ropes[:, 2, :]
                    quarter = 0.25 if k == 0 else 0.0
                    link(dve.tensor_scalar(a, invf, posf[:, r:r + 1], None, ALU.mult))
                    link(dve.tensor_scalar(t, a, 1.0 / (2.0 * np.pi), quarter, ALU.mult, ALU.add))
                    link(dve.tensor_scalar(m, t, MAGIC, None, ALU.add))
                    link(dve.tensor_scalar(t, m, -MAGIC, None, ALU.add))
                    for q, part in enumerate(TWO_PI_PARTS):
                        src, dst = ((a, m), (m, a), (a, m))[q]
                        link(dve.scalar_tensor_tensor(dst, t, -part, src, ALU.mult, ALU.add))
                    link(dve.tensor_scalar(a, m, np.pi / 2 if k == 0 else 0.0, None, ALU.add))
                    dve.tensor_scalar(ang[:, r, k, :], a, 3.1415925, -3.1415925, ALU.min, ALU.max).then_inc(S("angle"), 1)
                    if r + k < 2:
                        dve.wait_ge(S("angle"), 2 * r + k + 1)
            mod_fin(2)
            shift_f = iter(range(KT))

            def ada_some(n):
                for k in (next(shift_f) for _ in range(n)):
                    ada(k)

            dve.wait_ge(S("mod_ready"), 3)
            ada_some(2)
            dve.wait_ge(S("a_turned"), 1)
            dve.tensor_copy(aT[:, :], PB[6][0:GR, 0:SEQ]).then_inc(S("a_out"), 1)
            ada_some(2)
            for r in range(RB):
                dve.wait_ge(S("log1p"), r + 1)
                link(dve.scalar_tensor_tensor(la[:, r, :], PB[r][:, :], 0.0, kd[:, r, :], ALU.min, ALU.subtract))
                dve.tensor_scalar(la[:, r, :], la[:, r, :], 1.0 / 16.0, None, ALU.mult).then_inc(S("log_a"), 1)
            ada_some(3)
            dve.wait_ge(S("cum"), 2 * RB)
            dve.wait_ge(S("einv_out"), RB)
            for r in range(RB):
                tt(bcs[:, r, :], PB[6 + r][:, :], bcs[:, r, :], ALU.subtract).then_inc(S("left"), 1)
            for r in range(RB):
                q, k = Z[:, r, Z_QG:Z_KG], Z[:, r, Z_KG:Z_VG]
                dve.scalar_tensor_tensor(q, q, GK ** -0.5, eb[:, r, :], ALU.mult, ALU.mult).then_inc(S("decayed"), 1)
                dve.wait_ge(S("edec_out"), r + 1)
                tt(kd[:, r, :], k, kd[:, r, :], ALU.mult).then_inc(S("k_decayed"), 1)
                dve.wait_ge(S("k_decayed"), r + 1)
                tt(k, k, einv[:, r, :], ALU.mult).then_inc(S("decayed"), 1)
            ada_some(3)
            link(dve.memset(attT[:, :, :, :], 0.0))
            for b in range(2):
                dve.wait_ge(S("gla_scored"), b + 1)
                for k in range(2):
                    for r in range(RB):
                        ins = dve.copy_predicated(attT[:, 2 * b + k, r, :], tri.bitcast(U32),
                                                  PB[4 + b][:, SEQ * k + P * r:SEQ * k + P * r + P])
                ins.then_inc(S("att_masked"), 1)
            for m in range(3 * GH):
                h, n = m // 3, m % 3
                dve.wait_ge(S("state_add"), 6 * (h // 2) + 6)
                bank, half = (6 + h // 2, h % 2) if n == 1 else (h, n // 2)
                src = PB[bank][:, GV * half:GV * half + GV]
                if n == 0:
                    dve.tensor_copy(states[:, h, 0, :], src).then_inc(S("stated"), 1)
                else:
                    dve.wait_ge(S("stated"), m)
                    dve.scalar_tensor_tensor(states[:, h, n, :], states[:, h, n - 1, :], decay[:, h, n:n + 1], src,
                                             ALU.mult, ALU.add).then_inc(S("stated"), 1)
            ada_some(3)
            dve.wait_ge(S("r_gated"), RB)
            for r in range(RB):
                gate = Z[:, r, Z_RG:Z_RG + GVAL].rearrange("p (h v) -> p h v", h=GH)
                tt(gate, gate, ggla[:, :].unsqueeze(1).broadcast_to([P, GH, GV]), ALU.mult).then_inc(S("r_gained"), 1)
            dve.wait_ge(S("r_gained"), RB)
            dve.wait_ge(S("gla_root"), 1)
            link(dve.reciprocal(gst[:, 2, :, :], gst[:, 1, :, :]))
            for h in range(GH):
                for r in range(RB):
                    v, g = Z_VG + GV * h, Z_RG + GV * h
                    dve.scalar_tensor_tensor(Z[:, r, v:v + GV], PB[h][:, GV * r:GV * r + GV], gst[:, 2, h, r:r + 1],
                                             Z[:, r, g:g + GV], ALU.mult, ALU.mult).then_inc(S("gla_done"), 1)
            norm_inv("cq")
            norm_inv("ckv")
            turn_lo("cq", XTh, XTl, gain=vT[:, V_GQ:V_GQ + 4])
            turn_lo("ckv", XTh, XTl, gain=vT[:, V_GKV:V_GKV + 2], k0=4)
            ada_some(3)
            lo()
            lo()
            mod_fin(3)
            dve.wait_ge(S("mod_ready"), 4)
            lo()
            lo()
            dve.wait_ge(S("sines"), 2 * RB)
            dve.wait_ge(chunk_out, RB * CHUNK0["uv"])
            for r in range(RB):
                kr = Z[:, r, Z_KR:Z_QG].rearrange("p (h d) -> p h d", h=1)
                for x, n in ((qrow[r][:, :, NOPE:QKD], MH), (kr, 1)):
                    cos = cs[:, r, 0:1, :].broadcast_to([P, n, HALF])
                    sin = cs[:, r, 1:2, :].broadcast_to([P, n, HALF])
                    x1, x2 = x[:, :, 0:HALF], x[:, :, HALF:ROPE]
                    t = [rt[k][:, 0:n, :] for k in range(4)]
                    tt(t[0], x1, cos, ALU.mult)
                    tt(t[1], x2, sin, ALU.mult)
                    tt(t[2], x2, cos, ALU.mult)
                    link(tt(t[3], x1, sin, ALU.mult))
                    tt(x1, t[0], t[1], ALU.subtract).then_inc(S("roped_half"), 1)
                    tt(x2, t[2], t[3], ALU.add).then_inc(S("roped"), 1)
                    dve.wait_ge(S("roped"), 2 * r + (n == 1) + 1)
            for t in range(MH + 3):
                h = t - 1
                if 0 <= h < MH:
                    dve.wait_ge(S("scored"), h + 1)
                    if h >= 2:
                        dve.wait_ge(S("p_turned"), h - 1)
                    tt(prob[:, h % 2, :], PB[6 + h % 2][:, 0:3 * P], mask3, ALU.add).then_inc(S("masked"), 1)
                    dve.wait_ge(S("masked"), h + 1)
                    for r in range(RB):
                        dve.tensor_reduce(mst[:, h % 4, 0, r:r + 1], prob[:, h % 2, P * r:P * (2 * r + 1)], AX.X, ALU.max,
                                          negate=True).then_inc(S("maxed"), 1)
                h = t - 3
                if 0 <= h < MH:
                    dve.wait_ge(S("pv_done"), h + 1)
                    link(dve.reciprocal(mst[:, h % 4, 2, :], mst[:, h % 4, 1, :]))
                    for r in range(RB):
                        dve.tensor_scalar(Z[:, r, Z_QG + VD * h:Z_QG + VD * h + VD], PB[h % 2][:, P * r:P * r + VD],
                                          mst[:, h % 4, 2, r:r + 1], None, ALU.mult).then_inc(S("mla_o"), 1)
            lo()
            scale_f = iter(range(KT))

            def ada_lo():
                ada(next(scale_f))
                lo()

            turn_lo("o", XTh, XTl, between=ada_lo)
            for c in range(4):
                for s in range(4):
                    if c or s == 3:
                        ada_lo()
                    if c and s == 2:
                        weigh("o", c - 1)
            mod_fin(4)
            add_normed("o")

            def ffn(k, pre, gain, shift, more):
                if k == 0:
                    norm_row2(pre)
                turn_lo(pre, XTh, XTl, gain=gain, shift=shift, between=lo)
                if k:
                    norm_inv(pre)
                    dve.wait_ge(S("rooted_inv"), NORMS.index(pre) + 1)
                for n in range(4):
                    for r in range(RB):
                        dve.memset(ROWB[:, r, 512 * n:512 * n + 512], 0.0).then_inc(S("y_added"), 1)
                b0 = RB * FN * k
                y0 = 8 * (FN + 1) * k

                def hidden(j):
                    for r in range(RB):
                        dve.wait_ge(S("silu_out"), j * RB + (b0 + r + 1))
                        if not isinstance(j, int) or j or k:
                            dve.wait_ge(S("h_turned"), j * 2 + b0)
                        if k == 0:
                            ins = tt(HROW[:, r, :], SIL[:, r, :], PB[2 + r][:, :], ALU.mult)
                        else:
                            by = nstat[:, NORMS.index(pre), 2, r:r + 1]
                            ins = dve.scalar_tensor_tensor(HROW[:, r, :], PB[2 + r][:, :], by, SIL[:, r, :], ALU.mult,
                                                           ALU.mult)
                        ins.then_inc(S("h_made"), 1)

                def hidden_lo(j):
                    for b in range(2):
                        dve.wait_ge(S("hid_hi"), j * 2 + (b0 + b + 1))
                        tt(HTl[:, 2 * b:2 * b + 2, :].rearrange("p t n -> p (t n)"), PB[4 + b][:, :],
                           f32(HTh[:, 2 * b:2 * b + 2, :].rearrange("p t n -> p (t n)")), ALU.subtract)\
                            .then_inc(S("hid_lo"), 1)

                def add(n, j, used):
                    dve.wait_ge(slab_used, used)
                    dve.wait_ge(S("y_added"), j * 8 + (y0 + 2 * n + RB))
                    banks = ((6, 7), (0, 1), (6, 7), (2, 3))[n]
                    for r in range(RB):
                        y = ROWB[:, r, 512 * n:512 * n + 512]
                        tt(y, y, PB[banks[r]][:, :], ALU.add).then_inc(S("y_added"), 1)

                for _ in range(4):
                    lo()
                dve.wait_ge(slab_used, st.lins())
                hidden(0)
                lo()
                hidden_lo(0)
                if k == 0:
                    link(dve.memset(ACC[:, :], 0.0))
                for first, last, per in ((0, FN_ADA, 16), (FN_ADA, FN - 1, 12)) if k == 0 else ((0, FN - 1, 12),):
                    with dve.Fori(first, last) as i, st.loop(i, last - first, per, 12, first):
                        def ada_row(q):
                            if per == 16:
                                ada(q, i * 4)

                        for s in range(8):
                            if s in (3, 7):
                                ada_row(s // 4)
                            lo()
                        dve.wait_ge(slab_used, st.lins(-1))
                        hidden(i + 1)
                        lo()
                        ada_row(2)
                        lo()
                        add(0, i, st.lins(-2))
                        lo()
                        add(1, i, st.lins(-2))
                        ada_row(3)
                        lo()
                        add(2, i, st.lins(-2))
                        add(3, i, st.lins(-1))
                        hidden_lo(i + 1)
                    if per == 16:
                        mod_fin(5)
                for n in range(4):
                    if n < 3 or more:
                        lo()
                    last = st.lins(-1) if n < 3 or more else st.lins()
                    add(n, FN - 1, last)
                    if n == 0 and k:
                        dve.wait_ge(S("gain_in"), 48)
                    if n:
                        weigh(("y1", "y2")[k], n - 1)
                add_normed(("y1", "y2")[k])

            dve.wait_ge(S("mod_ready"), 5)
            ffn(0, "f1", modA[:, 3, :], modA[:, 2, :], True)
            turn_lo("z2", XTh, XTl, gain=vT[:, V_LN_MIX:V_LN_MIX + KT])
            norm_inv("z2")
            for _, width in Z2_PARTS:
                with dve.Fori(0, Z2N // 2) as i, st.loop(i, Z2N // 2, 8, 8):
                    for c in range(2):
                        for s in range(3):
                            lo(4 * width)
                        lo()
            dve.wait_ge(S("pe_turned"), 1)
            dve.tensor_copy(peT[:, :, :].rearrange("p k l -> p (k l)"), PB[6][:, 0:2 * CS]).then_inc(S("pe_out"), 1)
            dve.wait_ge(S("pe_out"), 1)
            for b in range(4):
                dve.wait_ge(S("raw_turned"), b + 1)
                k, g, n = b // 2, 2 * (b % 2), SEQ // CS

                def tokens(ap):
                    return ap.rearrange("p (m l) -> p m l", l=CS)

                tt(tokens(rawT[0:HD, k, g:g + 2, :].rearrange("p g n -> p (g n)")), tokens(PB[b][0:HD, :]),
                   peT[0:HD, k:k + 1, :].broadcast_to([HD, 2 * n, CS]), ALU.add)
                for q in range(2):
                    ins = tt(tokens(rawT[HD:2 * HD, k, g + q, 0:SEQ - CS]), tokens(PB[b][HD:2 * HD, SEQ * q + CS:SEQ * q + SEQ]),
                             peT[HD:2 * HD, k:k + 1, :].broadcast_to([HD, n - 1, CS]), ALU.add)
                ins.then_inc(S("raw_out"), 1)
            dve.wait_ge(S("gates_out"), RB)
            dve.wait_ge(S("rel_in"), 16)
            for t in range(NH * RB + 4):
                u = t - 3
                if 0 <= u < NH * RB:
                    b, n_c = u % 2, (NCMP0, NCMP)[u % 2]
                    dve.wait_ge(S("n_turned"), u + 1)
                    if u >= 2:
                        dve.wait_ge(S("n_pv"), u - 1)
                    dve.tensor_copy(pcT[0:n_c, b, :], PB[2 + b][0:n_c, P:2 * P]).then_inc(S("n_cT"), 1)
                u = t
                if u < NH * RB:
                    h, r = u // 2, u % 2
                    nk, n_c = P * (r + 1), (NCMP0, NCMP)[r]
                    dve.wait_ge(S("n_scored"), u + 1)
                    if u >= 4:
                        dve.wait_ge(S("n_turned"), u - 3)
                    b = u % 2
                    off = P if r == 0 else 0
                    s3 = NSPROB(u % 4)[:, 0:2 * nk].rearrange("p (c n) -> p c n", c=2)
                    for c in range(2):
                        tt(s3[:, c, :], PB[b][:, nk * c:nk * c + nk], REL[:, h, off:off + nk], ALU.add)
                    c0 = (P - 1 + CL if r == 0 else CL - 1)
                    tt(pc[:, u % 4, 0:n_c], PB[2 + b][:, 0:n_c], REL[:, h, c0:c0 + CS * (n_c - 1) + 1:CS], ALU.add)\
                        .then_inc(S("n_added"), 1)
                    dve.wait_ge(S("n_added"), u + 1)
                    dve.tensor_reduce(nst[:, u % 8, 2, 0:2], s3, AX.X, ALU.max)
                    link(dve.tensor_reduce(nst[:, u % 8, 2, 2:3], pc[:, u % 4, 0:n_c], AX.X, ALU.max))
                    dve.tensor_scalar(nst[:, u % 8, 0, :], nst[:, u % 8, 2, :], -1e29, -1.0, ALU.max, ALU.mult)\
                        .then_inc(S("n_maxed"), 1)
                u = t - 4
                if 0 <= u < NH * RB:
                    h, r, b = u // 2, u % 2, u % 2
                    link(dve.tensor_scalar(nst[:, u % 8, 1, :], nst[:, u % 8, 1, :], 1.0, None, ALU.max))
                    link(dve.reciprocal(nst[:, u % 8, 1, :], nst[:, u % 8, 1, :]))
                    gl = Z2[:, r, Z2_GL + 3 * h:Z2_GL + 3 * h + 3]
                    wt = nwt[:, u % 8, :]
                    link(tt(wt, nst[:, u % 8, 1, :], gl, ALU.mult))
                    dve.wait_ge(S("n_pv"), u + 1)
                    o = Z2[:, r, HD * h:HD * h + HD]
                    po = PB[6 + b]
                    for c, q in enumerate((1, 2, 0)):
                        src = po[:, HD * c:HD * c + HD]
                        if c == 0:
                            ins = dve.tensor_scalar(o, src, nwt[:, u % 8, q:q + 1], None, ALU.mult)
                        else:
                            ins = dve.scalar_tensor_tensor(o, src, nwt[:, u % 8, q:q + 1], o, ALU.mult, ALU.add)
                        ins.then_inc(S("nsa_o"), 1)
                        if c < 2:
                            dve.wait_ge(S("nsa_o"), 3 * u + c + 1)
            for g in range(PG):
                dve.wait_ge(S("pool_hi"), g + 1)
                sl = (slice(None), slice(2 * g, 2 * g + 2), slice(None))
                tt(XTl[sl].rearrange("p t n -> p (t n)"), PB[g][:, :], f32(XTh[sl].rearrange("p t n -> p (t n)")),
                   ALU.subtract).then_inc(S("pool_lo"), 1)
            lo()
            for g in range(PG):
                dve.wait_ge(S("pool_lin"), g + 1) if g < PG - 1 else dve.wait_ge(slab_used, st.lins(-1))
                for q in range(2):
                    k = V_PS + 2 * g + q
                    ins = dve.tensor_scalar(TMPP[:, g % 2, SEQ * q:SEQ * q + SEQ], PB[4 + g][:, SEQ * q:SEQ * q + SEQ],
                                            vT[:, k:k + 1], None, ALU.mult)
                ins.then_inc(S("pool_scaled"), 1)
                dve.wait_ge(S("pool_hi"), PG + g + 1)
                sl = (slice(None), slice(8 + 2 * g, 10 + 2 * g), slice(None))
                tt(XTl[sl].rearrange("p t n -> p (t n)"), TMPP[:, g % 2, :], f32(XTh[sl].rearrange("p t n -> p (t n)")),
                   ALU.subtract).then_inc(S("pool_lo"), 1)
            turn_lo("att", XTh, XTl)
            dve.wait_ge(S("merge_gated"), RB)
            before = st.lin - 1

            def merge(c):
                dve.wait_ge(slab_used, before + 4 * (c + 1))
                cols = slice(512 * c, 512 * c + 512)
                for r in range(RB):
                    ga, gp = (Z2[:, r, Z2_M + D * k + 512 * c:Z2_M + D * k + 512 * c + 512] for k in range(2))
                    tt(ga, ga, PB[4 * (c % 2) + r][:, :], ALU.mult).then_inc(S("merged"), 1)
                    tt(gp, gp, PB[4 * (c % 2) + 2 + r][:, :], ALU.mult).then_inc(S("merged"), 1)
                    dve.wait_ge(S("merged"), 6 * c + 3 * r + 2)
                    tt(Z2[:, r, cols], ga, gp, ALU.add).then_inc(S("merged"), 1)

            for c in range(4):
                for s in range(4):
                    lo()
                    if c and s == 1:
                        merge(c - 1)
            merge(3)
            turn_lo("y", XTh, XTl, between=lo)
            for c in range(4):
                for s in range(4):
                    if c or s == 3:
                        lo()
                    if c and s == 2:
                        dve.wait_ge(S("gain_in"), 16)
                        weigh("mix", c - 1)
            add_normed("mix")
            turn_lo("xq", XTh, XTl, gain=vT[:, V_LN_X:V_LN_X + KT], between=lo)
            norm_inv("xq")
            lo()
            for t in range(XH + 2):
                h = t
                if h < XH:
                    dve.wait_ge(S("x_scored"), h + 1)
                    if h >= 2:
                        dve.wait_ge(S("x_exped"), RB * (h - 1))
                    dve.tensor_reduce(mst[:, h % 4, 0, :], PB[h % 2][:, :].rearrange("p (r n) -> p r n", r=RB), AX.X, ALU.max,
                                      negate=True).then_inc(S("x_maxed"), 1)
                h = t - 2
                if 0 <= h < XH:
                    dve.wait_ge(S("x_pv"), h + 1)
                    link(dve.reciprocal(mst[:, h % 4, 2, :], mst[:, h % 4, 1, :]))
                    for r in range(RB):
                        dve.tensor_scalar(SIL[:, r, XD * h:XD * h + XD], PB[2 + h % 2][:, P * r:P * r + XD],
                                          mst[:, h % 4, 2, r:r + 1], None, ALU.mult).then_inc(S("xatt_o"), 1)
            turn_lo("xo", XTh, XTl, k0=12)
            for c in range(4):
                lo()
                if c:
                    dve.wait_ge(S("gain_in"), 32)
                    weigh("xo", c - 1)
            add_normed("xo")
            ffn(1, "f2", vT[:, V_LN_FFN:V_LN_FFN + KT], None, False)


def kernel(**inputs):
    import concourse.bacc as bacc
    from concourse.bass_utils import run_bass_kernel_spmd

    nc = bacc.Bacc("TRN2", target_bir_lowering=False, num_devices=1, dynamic_dma_scratch_size=4096)
    const, band, onehot = shape_constants()
    host = {name: np.ascontiguousarray(a) for name, a in inputs.items()}
    drop = ("w_ada", "b_ada", "g_pre_mix", "g_post_mix", "w_in", "g_q", "w_uq", "g_kv", "w_uk", "w_uv", "w_gate_up", "b_gate",
            "g_gla", "w_out", "g_pre_ffn", "g_post_ffn", "w_ffn_gate", "w_ffn_up", "w_ffn_down", "x", "c", "positions")
    for name, a in host.items():
        if name in drop or (name.endswith("_2") and name != "rel_bias_2"):
            host[name] = a[0]
    host.update(const=const, band=band, onehot=onehot)
    A = {name: nc.dram_tensor(f"in_{name}", a.shape, mybir.dt.from_np(a.dtype), kind="ExternalInput").ap()
         for name, a in host.items()}
    out = nc.dram_tensor("out_x", (SEQ, D), F32, kind="ExternalOutput").ap()
    build(nc, A, out)
    r = run_bass_kernel_spmd(nc, [{f"in_{name}": a for name, a in host.items()}], core_ids=[0])
    return r.results[0]["out_x"].reshape(1, SEQ, D)
```
